# Optimizing a Trainium2 kernel written in Bass

```python
import jax, jax.numpy as jnp
from jax import lax
import numpy as np

D_MODEL = 1024
BATCH = 1
SEQ = 128
DEPTH = 1
DEC_BATCH = 1
DEC_SEQ = 1024
PAST_LEN = 256

GRID_W = 64
W_A = 256
W_B = 256
W_C = 512
HEAD_C = 64
H_C = W_C // HEAD_C
D_MIX = W_A + W_B + W_C
CONV_A = 3
CONV_B = 31
LORA_W = 64
LORA_A = 64
N_DIR = 2
OFF_B = 4 * W_A
OFF_C = OFF_B + 3 * W_B
SHIFT_W = 3 * W_C + N_DIR * LORA_W + N_DIR * LORA_A
OFF_G = OFF_C + SHIFT_W
D_IN = OFF_G + W_C
RMS_EPS = 1e-6
LN_EPS = 1e-5
GN_EPS = 64e-5

kernel_name = "hybrid_conv_rwkv7_flow_step"

def rms_norm(x, g):
    xf = x.astype(jnp.float32)
    y = xf * lax.rsqrt(jnp.mean(xf * xf, -1, keepdims=True) + RMS_EPS)
    return (y * g.astype(jnp.float32)).astype(x.dtype)

def layer_norm(x, g, b, eps):
    xf = x.astype(jnp.float32)
    mu = jnp.mean(xf, -1, keepdims=True)
    var = jnp.mean(jnp.square(xf - mu), -1, keepdims=True)
    y = (xf - mu) * lax.rsqrt(var + eps)
    return (y * g.astype(jnp.float32) + b.astype(jnp.float32)).astype(x.dtype)

def dwconv(x, w):
    k, ch = w.shape
    return lax.conv_general_dilated(x, w[:, None, :].astype(x.dtype), window_strides=(1,),
                                    padding=[(k // 2, k // 2)],
                                    dimension_numbers=('NWC', 'WIO', 'NWC'),
                                    feature_group_count=ch)

def conv_seq(x, w, latent, along_rows):
    if not latent:
        return dwconv(x, w)
    bn, t, ch = x.shape
    rows = t // GRID_W
    g = x.reshape(bn, rows, GRID_W, ch)
    if along_rows:
        return dwconv(g.reshape(bn * rows, GRID_W, ch), w).reshape(bn, t, ch)
    gt = g.transpose(0, 2, 1, 3).reshape(bn * GRID_W, rows, ch)
    y = dwconv(gt, w).reshape(bn, GRID_W, rows, ch).transpose(0, 2, 1, 3)
    return y.reshape(bn, t, ch)

def centred_shift(p, mu):
    prev = jnp.pad(p[:, :-1], ((0, 0), (1, 0), (0, 0)))
    nxt = jnp.pad(p[:, 1:], ((0, 0), (0, 1), (0, 0)))
    return p + mu * (0.5 * (prev + nxt) - p)

def rwkv7_scan(s0, r, decay, k, v, kk, a, reverse):
    def step(s, inp):
        r_t, w_t, k_t, v_t, kk_t, a_t = inp
        sa = jnp.einsum('bhvk,bhk->bhv', s, kk_t)
        s = (s * w_t[:, :, None, :] - sa[..., None] * (kk_t * a_t)[:, :, None, :]
             + v_t[..., None] * k_t[:, :, None, :])
        return s, jnp.einsum('bhvk,bhk->bhv', s, r_t)
    xs = tuple(jnp.swapaxes(t, 0, 1) for t in (r, decay, k, v, kk, a))
    s, ys = lax.scan(step, s0, xs, reverse=reverse)
    return s, jnp.swapaxes(ys, 0, 1)

def trunk_layer(x, mod, p, latent, s0_fwd, s0_bwd):
    bn, t, _ = x.shape
    dt = x.dtype
    ada = jax.nn.silu(mod) @ p['ada_w'] + p['ada_b']
    ada = ada[None, None] if mod.ndim == 1 else ada[:, None]
    shift, scale, gate = jnp.split(ada, 3, -1)
    h = rms_norm(x, p['g_pre']) * (1.0 + scale) + shift
    z = h @ p['w_in']
    za, zb, zc, gc = jnp.split(z, [OFF_B, OFF_C, OFF_G], -1)
    xa, bg, cg, ga = jnp.split(za, 4, -1)
    ya = bg * conv_seq(cg * xa, p['conv_a'], latent, True) * jax.nn.silu(ga)
    u1, u2, gb = jnp.split(zb, 3, -1)
    u = conv_seq(u1 * jax.nn.sigmoid(u2), p['conv_b'], latent, False) + p['conv_b_bias']
    u = layer_norm(u, p['ln_b_g'], p['ln_b_b'], LN_EPS)
    yb = jax.nn.silu(u) * jax.nn.silu(gb)
    zc = centred_shift(zc, p['mu'])
    r, k, v, lw, la = jnp.split(zc, [W_C, 2 * W_C, 3 * W_C, 3 * W_C + N_DIR * LORA_W], -1)
    lw = lw.reshape(bn, t, N_DIR, LORA_W).astype(jnp.float32)
    la = la.reshape(bn, t, N_DIR, LORA_A).astype(jnp.float32)
    rf, kf, vf = (q.astype(jnp.float32) for q in (r, k, v))
    wl = p['w0'].astype(jnp.float32) + jnp.einsum('btdr,drc->btdc', jnp.tanh(lw), p['w2'].astype(jnp.float32))
    decay = jnp.exp(-jnp.exp(-jax.nn.softplus(-wl) - 0.5))
    a = jax.nn.sigmoid(p['a0'].astype(jnp.float32) + jnp.einsum('btdr,drc->btdc', la, p['a2'].astype(jnp.float32)))
    kk = (kf * p['k_k'].astype(jnp.float32)).reshape(bn, t, H_C, HEAD_C)
    kk = kk * lax.rsqrt(jnp.sum(kk * kk, -1, keepdims=True) + 1e-12)
    kd = kf[:, :, None, :] * (1.0 + (a - 1.0) * p['k_a'].astype(jnp.float32))
    hd = lambda q: q.reshape(bn, t, H_C, HEAD_C)
    rh, vh = hd(rf), hd(vf)
    r_k = p['r_k'].astype(jnp.float32)
    s_fwd, y_fwd = rwkv7_scan(s0_fwd.astype(jnp.float32), rh, hd(decay[:, :, 0]), hd(kd[:, :, 0]),
                              vh, kk, hd(a[:, :, 0]), False)
    s_bwd, y_bwd = rwkv7_scan(s0_bwd.astype(jnp.float32), rh, hd(decay[:, :, 1]), hd(kd[:, :, 1]),
                              vh, kk, hd(a[:, :, 1]), True)
    bonus = (jnp.sum(rh * (hd(kd[:, :, 0]) + hd(kd[:, :, 1])) * r_k, -1, keepdims=True)) * vh
    ys = y_fwd + y_bwd
    mu_y = jnp.mean(ys, -1, keepdims=True)
    var_y = jnp.mean(jnp.square(ys - mu_y), -1, keepdims=True)
    yg = ((ys - mu_y) * lax.rsqrt(var_y + GN_EPS)).reshape(bn, t, W_C)
    yg = yg * p['gn_g'].astype(jnp.float32) + p['gn_b'].astype(jnp.float32)
    yc = (yg + bonus.reshape(bn, t, W_C)).astype(dt) * jax.nn.silu(gc)
    out = jnp.concatenate([ya, yb, yc], -1) @ p['w_out']
    x = x + gate * rms_norm(out, p['g_post'])
    return x, s_fwd.astype(dt), s_bwd.astype(dt)

def setup_inputs(seed: int = 0) -> dict:
    key = jax.random.key(seed)
    ks = jax.random.split(key, 32)
    nrm = lambda i, shape, s: jax.random.normal(ks[i], shape, jnp.float32) * s
    L = DEPTH
    return {
        'x_prompt': nrm(0, (BATCH, SEQ, D_MODEL), 1.0),
        'x_sample': nrm(1, (DEC_BATCH, DEC_SEQ, D_MODEL), 1.0),
        'c': nrm(2, (DEC_BATCH, D_MODEL), 1.0),
        'state_rwkv': nrm(3, (DEC_BATCH, DEPTH, N_DIR, H_C, HEAD_C, HEAD_C), 0.3),
        'c_ctx': nrm(4, (D_MODEL,), 1.0),
        'ada_w': nrm(5, (L, D_MODEL, 3 * D_MODEL), 0.5 * D_MODEL ** -0.5),
        'ada_b': nrm(6, (L, 3 * D_MODEL), 0.02),
        'g_pre': 1.0 + nrm(7, (L, D_MODEL), 0.05),
        'g_post': 1.0 + nrm(8, (L, D_MODEL), 0.05),
        'w_in': nrm(9, (L, D_MODEL, D_IN), D_MODEL ** -0.5),
        'conv_a': nrm(10, (L, CONV_A, W_A), CONV_A ** -0.5),
        'conv_b': nrm(11, (L, CONV_B, W_B), CONV_B ** -0.5),
        'conv_b_bias': nrm(12, (L, W_B), 0.02),
        'ln_b_g': 1.0 + nrm(13, (L, W_B), 0.05),
        'ln_b_b': nrm(14, (L, W_B), 0.02),
        'mu': jax.random.uniform(ks[15], (L, SHIFT_W), jnp.float32, 0.1, 0.9),
        'w0': jax.random.uniform(ks[16], (L, N_DIR, W_C), jnp.float32, -4.0, 1.0),
        'w2': nrm(17, (L, N_DIR, LORA_W, W_C), 0.1 * LORA_W ** -0.5),
        'a0': nrm(18, (L, N_DIR, W_C), 0.5),
        'a2': nrm(19, (L, N_DIR, LORA_A, W_C), 0.1 * LORA_A ** -0.5),
        'k_k': 0.85 + nrm(20, (L, W_C), 0.05),
        'k_a': 1.0 + nrm(21, (L, W_C), 0.05),
        'r_k': nrm(22, (L, H_C, HEAD_C), 0.1),
        'gn_g': 1.0 + nrm(23, (L, W_C), 0.05),
        'gn_b': nrm(24, (L, W_C), 0.02),
        'w_out': nrm(25, (L, D_MIX, D_MODEL), D_MIX ** -0.5),
    }

def reference(x_prompt, x_sample, c, state_rwkv, c_ctx, ada_w, ada_b, g_pre, g_post, w_in,
              conv_a, conv_b, conv_b_bias, ln_b_g, ln_b_b, mu, w0, w2, a0, a2, k_k, k_a,
              r_k, gn_g, gn_b, w_out):
    xp = x_prompt
    xs = x_sample
    bp = x_prompt.shape[0]
    new_states = []
    for l in range(DEPTH):
        p = {'ada_w': ada_w[l], 'ada_b': ada_b[l], 'g_pre': g_pre[l], 'g_post': g_post[l],
             'w_in': w_in[l], 'conv_a': conv_a[l], 'conv_b': conv_b[l],
             'conv_b_bias': conv_b_bias[l], 'ln_b_g': ln_b_g[l], 'ln_b_b': ln_b_b[l],
             'mu': mu[l], 'w0': w0[l], 'w2': w2[l], 'a0': a0[l], 'a2': a2[l], 'k_k': k_k[l],
             'k_a': k_a[l], 'r_k': r_k[l], 'gn_g': gn_g[l], 'gn_b': gn_b[l], 'w_out': w_out[l]}
        zeros = jnp.zeros((bp, H_C, HEAD_C, HEAD_C), xp.dtype)
        xp, sf, sb = trunk_layer(xp, c_ctx, p, False, zeros, zeros)
        new_states.append(jnp.stack([sf, sb], axis=1))
        xs, _, _ = trunk_layer(xs, c, p, True, state_rwkv[:, l, 0], state_rwkv[:, l, 1])
    new_state_rwkv = jnp.stack(new_states, axis=1)
    return (xp, xs, new_state_rwkv)


_drawn_inputs = setup_inputs


def setup_inputs(seed=0):
    import zlib

    import numpy as np

    out = dict(_drawn_inputs(seed))
    spreads = {}
    factors = {'state_rwkv': 7.734,
     'g_post': 3.986,
     'conv_b_bias': 8.0,
     'ln_b_g': 8.0,
     'ln_b_b': 49.869,
     'w2': 4.072,
     'gn_g': 5.306,
     'gn_b': 24.182}
    for name, (base, spread) in spreads.items():
        noise = np.random.default_rng([zlib.crc32(name.encode()), seed]).standard_normal(out[name].shape)
        drawn = base * np.exp(spread * noise) if base else spread * noise
        out[name] = __import__('jax').numpy.asarray(drawn.astype(out[name].dtype))
    for name, factor in factors.items():
        out[name] = (out[name] * factor).astype(out[name].dtype)
    return out
```

```python
from contextlib import ExitStack

import concourse.bass as bass
from concourse import mybir

ALU = mybir.AluOpType
ACT = mybir.ActivationFunctionType
F32 = mybir.dt.float32

P = 128
D_MODEL = 1024
KT = D_MODEL // P
SEQ, DEC_SEQ = 128, 1024
GRID_W = 64
ROWS = DEC_SEQ // GRID_W
TP, TS = 2, 132
W = TS + DEC_SEQ + 2
NB = 3
NC = W // NB
D_MIX = 1024
CONV_A, CONV_B = 3, 31
HEAD = 64
C = 64
PAIRS = 4
LEVELS = 6
E_HALF = 0.6065306597126334
RMS_EPS, LN_EPS, GN_EPS, KK_EPS = 1e-6, 1e-5, 64e-5, 1e-12

VEC_ROWS = {}
_n = 0
for _name, _rows in (("c_ctx", 8), ("c", 8), ("g_pre", 8), ("conv_b_bias", 2), ("ln_b_g", 2), ("ln_b_b", 2),
                     ("mu", 14), ("w0", 8), ("a0", 8), ("k_k", 4), ("k_a", 4), ("r_k", 4), ("gn_g", 4),
                     ("gn_b", 4), ("conv_a", 6)):
    VEC_ROWS[_name] = (_n, _rows)
    _n += _rows
N_VEC = _n
N_CB = 2 * CONV_B


PIECES = [("u2", 5), ("u1", 4), ("gb", 6), ("xa", 0), ("cg", 2), ("bg", 1), ("ga", 3),
          ("mix", 7), ("mix", 8), ("mix", 9), ("mix", 10), ("mix", 11), ("mix", 12), ("mix", 13),
          ("gc", 14), ("gc", 15)]
TILES = [kind for kind, _ in PIECES for _ in range(2)]
MIX0 = TILES.index("mix")
MIXES = TILES.count("mix")
GC0 = TILES.index("gc")
RING = 3
PIECE = 2048
N_ADA = KT
HT_BANKS = [(k, TP, P, 0, 0) for k in range(KT)] + \
           [(k, TS + 512 * g, 512, 1 + 4 * g, 1) for g in range(2) for k in range(KT)]


def hybrid_step_kernel(nc, x_prompt, x_sample, c, state_rwkv, c_ctx, ada_w, ada_b, g_pre, g_post, w_in,
                       conv_a, conv_b, conv_b_bias, ln_b_g, ln_b_b, mu, w0, w2, a0, a2, k_k, k_a,
                       r_k, gn_g, gn_b, w_out, y_prompt, y_sample, new_state):
    ctx = ExitStack()
    with ctx:
        def sb(name, *shape):
            return ctx.enter_context(nc.sbuf_tensor(name, [P, *shape], F32))

        def sem(name):
            return ctx.enter_context(nc.semaphore(name))

        ps = ctx.enter_context(nc.psum_tensor("ps", [P, 8, 512], F32))
        mix_dram = nc.dram_tensor("mix_scratch", [8, P, W], F32, kind="Internal").ap()

        hT = sb("hT", KT, W)
        y = hT[:, 0:4, :]
        q = hT[:, 4:8, :]
        zc = sb("zc", 18, W)
        rT, kT, vT, kkT = (zc[:, 4 * n:4 * n + 4, :] for n in range(4))
        lwT, laT = zc[:, 16, :], zc[:, 17, :]
        zflat = zc[:, :, :].rearrange("p a w -> p (a w)")
        xtok = zflat[:, 0:9 * D_MODEL].rearrange("p (i d) -> p i d", i=9)
        ARENA = 19400
        arena = sb("arena", ARENA)
        vec = sb("vec", N_VEC)
        cb = sb("cb", N_CB)
        cah = sb("cah", 6)
        smod = sb("smod", 16)
        hmu = sb("hmu", 14)
        omu = sb("omu", 14)
        shf = sb("shf", KT, 2)
        scl = sb("scl", KT, 2)
        small = sb("small", 36)
        epst = sb("epst", 4)
        lvl = sb("lvl", LEVELS, P)
        eye = sb("eye", P)
        heads = sb("heads", P)
        ones = sb("ones", P)
        tri = sb("tri", 2, 3, C)
        w2s = sb("w2s", 512)
        a2s = sb("a2s", 512)

        def carve(start=0):
            at = [start]

            def take(*shape):
                n = 1
                for s in shape:
                    n *= s
                v = arena[:, at[0]:at[0] + n]
                at[0] += n
                assert at[0] <= ARENA, at[0]
                if len(shape) == 1:
                    return v
                names = "abcd"[:len(shape)]
                return v.rearrange(f"p ({' '.join(names)}) -> p {' '.join(names)}",
                                   **{names[i]: shape[i] for i in range(len(shape))})
            return take

        def cols(name):
            return vec[:, VEC_ROWS[name][0]:VEC_ROWS[name][0] + VEC_ROWS[name][1]]

        def col(name, i):
            return cols(name)[:, i:i + 1]


        take = carve()
        ring = take(RING, PIECE)
        T = take(10, W)
        va, vb = T[:, 0, 0:P], T[:, 0, P:2 * P]
        junk = T[:, 1, 0:D_MODEL]
        spare = T[:, 2:6, :].rearrange("p a w -> p (a w)")
        row, adab = spare[0:2, 0:2048], spare[0:2, 2048:4096]
        blocks = T[:, 6, 0:7 * P].rearrange("p (l j) -> p l j", l=7)
        triw = T[:, 7, 0:4 * P].rearrange("p (l j) -> p l j", l=4)
        ss, rs = small[:, 0:9], small[:, 9:18]

        s_vec = sem("vectors_landed")
        s_w2 = sem("lora_landed")
        s_x = [sem(f"x_landed_{i}") for i in range(3)]
        s_adab = sem("ada_b_landed")
        s_wl = [sem(f"weights_landed_{i}") for i in range(RING)]
        s_wu = sem("weights_used")
        s_const = sem("constants_built")
        s_pool = sem("pool_chain")
        s_dve = sem("dve_chain")
        s_act = sem("act_chain")
        s_vt = sem("vectors_transposed")
        s_vc = sem("vectors_copied")
        s_tm = sem("tanh_of_modulation")
        s_smod = sem("silu_of_modulation")
        s_row = sem("ada_rows_copied")
        s_at = sem("ada_transposed")
        s_sc = sem("scale_shift_ready")
        s_ss = sem("squares_summed")
        s_ms = sem("mean_square_ready")
        s_sd = sem("x_deviation_ready")
        s_xn = sem("x_normalised")
        s_xt = sem("x_transposed")
        s_ha = sem("hT_written_by_act")
        s_hd = sem("hT_written_by_dve")
        s_z = sem("tile_projected")
        s_th = sem("tanh_ready")
        s_glu = sem("glu_ready")
        s_gb = sem("gate_b_ready")
        s_xa = sem("xa_copied")
        s_cx = sem("cg_times_xa_ready")
        s_bg = sem("bg_applied")
        s_ya = sem("ya_ready")
        s_raw = sem("raw_copied")
        s_sum = sem("neighbours_summed")
        s_mix = sem("shift_mixed")
        s_lwt = sem("lw_tanh_ready")
        s_cv = sem("conv_b_done")
        s_lm = sem("ln_mean_summed")
        s_lx = sem("ln_centred")
        s_lq = sem("ln_squared")
        s_lv = sem("ln_variance_summed")
        s_ls = sem("ln_deviation_ready")
        s_lr = sem("ln_scaled")
        s_lt = sem("ln_tanh_ready")
        s_yb = sem("yb_ready")
        s_kk = sem("kk_scaled")
        s_kq = sem("kk_squared")
        s_ks = sem("kk_square_summed")
        s_kd = sem("kk_deviation_ready")
        s_kn = sem("kk_normalised")
        s_gc = sem("gate_c_ready")
        s_sa = sem("ya_spilled")
        s_sb = sem("yb_spilled")
        s_sg = sem("gate_c_spilled")

        def dest(m):
            return zc[:, m if m < 12 else m + 4, :]

        def zbanks(j):
            return ps[:, NB * (j % 2):NB * (j % 2) + NB, 0:NC]

        def as3(a):
            return a.rearrange("p (n w) -> p n w", n=NB)

        def read_by(j):
            i = j - TILES.index(TILES[j])
            return {"u2": s_th, "u1": s_glu, "gb": s_gb, "xa": s_xa, "cg": s_cx, "bg": s_bg, "ga": s_ya,
                    "mix": s_raw, "gc": s_gc}[TILES[j]], i + 1

        with nc.Block() as block:
            @block.sync
            def _(sp):
                def flat(a):
                    names = "abcd"[:len(a.shape)]
                    return a if len(names) == 1 else a.rearrange(f"{' '.join(names)} -> ({' '.join(names)})")

                given = {"c_ctx": c_ctx, "c": c, "g_pre": g_pre, "conv_b_bias": conv_b_bias, "ln_b_g": ln_b_g,
                         "ln_b_b": ln_b_b, "mu": mu, "w0": w0, "a0": a0, "k_k": k_k, "k_a": k_a, "r_k": r_k,
                         "gn_g": gn_g, "gn_b": gn_b, "conv_a": conv_a}
                for name, (r0, n) in VEC_ROWS.items():
                    sp.dma_start(va[r0:r0 + n, :], flat(given[name]).rearrange("(r p) -> r p", p=P)).then_inc(s_vec, 16)
                sp.dma_start(vb[0:N_CB, :], conv_b.rearrange("a j (h p) -> (a j h) p", p=P)).then_inc(s_vec, 16)

                def spill(first, tiles, ready, count, spilled):
                    sp.wait_ge(ready, count)
                    sp.dma_start(mix_dram[first:first + 2].rearrange("m p w -> p m w"), tiles).then_inc(spilled, 16)

                for n in range(N_ADA + len(PIECES)):
                    if n >= RING:
                        last = n - RING
                        if last < N_ADA:
                            sp.wait_ge(s_wu, last + 1)
                        else:
                            sp.wait_ge(s_z, 2 * (last - N_ADA + 1))
                    slot = ring[:, n % RING, :]
                    if n < N_ADA:
                        sp.dma_start(slot, ada_w[0, n * P:(n + 1) * P, 0:2048]).then_inc(s_wl[n % RING], 16)
                    else:
                        at = 256 * PIECES[n - N_ADA][1]
                        sp.dma_start(slot.rearrange("p (k n) -> p k n", k=KT),
                                     w_in[0, :, at:at + 256].rearrange("(k p) n -> p k n", p=P)).then_inc(s_wl[n % RING], 16)
                    if n == 0:
                        for s in range(2):
                            sp.dma_start(adab[s:s + 1, :], ada_b[:, 0:2048]).then_inc(s_adab, 16)
                    if n == N_ADA + MIX0 // 2 + RING:
                        spill(0, kkT[:, 0:2, :], s_ya, 2, s_sa)
                    if n == N_ADA + MIX0 // 2 + RING + 1:
                        spill(2, T[:, 6:8, :], s_yb, 2, s_sb)
                spill(4, T[:, 4:6, :], s_gc, 2, s_sg)
                spill(6, T[:, 6:8, :], s_gc, 4, s_sg)
                sp.wait_ge(s_sg, 32)
                sp.wait_ge(s_sa, 16)
                sp.wait_ge(s_sb, 16)

            @block.gpsimd
            def _(pool):
                n_pool = [0]

                def link(ins):
                    n_pool[0] += 1
                    ins.then_inc(s_pool, 1)
                    pool.wait_ge(s_pool, n_pool[0])

                link(pool.memset(blocks, 1.0))
                for l in range(7):
                    b = 1 << l
                    m = blocks[:, l, :].rearrange("p (n b) -> p n b", b=b)
                    link(pool.affine_select(out=m, in_=m, compare_op=ALU.is_ge, fill=0.0, base=0,
                                            pattern=[[-b, P // b], [0, b]], channel_multiplier=1))
                    link(pool.affine_select(out=m, in_=m, compare_op=ALU.is_ge, fill=0.0, base=b - 1,
                                            pattern=[[b, P // b], [0, b]], channel_multiplier=-1))
                    if l == 0:
                        pool.tensor_copy(eye[:, :], blocks[:, 0, :]).then_inc(s_const, 1)
                pool.tensor_copy(heads[:, :], blocks[:, 6, :])
                pool.tensor_tensor(lvl[:, :, :], blocks[:, 1:7, :], blocks[:, 0:6, :], ALU.subtract)
                pool.memset(ones[:, :], 1.0 / 256)
                link(pool.memset(triw, 1.0))
                for n, (sign, base) in enumerate(((1, -1), (1, 0), (-1, -1), (-1, 0))):
                    link(pool.affine_select(out=triw[:, n, :], in_=triw[:, n, :], compare_op=ALU.is_ge, fill=0.0,
                                            base=base, pattern=[[sign, P]], channel_multiplier=-sign))
                for d in range(2):
                    for half in range(2):
                        r = slice(64 * half, 64 * half + 64)
                        for slot, kind in enumerate((0, 1, 0)):
                            link(pool.tensor_copy(tri[r, d, slot, :], triw[r, 2 * d + kind, r]))
                for n, e in enumerate((RMS_EPS, LN_EPS, KK_EPS, GN_EPS)):
                    pool.memset(epst[:, n:n + 1], e)
                for a in (0, TS - 2, W - 2):
                    last = pool.memset(hT[:, :, a:a + 2], 0.0)
                last.then_inc(s_const, 1)
                pool.wait_ge(s_yb, 2)
                for m in range(MIXES):
                    if m >= 2:
                        pool.wait_ge(s_mix, m - 1)
                    pool.wait_ge(s_raw, m + 1)
                    raw = T[:, 8 + m % 2, :]
                    pool.tensor_tensor(T[:, 2 + m % 2, 1:W - 1], raw[:, 0:W - 2], raw[:, 2:W], ALU.add).then_inc(s_sum, 1)

            @block.scalar
            def _(act):
                xs = x_sample[0].rearrange("(i p) d -> p i d", p=P)
                act.dma_start(xtok[:, 0, :], x_prompt[0]).then_inc(s_x[0], 16)
                act.dma_start(xtok[:, 1:5, :], xs[:, 0:4, :]).then_inc(s_x[1], 16)
                act.dma_start(xtok[:, 5:9, :], xs[:, 4:8, :]).then_inc(s_x[2], 16)
                act.dma_start(w2s[:, :], w2.rearrange("a n r d -> (a n r) d")).then_inc(s_w2, 16)
                act.dma_start(a2s[:, :], a2.rearrange("a n r d -> (a n r) d")).then_inc(s_w2, 16)
                act.wait_ge(s_vc, 1)
                act.activation(small[:, 18:34], vec[:, 0:16], ACT.Tanh, scale=0.5).then_inc(s_tm, 1)
                for i in range(9):
                    if i in (0, 1, 5):
                        act.wait_ge(s_x[(0, 1, 5).index(i)], 16)
                    if i:
                        act.wait_ge(s_ss, i)
                    act.activation(junk, xtok[:, i, :], ACT.Square, accum_out=ss[:, i:i + 1]).then_inc(s_ss, 1)
                act.wait_ge(s_ms, 1)
                act.activation(ss, ss, ACT.Sqrt).then_inc(s_sd, 1)
                act.wait_ge(s_sc, 1)
                for n in range(0, len(HT_BANKS), 2):
                    k, at, w, _, s = HT_BANKS[n]
                    act.wait_ge(s_xt, n + 1)
                    act.activation(hT[:, k, at:at + w], ps[:, n % 4, 0:w], ACT.Identity,
                                   bias=shf[:, k, s:s + 1], scale=scl[:, k, s:s + 1]).then_inc(s_ha, 1)

                def kk_norm(m):
                    act.wait_ge(s_kk, m + 1)
                    act.activation(T[:, 0, :], kkT[:, m, :], ACT.Square).then_inc(s_kq, 1)
                    for n in range(NB):
                        act.wait_ge(s_ks, NB * m + n + 1)
                        if n == 0 and m:
                            act.wait_ge(s_kn, m)
                        act.activation(T[:, 1, n * NC:(n + 1) * NC], ps[:, 6 + n % 2, 0:NC], ACT.Sqrt,
                                       bias=epst[:, 2:3]).then_inc(s_kd, 1)

                def layer_norm():
                    for n in range(NB):
                        cut = slice(n * NC, (n + 1) * NC)
                        act.wait_ge(s_lx, n + 1)
                        act.activation(T[:, 2:4, cut], T[:, 0:2, cut], ACT.Square).then_inc(s_lq, 1)
                        act.wait_ge(s_lv, n + 1)
                        act.activation(T[:, 8, cut], ps[:, 7, 0:NC], ACT.Sqrt, bias=epst[:, 1:2]).then_inc(s_ls, 1)
                    for g in range(2):
                        act.wait_ge(s_lr, g + 1)
                        act.activation(T[:, 2 + g, :], T[:, g, :], ACT.Tanh, scale=0.5).then_inc(s_lt, 1)

                for j, kind in enumerate(TILES):
                    h, z = j % 2, zbanks(j)
                    if kind in ("u2", "gb", "ga", "gc", "xa", "mix"):
                        act.wait_ge(s_z, j + 1)
                    if kind == "u2":
                        act.activation(as3(T[:, h, :]), z, ACT.Tanh, scale=0.5).then_inc(s_th, 1)
                    elif kind == "gb":
                        act.activation(as3(T[:, 6 + h, :]), z, ACT.Tanh, scale=0.5).then_inc(s_th, 1)
                    elif kind == "xa":
                        act.activation(as3(vT[:, h, :]), z, ACT.Copy).then_inc(s_xa, 1)
                    elif kind == "ga":
                        act.activation(as3(vT[:, 2 + h, :]), z, ACT.Tanh, scale=0.5).then_inc(s_th, 1)
                    elif kind == "mix":
                        m = j - MIX0
                        if m >= 2:
                            act.wait_ge(s_sum, m - 1)
                        act.activation(as3(dest(m)), z, ACT.Copy, scale=omu[:, m:m + 1])
                        act.activation(as3(T[:, 8 + m % 2, :]), z, ACT.Copy).then_inc(s_raw, 1)
                    elif kind == "gc":
                        i = j - GC0
                        if i == 2:
                            act.wait_ge(s_sb, 16)
                        act.activation(as3(T[:, 4 + i, :]), z, ACT.Tanh, scale=0.5).then_inc(s_th, 1)
                    if j == MIX0 - 1:
                        layer_norm()
                    if MIX0 + 5 <= j <= MIX0 + 8:
                        kk_norm(j - MIX0 - 5)
                    if j == MIX0 + 13:
                        act.wait_ge(s_mix, 13)
                        act.activation(lwT, lwT, ACT.Tanh).then_inc(s_lwt, 1)

            @block.tensor
            def _(pe):
                pe.wait_ge(s_const, 1)
                pe.wait_ge(s_vec, 16 * (len(VEC_ROWS) + 1))
                pe.transpose(ps[:, 6, 0:N_VEC], va[0:N_VEC, :], eye[0:N_VEC, 0:N_VEC]).then_inc(s_vt, 1)
                pe.transpose(ps[:, 7, 0:N_CB], vb[0:N_CB, :], eye[0:N_CB, 0:N_CB]).then_inc(s_vt, 1)
                pe.wait_ge(s_smod, 1)
                mods = smod[:, :].rearrange("p (s k) -> p k s", k=KT)
                for k in range(KT):
                    pe.wait_ge(s_wl[k % RING], 16 * (k // RING + 1))
                    for b in range(4):
                        last = pe.matmul(ps[0:2, b, :], mods[:, k, :], ring[:, k % RING, 512 * b:512 * b + 512],
                                         start=(k == 0), stop=(k == KT - 1))
                    last.then_inc(s_wu, 1)
                pe.wait_ge(s_row, 1)
                for m in range(16):
                    last = pe.transpose(ps[:, 4, 2 * m:2 * m + 2], row[:, P * m:P * m + P], eye[0:2, 0:2])
                last.then_inc(s_at, 1)
                pe.wait_ge(s_xn, 9)
                for n, (k, at, w, i0, _) in enumerate(HT_BANKS):
                    if n >= 4:
                        pe.wait_ge((s_ha, s_hd)[n % 2], (n - 4) // 2 + 1)
                    for i in range(w // P):
                        last = pe.transpose(ps[:, n % 4, P * i:P * i + P], xtok[:, i0 + i, P * k:P * k + P], eye[:, :])
                    last.then_inc(s_xt, 1)

                def layer_norm():
                    pe.wait_ge(s_cv, 2)
                    for n in range(NB):
                        cut = slice(n * NC, (n + 1) * NC)
                        if n:
                            pe.wait_ge(s_lx, n)
                        pe.matmul(ps[:, 6, 0:NC], ones[:, :], T[:, 4, cut], start=True, stop=False)
                        pe.matmul(ps[:, 6, 0:NC], ones[:, :], T[:, 5, cut], start=False, stop=True).then_inc(s_lm, 1)
                        pe.wait_ge(s_lq, n + 1)
                        if n:
                            pe.wait_ge(s_ls, n)
                        pe.matmul(ps[:, 7, 0:NC], ones[:, :], T[:, 2, cut], start=True, stop=False)
                        pe.matmul(ps[:, 7, 0:NC], ones[:, :], T[:, 3, cut], start=False, stop=True).then_inc(s_lv, 1)

                def kk_norm(m):
                    pe.wait_ge(s_kq, m + 1)
                    for n in range(NB):
                        if n == 2:
                            pe.wait_ge(s_kd, NB * m + 1)
                        elif m:
                            pe.wait_ge(s_kd, NB * m)
                        pe.matmul(ps[:, 6 + n % 2, 0:NC], heads[:, :], T[:, 0, n * NC:(n + 1) * NC],
                                  start=True, stop=True).then_inc(s_ks, 1)

                pe.wait_ge(s_const, 2)
                pe.wait_ge(s_w2, 32)
                pe.wait_ge(s_ha, 12)
                pe.wait_ge(s_hd, 12)
                for j in range(len(TILES)):
                    n = N_ADA + j // 2
                    slot = ring[:, n % RING, :].rearrange("p (k n) -> p k n", k=KT)
                    if j % 2 == 0:
                        pe.wait_ge(s_wl[n % RING], 16 * (n // RING + 1))
                    if j >= 2:
                        pe.wait_ge(*read_by(j - 2))
                    for b in range(NB):
                        for k in range(KT):
                            last = pe.matmul(ps[:, NB * (j % 2) + b, 0:NC], slot[:, k, P * (j % 2):P * (j % 2) + P],
                                             hT[:, k, NC * b:NC * (b + 1)], start=(k == 0), stop=(k == KT - 1))
                    last.then_inc(s_z, 1)
                    if j == MIX0:
                        layer_norm()
                    if MIX0 + 5 <= j <= MIX0 + 8:
                        kk_norm(j - MIX0 - 5)

            @block.vector
            def _(dve):
                n_dve = [0]

                def link(ins):
                    n_dve[0] += 1
                    ins.then_inc(s_dve, 1)
                    dve.wait_ge(s_dve, n_dve[0])

                dve.wait_ge(s_vt, 1)
                dve.tensor_copy(vec[:, :], ps[:, 6, 0:N_VEC]).then_inc(s_vc, 1)
                dve.wait_ge(s_vt, 2)
                dve.tensor_scalar(cb[:, :], ps[:, 7, 0:N_CB], 0.5, None, ALU.mult)
                dve.wait_ge(s_vc, 1)
                dve.tensor_scalar(cah[:, :], cols("conv_a"), 0.5, None, ALU.mult)
                dve.tensor_scalar(hmu[:, :], cols("mu"), 0.5, None, ALU.mult)
                dve.tensor_scalar(omu[:, :], cols("mu"), -1.0, 1.0, ALU.mult, ALU.add)
                dve.wait_ge(s_tm, 1)
                link(dve.scalar_tensor_tensor(out=smod[:, :], in0=small[:, 18:34], scalar=1.0, in1=vec[:, 0:16],
                                              op0=ALU.add, op1=ALU.mult))
                dve.tensor_scalar(smod[:, :], smod[:, :], 0.5, None, ALU.mult).then_inc(s_smod, 1)
                dve.wait_ge(s_ss, 9)
                dve.tensor_scalar(ss, ss, 1.0 / D_MODEL, RMS_EPS, ALU.mult, ALU.add).then_inc(s_ms, 1)
                dve.wait_ge(s_sd, 1)
                link(dve.reciprocal(rs, ss))
                for i in range(9):
                    dve.tensor_scalar(xtok[:, i, :], xtok[:, i, :], rs[:, i:i + 1], None, ALU.mult).then_inc(s_xn, 1)
                dve.wait_ge(s_wu, KT)
                dve.wait_ge(s_adab, 32)
                dve.tensor_tensor(row, ps[0:2, 0:4, :].rearrange("p b n -> p (b n)"), adab, ALU.add).then_inc(s_row, 1)
                dve.wait_ge(s_at, 1)
                cols4 = ps[:, 4, 0:32].rearrange("p (m s) -> p m s", s=2)
                dve.tensor_copy(shf[:, :, :], cols4[:, 0:KT, :])
                dve.scalar_tensor_tensor(out=scl[:, :, :], in0=cols4[:, KT:, :], scalar=1.0,
                                         in1=cols("g_pre").unsqueeze(2).to_broadcast([P, KT, 2]),
                                         op0=ALU.add, op1=ALU.mult).then_inc(s_sc, 1)
                dve.wait_ge(s_sc, 1)
                for n in range(1, len(HT_BANKS), 2):
                    k, at, w, _, s = HT_BANKS[n]
                    dve.wait_ge(s_xt, n + 1)
                    dve.tensor_scalar(hT[:, k, at:at + w], ps[:, n % 4, 0:w], scl[:, k, s:s + 1], shf[:, k, s:s + 1],
                                      ALU.mult, ALU.add).then_inc(s_hd, 1)

                def conv_taps(g, first, last):
                    x, o = T[:, 2 + g, :], T[:, 4 + g, :]
                    order = [CONV_B // 2] + [t for t in range(CONV_B) if t != CONV_B // 2]
                    for t in order[first:last]:
                        w = cb[:, 2 * t + g:2 * t + g + 1]
                        off = t - CONV_B // 2
                        if off == 0:
                            link(dve.tensor_scalar(o, x, w, col("conv_b_bias", g), ALU.mult, ALU.add))
                            continue
                        for at, n, step in ((TP, SEQ, 1), (TS, ROWS, GRID_W)):
                            lo, hi = max(0, -off), min(n, n - off)
                            if hi <= lo:
                                continue
                            a, b = at + lo * step, at + hi * step
                            done = dve.scalar_tensor_tensor(out=o[:, a:b], in0=x[:, a + off * step:b + off * step], scalar=w,
                                                            in1=o[:, a:b], op0=ALU.mult, op1=ALU.add)
                        if t == order[-1]:
                            done.then_inc(s_cv, 1)
                        else:
                            link(done)

                def conv_a_half(g):
                    x, o = vT[:, g, :], kkT[:, g, :]
                    link(dve.tensor_scalar(o, x, cah[:, 2 + g:3 + g], None, ALU.mult))
                    xg, og = (a[:, TS:TS + DEC_SEQ].rearrange("p (r w) -> p r w", w=GRID_W) for a in (x, o))
                    for t, off in ((0, -1), (2, 1)):
                        w = cah[:, 2 * t + g:2 * t + g + 1]
                        dve.scalar_tensor_tensor(out=o[:, TP:TP + SEQ], in0=x[:, TP + off:TP + SEQ + off], scalar=w,
                                                 in1=o[:, TP:TP + SEQ], op0=ALU.mult, op1=ALU.add)
                        lo, hi = max(0, -off), GRID_W - max(0, off)
                        link(dve.scalar_tensor_tensor(out=og[:, :, lo:hi], in0=xg[:, :, lo + off:hi + off], scalar=w,
                                                      in1=og[:, :, lo:hi], op0=ALU.mult, op1=ALU.add))

                def layer_norm():
                    for n in range(NB):
                        cut = slice(n * NC, (n + 1) * NC)
                        dve.wait_ge(s_lm, n + 1)
                        dve.tensor_tensor(T[:, 0:2, cut], T[:, 4:6, cut],
                                          ps[:, 6, 0:NC].unsqueeze(1).to_broadcast([P, 2, NC]), ALU.subtract).then_inc(s_lx, 1)
                        dve.wait_ge(s_ls, n + 1)
                        link(dve.reciprocal(T[:, 8, cut], T[:, 8, cut]))
                        link(dve.tensor_tensor(T[:, 0:2, cut], T[:, 0:2, cut],
                                               T[:, 8, cut].unsqueeze(1).to_broadcast([P, 2, NC]), ALU.mult))
                    for g in range(2):
                        dve.tensor_scalar(T[:, g, :], T[:, g, :], col("ln_b_g", g), col("ln_b_b", g),
                                          ALU.mult, ALU.add).then_inc(s_lr, 1)
                    for g in range(2):
                        dve.wait_ge(s_lt, g + 1)
                        link(dve.scalar_tensor_tensor(out=T[:, 2 + g, :], in0=T[:, 2 + g, :], scalar=1.0, in1=T[:, g, :],
                                                      op0=ALU.add, op1=ALU.mult))
                        dve.scalar_tensor_tensor(out=T[:, 6 + g, :], in0=T[:, 2 + g, :], scalar=0.25, in1=T[:, 6 + g, :],
                                                 op0=ALU.mult, op1=ALU.mult).then_inc(s_yb, 1)

                def kk_norm(m):
                    dve.wait_ge(s_kd, NB * (m + 1))
                    link(dve.reciprocal(T[:, 1, :], T[:, 1, :]))
                    dve.tensor_tensor(kkT[:, m, :], kkT[:, m, :], T[:, 1, :], ALU.mult).then_inc(s_kn, 1)

                for j, kind in enumerate(TILES):
                    h, z = j % 2, zbanks(j)
                    i = j - TILES.index(kind)
                    if kind in ("u1", "gb", "cg", "bg", "ga", "gc"):
                        dve.wait_ge(s_z, j + 1)
                    if kind == "u1":
                        dve.wait_ge(s_th, h + 1)
                        dve.scalar_tensor_tensor(out=as3(T[:, 2 + h, :]), in0=as3(T[:, h, :]), scalar=1.0, in1=z,
                                                 op0=ALU.add, op1=ALU.mult).then_inc(s_glu, 1)
                        dve.wait_ge(s_glu, h + 1)
                        conv_taps(h, 0, 12)
                    elif kind == "gb":
                        dve.wait_ge(s_th, 3 + h)
                        dve.scalar_tensor_tensor(out=as3(T[:, 6 + h, :]), in0=as3(T[:, 6 + h, :]), scalar=1.0, in1=z,
                                                 op0=ALU.add, op1=ALU.mult).then_inc(s_gb, 1)
                        conv_taps(0, 12 + 10 * h, 22 + 9 * h)
                    elif kind == "cg":
                        dve.wait_ge(s_xa, h + 1)
                        dve.tensor_tensor(as3(vT[:, h, :]), as3(vT[:, h, :]), z, ALU.mult).then_inc(s_cx, 1)
                        dve.wait_ge(s_cx, h + 1)
                        conv_a_half(h)
                        conv_taps(1, 12 + 6 * h, 18 + 6 * h)
                    elif kind == "bg":
                        dve.tensor_tensor(as3(kkT[:, h, :]), as3(kkT[:, h, :]), z, ALU.mult).then_inc(s_bg, 1)
                        if h:
                            conv_taps(1, 24, 31)
                    elif kind == "ga":
                        dve.wait_ge(s_th, 5 + h)
                        link(dve.scalar_tensor_tensor(out=as3(vT[:, 2 + h, :]), in0=as3(vT[:, 2 + h, :]), scalar=1.0, in1=z,
                                                      op0=ALU.add, op1=ALU.mult))
                        dve.wait_ge(s_bg, h + 1)
                        dve.tensor_tensor(kkT[:, h, :], kkT[:, h, :], vT[:, 2 + h, :], ALU.mult).then_inc(s_ya, 1)
                        if h:
                            layer_norm()
                    elif kind == "mix":
                        dve.wait_ge(s_sum, i + 1)
                        o = dest(i)[:, 1:W - 1]
                        dve.scalar_tensor_tensor(out=o, in0=T[:, 2 + i % 2, 1:W - 1], scalar=hmu[:, i:i + 1], in1=o,
                                                 op0=ALU.mult, op1=ALU.add).then_inc(s_mix, 1)
                        if 4 <= i < 8:
                            if i == 4:
                                dve.wait_ge(s_sa, 16)
                            dve.wait_ge(s_mix, i + 1)
                            dve.tensor_scalar(kkT[:, i - 4, :], kT[:, i - 4, :], col("k_k", i - 4), None,
                                              ALU.mult).then_inc(s_kk, 1)
                        if 5 <= i < 9:
                            kk_norm(i - 5)
                    elif kind == "gc":
                        dve.wait_ge(s_th, 7 + i)
                        dve.scalar_tensor_tensor(out=as3(T[:, 4 + i, :]), in0=as3(T[:, 4 + i, :]), scalar=1.0, in1=z,
                                                 op0=ALU.add, op1=ALU.mult).then_inc(s_gc, 1)

        take = carve()
        DIRS = range(2)
        ls = take(2, P)
        xw = take(PAIRS, 2, C)
        av = take(PAIRS, 2, C)
        LA = take(PAIRS, 2, C)
        LB = take(PAIRS, 2, C)
        eA, eB, eN = take(PAIRS, 2, C), take(PAIRS, 2, C), take(PAIRS, 2, C)
        kd = take(2, PAIRS, C)
        keep = take(512)
        GL = [take(PAIRS, 3, C) for _ in DIRS]
        GR = [take(PAIRS, 4, C) for _ in DIRS]
        Ub = [take(PAIRS, P) for _ in DIRS]
        Um = [take(PAIRS, P) for _ in DIRS]
        X = [take(PAIRS, P) for _ in DIRS]
        Y = [take(PAIRS, P) for _ in DIRS]
        PX = [take(PAIRS, P) for _ in DIRS]
        KB = [take(PAIRS, 2, C) for _ in DIRS]
        SU = [take(2, PAIRS, 2, C) for _ in DIRS]
        AB = [take(PAIRS, C) for _ in DIRS]
        RH = [take(PAIRS, C) for _ in DIRS]
        VD = [take(PAIRS, 2, C) for _ in DIRS]
        stin = GL[0].rearrange("p a b c -> p (a b c)")[:, 0:512], GL[1].rearrange("p a b c -> p (a b c)")[:, 0:512]
        sout = X

        s_set = sem("scan_buffers_set")
        s_so = sem("final_state_transposed")
        s_sc2 = sem("final_state_copied")
        s_sz = sem("state_staging_zero")
        s_sl = sem("state_landed")
        s_st = sem("state_transposed")
        s_sw = sem("state_written")
        s_ns = sem("new_state_stored")

        with nc.Block() as block:
            @block.vector
            def _(dve):
                dve.memset(hT[:, :, :], 0.0)
                for d in DIRS:
                    dve.memset(Ub[d], 0.0)
                    dve.memset(SU[d], 0.0)
                dve.memset(ls, 0.0)
                dve.memset(keep, 1.0).then_inc(s_set, 1)
                dve.wait_ge(s_set, 1)
                dve.memset(keep.rearrange("p (n c) -> p n c", c=C)[:, :, 0:1], 0.0)

        step_sems = []

        def ssem(name):
            s = sem(name)
            step_sems.append(s)
            return s

        l_stage = ssem("lora_input_staged")
        l_lora = ssem("lora_multiplied")
        l_x = ssem("lora_bias_added")
        l_tanh = ssem("gates_tanh_ready")
        l_dve = ssem("step_dve_chain")
        l_pool = ssem("step_pool_chain")
        l_log = ssem("log_decay_ready")
        l_exp = ssem("decay_ready")
        l_kd = ssem("kd_ready")
        l_kd2 = ssem("kd_and_b_ready")
        l_S2 = ssem("state_summed")
        l_ops = [ssem(f"operands_ready_{d}") for d in DIRS]
        l_gram = [ssem(f"products_ready_{d}") for d in DIRS]
        l_vd = [ssem(f"v_doubled_{d}") for d in DIRS]
        l_vt = [ssem(f"v_transposed_{d}") for d in DIRS]
        l_kt = [ssem(f"keys_transposed_{d}") for d in DIRS]
        l_v = [ssem(f"v_by_token_{d}") for d in DIRS]
        l_kb = [ssem(f"keys_by_token_{d}") for d in DIRS]
        l_u = [ssem(f"m_b_masked_{d}") for d in DIRS]
        l_g = [ssem(f"products_masked_{d}") for d in DIRS]
        l_um = [ssem(f"level_masked_{d}") for d in DIRS]
        l_X = [ssem(f"inverse_ready_{d}") for d in DIRS]
        l_Y = [ssem(f"inverse_transposed_ready_{d}") for d in DIRS]
        l_P = [ssem(f"level_product_{d}") for d in DIRS]
        l_pc = [ssem(f"level_product_copied_{d}") for d in DIRS]
        l_Q = [ssem(f"level_update_{d}") for d in DIRS]
        l_rhs = [ssem(f"rhs_multiplied_{d}") for d in DIRS]
        l_rh = [ssem(f"rhs_copied_{d}") for d in DIRS]
        l_U = [ssem(f"u_multiplied_{d}") for d in DIRS]
        l_uc = [ssem(f"u_copied_{d}") for d in DIRS]
        l_S = [ssem(f"outputs_multiplied_{d}") for d in DIRS]
        nums = [s.num for s in step_sems]
        assert nums == list(range(nums[0], nums[0] + len(nums)))

        def pairs(bank, w):
            return ps[:, bank, 0:PAIRS * w].rearrange("p (a b) -> p a b", a=PAIRS)

        def scan(base, chunks):
            with nc.Fori(0, chunks) as i:
                at = [base + C * i, base + C * (chunks - 1) - C * i]

                def chunk(tiles, d):
                    return tiles[:, :, bass.ds(at[d], C)]

                with nc.Block() as block:
                    @block.scalar
                    def _(act):
                        for n, src in enumerate((lwT, laT)):
                            for d in DIRS:
                                r = slice(64 * d, 64 * d + 64)
                                act.activation(ls[r, n, r], src[r, bass.ds(at[d], C)], ACT.Copy).then_inc(l_stage, 1)
                        for d in DIRS:
                            act.activation(VD[d], chunk(vT, d).unsqueeze(2).to_broadcast([P, PAIRS, 2, C]),
                                           ACT.Copy).then_inc(l_vd[d], 1)
                        for n, x in enumerate((xw, av)):
                            act.wait_ge(l_x, n + 1)
                            act.activation(x, x, ACT.Tanh, scale=0.5).then_inc(l_tanh, 1)
                        act.wait_ge(l_log, 1)
                        act.activation(eB, LB, ACT.Exp).then_inc(l_exp, 1)
                        act.wait_ge(l_log, 2)
                        act.activation(eA, LA, ACT.Exp).then_inc(l_exp, 1)
                        act.activation(eN, LA, ACT.Exp, scale=-1.0).then_inc(l_exp, 1)
                        for d in DIRS:
                            act.wait_ge(l_vt[d], 1)
                            vt = ps[:, 4 + d, :].rearrange("p (a h c) -> p a h c", a=PAIRS, h=2)
                            for g, r in ((0, slice(64, 128)), (1, slice(0, 64))):
                                act.activation(SU[d][r, :, :, g, :],
                                               vt[r, :, g, :].unsqueeze(1).to_broadcast([64, 2, PAIRS, C]),
                                               ACT.Copy).then_inc(l_v[d], 1)
                        for d in DIRS:
                            for g in range(2):
                                act.wait_ge(l_kt[d], g + 1)
                                act.activation(KB[d][:, :, g, :], pairs(6 + g, P)[:, :, 64 * g:64 * g + 64],
                                               ACT.Copy).then_inc(l_kb[d], 1)
                        for d in DIRS:
                            act.wait_ge(l_rhs[d], 1)
                            act.activation(RH[d], pairs(4 + d, C), ACT.Copy, scale=-1.0).then_inc(l_rh[d], 1)
                        for l in range(1, LEVELS):
                            for d in DIRS:
                                act.wait_ge(l_P[d], l)
                                act.activation(PX[d], pairs(2 * d, P), ACT.Copy).then_inc(l_pc[d], 1)
                        for d in DIRS:
                            act.wait_ge(l_U[d], 1)
                            u = ps[:, 4 + d, 256:512].rearrange("p (a c) -> p a c", a=PAIRS)
                            for g, r in ((0, slice(0, 64)), (1, slice(64, 128))):
                                act.activation(SU[d][r, 1, :, g, :], u[r], ACT.Copy).then_inc(l_uc[d], 1)

                    @block.tensor
                    def _(pe):
                        for n, w in enumerate((w2s, a2s)):
                            pe.wait_ge(l_stage, 2 * n + 2)
                            for a in range(PAIRS):
                                last = pe.matmul(pairs(4 + n, P)[:, a, :], w[:, P * a:P * a + P], ls[:, n, :],
                                                 start=True, stop=True)
                            last.then_inc(l_lora, 1)
                        for d in DIRS:
                            pe.wait_ge(l_ops[d], 1)
                            for g in range(2):
                                r = slice(64 * g, 64 * g + 64)
                                for a in range(PAIRS):
                                    last = pe.matmul(pairs(2 * d + g, P)[:, a, :], GL[d][r, a, g:g + 2, :],
                                                     GR[d][r, a, 2 * g:2 * g + 2, :], start=True, stop=True)
                                last.then_inc(l_gram[d], 1)
                        for d in DIRS:
                            pe.wait_ge(l_vd[d], 1)
                            pe.wait_ge(l_x, d + 1)
                            for a in range(PAIRS):
                                last = pe.transpose(pairs(4 + d, P)[:, a, :], VD[d][:, a].rearrange("p b c -> p (b c)"), eye[:, :])
                            last.then_inc(l_vt[d], 1)
                        for d in DIRS:
                            if d:
                                pe.wait_ge(l_kb[0], 2)
                            for g in range(2):
                                for a in range(PAIRS):
                                    last = pe.transpose(pairs(6 + g, P)[:, a, :],
                                                        GL[d][:, a, g:g + 2, :].rearrange("p b c -> p (b c)"), eye[:, :])
                                last.then_inc(l_kt[d], 1)
                        for d in DIRS:
                            pe.wait_ge(l_v[d], 2)
                            pe.wait_ge(l_g[d], 1)
                            for a in range(PAIRS):
                                for g in range(2):
                                    last = pe.matmul(pairs(4 + d, C)[64 * g:64 * g + 64, a, :], GR[d][:, a, 3 * g, :],
                                                     SU[d][:, 0, a, g, :], start=True, stop=True)
                            last.then_inc(l_rhs[d], 1)
                        for l in range(1, LEVELS):
                            for d in DIRS:
                                pe.wait_ge(l_um[d], l + 1)
                                pe.wait_ge(l_X[d], l)
                                for a in range(PAIRS):
                                    last = pe.matmul(pairs(2 * d, P)[:, a, :], Um[d][:, a, :], X[d][:, a, :], start=True, stop=True)
                                last.then_inc(l_P[d], 1)
                            for d in DIRS:
                                pe.wait_ge(l_pc[d], l)
                                for a in range(PAIRS):
                                    last = pe.matmul(pairs(2 * d + 1, P)[:, a, :], PX[d][:, a, :], Y[d][:, a, :], start=True, stop=True)
                                last.then_inc(l_Q[d], 1)
                        for d in DIRS:
                            pe.wait_ge(l_Y[d], LEVELS)
                            pe.wait_ge(l_rh[d], 1)
                            for a in range(PAIRS):
                                last = pe.matmul(ps[:, 4 + d, 256 + C * a:256 + C * a + C], Y[d][:, a, :], RH[d][:, a, :],
                                                 start=True, stop=True)
                            last.then_inc(l_U[d], 1)
                        pe.wait_ge(l_kb[1], 2)
                        for d in DIRS:
                            pe.wait_ge(l_uc[d], 2)
                            for a in range(PAIRS):
                                for g in range(2):
                                    r = slice(64 * g, 64 * g + 64)
                                    o = pairs(6 + d, C)[r, a, :]
                                    pe.matmul(o, SU[d][:, 0, a, g, :], GR[d][:, a, 1 + g, :], start=True, stop=False)
                                    pe.matmul(o, SU[d][r, 1, a, g, :], AB[d][r, a, :], start=False, stop=True)
                            for a in range(PAIRS):
                                for g in range(2):
                                    last = pe.matmul(ps[64 * g:64 * g + 64, 6 + d, 256 + C * a:256 + C * a + C],
                                                     KB[d][:, a, g, :], SU[d][:, 1, a, g, :], start=True, stop=True)
                            last.then_inc(l_S[d], 1)

                    @block.gpsimd
                    def _(pool):
                        n_pool = [0]

                        def link(ins):
                            n_pool[0] += 1
                            ins.then_inc(l_pool, 1)
                            pool.wait_ge(l_pool, n_pool[0])

                        for l in range(LEVELS):
                            for d in DIRS:
                                if l == 0:
                                    pool.wait_ge(l_u[d], 2)
                                elif l == 1:
                                    pool.wait_ge(l_Y[d], 1)
                                else:
                                    pool.wait_ge(l_P[d], l - 1)
                                pool.tensor_tensor(Um[d], Ub[d], lvl[:, l, :].unsqueeze(1).to_broadcast([P, PAIRS, P]),
                                                   ALU.mult).then_inc(l_um[d], 1)
                        for d in DIRS:
                            pool.wait_ge(l_kd, d + 1)
                            link(pool.tensor_tensor(kd[:, d], kd[:, d], chunk(rT, d), ALU.mult))
                            link(pool.tensor_tensor(chunk(q, d), chunk(q, d), kd[:, d], ALU.add))

                    @block.vector
                    def _(dve):
                        n_dve = [0]

                        def link(ins):
                            n_dve[0] += 1
                            ins.then_inc(l_dve, 1)
                            dve.wait_ge(l_dve, n_dve[0])

                        def wide(name):
                            return cols(name).rearrange("p (d a) -> p a d", d=2).unsqueeze(3).to_broadcast([P, PAIRS, 2, C])

                        for n, (x, bias) in enumerate(((xw, "w0"), (av, "a0"))):
                            dve.wait_ge(l_lora, n + 1)
                            dve.tensor_tensor(x, ps[:, 4 + n, :].rearrange("p (a d c) -> p a d c", a=PAIRS, d=2),
                                              wide(bias), ALU.add).then_inc(l_x, 1)
                        dve.wait_ge(l_tanh, 1)
                        link(dve.tensor_scalar(xw, xw, -E_HALF / 2, -E_HALF / 2, ALU.mult, ALU.add))
                        link(dve.tensor_tensor_scan(LA.rearrange("p a d c -> p (a d c)"), keep,
                                                    xw.rearrange("p a d c -> p (a d c)"), 0.0, ALU.mult, ALU.add))
                        dve.tensor_tensor(LB[:, :, 0], LA[:, :, 0], xw[:, :, 0], ALU.subtract)
                        link(dve.tensor_tensor(LB[:, :, 1], LA[:, :, 1, C - 1:C].to_broadcast([P, PAIRS, C]),
                                               LA[:, :, 1], ALU.subtract))
                        dve.tensor_tensor(LA[:, :, 1], LB[:, :, 1], xw[:, :, 1], ALU.add).then_inc(l_log, 2)
                        dve.wait_ge(l_log, 2)
                        dve.wait_ge(l_tanh, 2)
                        link(dve.tensor_scalar(av, av, 0.5, 0.5, ALU.mult, ALU.add))
                        m1, a2d = (v.rearrange("p a d c -> p a (d c)") for v in (xw, av))
                        link(dve.scalar_tensor_tensor(out=m1, in0=a2d, scalar=-1.0,
                                                      in1=cols("k_a").unsqueeze(2).to_broadcast([P, PAIRS, P]),
                                                      op0=ALU.add, op1=ALU.mult))
                        for d in DIRS:
                            dve.scalar_tensor_tensor(out=kd[:, d], in0=xw[:, :, d], scalar=1.0, in1=chunk(kT, d),
                                                     op0=ALU.add, op1=ALU.mult).then_inc(l_kd2, 1)
                            dve.tensor_tensor(GL[d][:, :, 0, :], chunk(kkT, d), av[:, :, d], ALU.mult).then_inc(l_kd2, 1)
                        dve.wait_ge(l_kd2, 4)
                        for d in DIRS:
                            kk2 = chunk(kkT, d).unsqueeze(2).to_broadcast([P, PAIRS, 2, C])
                            r2 = chunk(rT, d).unsqueeze(2).to_broadcast([P, PAIRS, 2, C])
                            dve.wait_ge(l_exp, 1)
                            dve.tensor_tensor(GR[d][:, :, 0:4:3, :], kk2,
                                              eB[:, :, d].unsqueeze(2).to_broadcast([P, PAIRS, 2, C]), ALU.mult)
                            dve.wait_ge(l_exp, 3)
                            dve.tensor_tensor(GR[d][:, :, 1:3, :], r2,
                                              eA[:, :, d].unsqueeze(2).to_broadcast([P, PAIRS, 2, C]), ALU.mult)
                            dve.tensor_tensor(GL[d][:, :, 1, :], kd[:, d], eN[:, :, d], ALU.mult).then_inc(l_kd, 1)
                            dve.tensor_tensor(GL[d][:, :, 2, :], GL[d][:, :, 0, :], eN[:, :, d], ALU.mult)
                            dve.tensor_tensor(GL[d][:, :, 0, :], GL[d][:, :, 0, :], eN[:, :, d], ALU.mult).then_inc(l_ops[d], 1)
                        lo, hi = slice(0, 64), slice(64, 128)

                        def mask(d, r, slots):
                            return tri[r, d, slots, :].unsqueeze(1).to_broadcast([64, PAIRS, slots.stop - slots.start, C])

                        for d in DIRS:
                            ga, gb = (ps[:, 2 * d + g, :].rearrange("p (a s c) -> p a s c", a=PAIRS, s=2) for g in range(2))
                            dve.wait_ge(l_gram[d], 1)
                            dve.tensor_tensor(Ub[d][lo, :, 0:64], ga[lo, :, 0], mask(d, lo, slice(0, 1))[:, :, 0], ALU.mult).then_inc(l_u[d], 1)
                            dve.wait_ge(l_gram[d], 2)
                            dve.tensor_tensor(Ub[d][hi, :, 64:128], gb[hi, :, 1], mask(d, hi, slice(0, 1))[:, :, 0], ALU.mult).then_inc(l_u[d], 1)
                            dve.tensor_tensor(GR[d][hi, :, 0:2, :], ga[hi], mask(d, hi, slice(0, 2)), ALU.mult)
                            dve.tensor_tensor(GR[d][lo, :, 2:4, :], gb[lo], mask(d, lo, slice(1, 3)), ALU.mult)
                            dve.tensor_tensor(AB[d][lo], ga[lo, :, 1], mask(d, lo, slice(1, 2))[:, :, 0], ALU.mult)
                            dve.tensor_tensor(AB[d][hi], gb[hi, :, 0], mask(d, hi, slice(1, 2))[:, :, 0], ALU.mult).then_inc(l_g[d], 1)
                        for d in DIRS:
                            dve.wait_ge(l_um[d], 1)
                            dve.tensor_tensor(Y[d], eye[:, :].unsqueeze(1).to_broadcast([P, PAIRS, P]), Um[d],
                                              ALU.subtract).then_inc(l_Y[d], 1)
                            dve.wait_ge(l_Y[d], 1)
                            dve.transpose(X[d], Y[d]).then_inc(l_X[d], 1)
                        for l in range(1, LEVELS):
                            for d in DIRS:
                                dve.wait_ge(l_Q[d], l)
                                dve.tensor_tensor(Y[d], Y[d], pairs(2 * d + 1, P), ALU.subtract).then_inc(l_Y[d], 1)
                                if l < LEVELS - 1:
                                    dve.wait_ge(l_Y[d], l + 1)
                                    dve.transpose(X[d], Y[d]).then_inc(l_X[d], 1)
                        for d in DIRS:
                            dve.wait_ge(l_S[d], 1)
                            yc = chunk(y, d)
                            link(dve.tensor_tensor(yc, yc, pairs(6 + d, C), ALU.add))
                            s = ps[:, 6 + d, 256:512].rearrange("p (a c) -> p a c", a=PAIRS)
                            end = C - 1 if d == 0 else 0
                            for g, r in ((0, lo), (1, hi)):
                                dve.tensor_tensor(SU[d][r, 0, :, g, :], SU[d][r, 0, :, g, :], s[r], ALU.add).then_inc(l_S2, 1)
                            dve.wait_ge(l_S2, 2 * d + 2)
                            for g, r in ((0, lo), (1, hi)):
                                dve.tensor_tensor(SU[d][r, 0, :, g, :], SU[d][r, 0, :, g, :],
                                                  eA[r, :, d, end:end + 1].to_broadcast([64, PAIRS, C]), ALU.mult)
                nc.all_engine_barrier(sems_to_clear=range(nums[0], nums[-1] + 1))

        scan(TP, SEQ // C)

        state_in = state_rwkv[0, 0].rearrange("d (a g) v k -> d g v a k", g=2)
        state_out = new_state[0, 0].rearrange("d (a g) v k -> d g v a k", g=2)
        with nc.Block() as block:
            @block.sync
            def _(sp):
                sp.wait_ge(s_sz, 1)
                for d in DIRS:
                    for g in range(2):
                        r = slice(64 * g, 64 * g + 64)
                        sp.dma_start(stin[d].rearrange("p (a k) -> p a k", a=PAIRS)[r, :, r], state_in[d, g]).then_inc(s_sl, 16)
                sp.wait_ge(s_sc2, 1)
                for d in DIRS:
                    for g in range(2):
                        r = slice(64 * g, 64 * g + 64)
                        sp.dma_start(state_out[d, g], sout[d][r, :, r]).then_inc(s_ns, 16)
                sp.wait_ge(s_ns, 64)

            @block.tensor
            def _(pe):
                for d in DIRS:
                    for a in range(PAIRS):
                        last = pe.transpose(pairs(d, P)[:, a, :], SU[d][:, 0, a].rearrange("p b c -> p (b c)"), eye[:, :])
                last.then_inc(s_so, 1)
                pe.wait_ge(s_sl, 64)
                for d in DIRS:
                    for a in range(PAIRS):
                        last = pe.transpose(pairs(2 + d, P)[:, a, :], stin[d][:, P * a:P * a + P], eye[:, :])
                last.then_inc(s_st, 1)

            @block.vector
            def _(dve):
                dve.memset(stin[0], 0.0)
                dve.memset(stin[1], 0.0).then_inc(s_sz, 1)
                dve.wait_ge(s_so, 1)
                dve.tensor_copy(sout[0], pairs(0, P))
                dve.tensor_copy(sout[1], pairs(1, P)).then_inc(s_sc2, 1)
                dve.wait_ge(s_st, 1)
                for d in DIRS:
                    dve.tensor_copy(SU[d][:, 0].rearrange("p a b c -> p a (b c)"), pairs(2 + d, P))

        scan(TS, DEC_SEQ // C)

        take = carve()
        gt = take(4, W)
        sq, sd = take(W), take(W)
        XO = 3
        xr = take(XO, D_MODEL)
        gg = take(2, D_MODEL)
        grow, gb2, gpr = take(D_MODEL), take(D_MODEL), take(D_MODEL)
        sel = take(2, P)
        jk = take(D_MODEL)
        yab = kkT
        wo = zflat[:, 0:8 * D_MODEL].rearrange("p (k n) -> p k n", k=8)

        gwf = zflat[:, 12 * W:12 * W + 4 * D_MODEL].rearrange("p (k n) -> p k n", k=4)
        def gt2(i):
            return gt.rearrange("p a w -> p (a w)")[:, D_MODEL * (i % 2):D_MODEL * (i % 2) + D_MODEL]

        ss2, rs2 = small[:, 0:9], small[:, 9:18]

        s_gl = sem("gate_c_landed")
        s_wo = sem("w_out_landed")
        s_ab = sem("branches_landed")
        s_gw = sem("gate_weights_landed")
        s_gv = sem("gate_vectors_landed")
        s_gm = sem("gate_multiplied")
        s_gr = sem("gate_row_ready")
        s_gbc = sem("gate_broadcast")
        s_gcp = sem("gate_copied")
        s_sel = sem("selectors_ready")
        s_yc = sem("yc_ready")
        f_dve = sem("final_dve_chain")
        f_pm = sem("gn_mean_summed")
        f_xc = sem("gn_centred")
        f_sq = sem("gn_squared")
        f_pv = sem("gn_variance_summed")
        f_sd = sem("gn_deviation_ready")
        f_bq = sem("bonus_scaled")
        f_pb = sem("bonus_summed")
        f_bd = sem("bonus_read")
        s_xr = [sem(f"residual_landed_{i}") for i in range(XO)]
        s_o = sem("output_multiplied")
        s_oq = sem("output_squared")
        s_om = sem("output_mean_square")
        s_os = sem("output_deviation_ready")
        s_og = sem("output_gated")
        s_or = sem("output_ready")
        s_st2 = [sem(f"output_stored_{i}") for i in range(XO)]

        with nc.Block() as block:
            @block.sync
            def _(sp):
                def store(i):
                    sp.wait_ge(s_or, i + 1)
                    sp.dma_start(y_prompt[0] if i == 0 else y_sample[0, P * (i - 1):P * i, :],
                                 xr[:, i % XO, :]).then_inc(s_st2[i % XO], 16)

                sp.dma_start(gt, mix_dram[4:8].rearrange("m p w -> p m w")).then_inc(s_gl, 16)
                for g in range(2):
                    if g:
                        sp.wait_ge(s_gm, 1)
                    sp.dma_start(gwf, ada_w[0, 512 * g:512 * g + 512, 2048:3072].rearrange("(k p) n -> p k n", p=P)).then_inc(s_gw, 16)
                sp.dma_start(wo, w_out[0].rearrange("(k p) n -> p k n", p=P)).then_inc(s_wo, 16)
                for s in range(2):
                    sp.dma_start(gb2[s:s + 1, :], ada_b[:, 2048:3072]).then_inc(s_gv, 16)
                    sp.dma_start(gpr[s:s + 1, :], g_post).then_inc(s_gv, 16)
                sp.wait_ge(s_gm, 2)
                sp.dma_start(yab, mix_dram[0:4].rearrange("m p w -> p m w")).then_inc(s_ab, 16)
                for i in range(9):
                    if i >= XO:
                        sp.wait_ge(s_st2[i % XO], 16 * (i // XO))
                    sp.dma_start(xr[:, i % XO, :], x_prompt[0] if i == 0 else x_sample[0, P * (i - 1):P * i, :]).then_inc(s_xr[i % XO], 16)
                    if i >= XO - 1:
                        store(i - XO + 1)
                for i in range(9 - XO + 1, 9):
                    store(i)
                for i in range(XO):
                    sp.wait_ge(s_st2[i], 16 * 3)

            @block.gpsimd
            def _(pool):
                pool.memset(sel[0:2], 1.0).then_inc(s_sel, 1)
                pool.wait_ge(s_sel, 1)
                pool.affine_select(out=sel[0:2], in_=sel[0:2], compare_op=ALU.is_equal, fill=0.0, base=0,
                                   pattern=[[-1, 2], [0, P]], channel_multiplier=1).then_inc(s_sel, 1)

            @block.tensor
            def _(pe):
                mods = smod[:, :].rearrange("p (s k) -> p k s", k=KT)
                for k in range(KT):
                    if k % 4 == 0:
                        pe.wait_ge(s_gw, 16 * (k // 4 + 1))
                    for b in range(2):
                        last = pe.matmul(ps[0:2, b, :], mods[:, k, :], gwf[:, k % 4, 512 * b:512 * b + 512],
                                         start=(k == 0), stop=(k == KT - 1))
                    if k % 4 == 3:
                        last.then_inc(s_gm, 1)

                n = 0
                for a in range(4):
                    for b in range(NB):
                        cut = slice(b * NC, (b + 1) * NC)
                        if n:
                            pe.wait_ge(f_xc, n)
                        pe.matmul(ps[:, 2, 0:NC], heads[:, :], y[:, a, cut], start=True, stop=True).then_inc(f_pm, 1)
                        pe.wait_ge(f_bq, a + 1)
                        if n:
                            pe.wait_ge(f_bd, n)
                        pe.matmul(ps[:, 4, 0:NC], heads[:, :], q[:, a, cut], start=True, stop=True).then_inc(f_pb, 1)
                        pe.wait_ge(f_sq, n + 1)
                        if n:
                            pe.wait_ge(f_sd, n)
                        pe.matmul(ps[:, 3, 0:NC], heads[:, :], sq[:, cut], start=True, stop=True).then_inc(f_pv, 1)
                        n += 1
                pe.wait_ge(s_gr, 1)
                pe.wait_ge(s_sel, 2)
                for s in range(2):
                    if s:
                        pe.wait_ge(s_gcp, 1)
                    for b in range(2):
                        last = pe.matmul(ps[:, 6 + b, :], sel[0:2, s, :], grow[0:2, 512 * b:512 * b + 512], start=True, stop=True)
                    last.then_inc(s_gbc, 1)
                pe.wait_ge(s_wo, 16)
                pe.wait_ge(s_ab, 16)
                pe.wait_ge(s_yc, 4)
                for i in range(9):
                    at = TP if i == 0 else TS + P * (i - 1)
                    if i >= 3:
                        pe.wait_ge(s_og, i - 2)
                    for b in range(2):
                        for k in range(8):
                            src = yab[:, k, at:at + P] if k < 4 else y[:, k - 4, at:at + P]
                            last = pe.matmul(ps[:, 2 * (i % 3) + b, :], src, wo[:, k, 512 * b:512 * b + 512],
                                             start=(k == 0), stop=(k == 7))
                    last.then_inc(s_o, 1)

            @block.scalar
            def _(act):
                n = 0
                for a in range(4):
                    act.activation(q[:, a, :], q[:, a, :], ACT.Copy, scale=col("r_k", a)).then_inc(f_bq, 1)
                    for b in range(NB):
                        cut = slice(b * NC, (b + 1) * NC)
                        act.wait_ge(f_xc, n + 1)
                        act.activation(sq[:, cut], y[:, a, cut], ACT.Square).then_inc(f_sq, 1)
                        act.wait_ge(f_pv, n + 1)
                        act.activation(sd[:, cut], ps[:, 3, 0:NC], ACT.Sqrt, bias=epst[:, 3:4], scale=1.0 / HEAD).then_inc(f_sd, 1)
                        n += 1
                for i in range(9):
                    act.wait_ge(s_o, i + 1)
                    b = 2 * (i % 3)
                    act.activation(jk, ps[:, b:b + 2, :].rearrange("p b n -> p (b n)"), ACT.Square,
                                   accum_out=ss2[:, i:i + 1]).then_inc(s_oq, 1)
                    act.wait_ge(s_oq, i + 1)
                    act.activation(ss2[:, i:i + 1], ss2[:, i:i + 1], ACT.Sqrt, bias=epst[:, 0:1], scale=1.0 / D_MODEL).then_inc(s_os, 1)

            @block.vector
            def _(dve):
                n_dve = [0]

                def link(ins):
                    n_dve[0] += 1
                    ins.then_inc(f_dve, 1)
                    dve.wait_ge(f_dve, n_dve[0])

                dve.wait_ge(s_gm, 2)
                dve.wait_ge(s_gv, 64)
                link(dve.tensor_tensor(grow[0:2, :], ps[0:2, 0:2, :].rearrange("p b n -> p (b n)"), gb2[0:2, :], ALU.add))
                dve.tensor_tensor(grow[0:2, :], grow[0:2, :], gpr[0:2, :], ALU.mult).then_inc(s_gr, 1)
                dve.wait_ge(s_gl, 16)
                n = 0
                for a in range(4):
                    for b in range(NB):
                        cut = slice(b * NC, (b + 1) * NC)
                        dve.wait_ge(f_pm, n + 1)
                        dve.scalar_tensor_tensor(out=y[:, a, cut], in0=ps[:, 2, 0:NC], scalar=-1.0 / HEAD, in1=y[:, a, cut],
                                                 op0=ALU.mult, op1=ALU.add).then_inc(f_xc, 1)
                        dve.wait_ge(f_pb, n + 1)
                        dve.tensor_tensor(vT[:, a, cut], vT[:, a, cut], ps[:, 4, 0:NC], ALU.mult).then_inc(f_bd, 1)
                        dve.wait_ge(f_sd, n + 1)
                        link(dve.reciprocal(sd[:, cut], sd[:, cut]))
                        link(dve.tensor_tensor(y[:, a, cut], y[:, a, cut], sd[:, cut], ALU.mult))
                        n += 1
                    link(dve.tensor_scalar(y[:, a, :], y[:, a, :], col("gn_g", a), col("gn_b", a), ALU.mult, ALU.add))
                    link(dve.tensor_tensor(y[:, a, :], y[:, a, :], vT[:, a, :], ALU.add))
                    dve.scalar_tensor_tensor(out=y[:, a, :], in0=gt[:, a, :], scalar=0.5, in1=y[:, a, :],
                                             op0=ALU.mult, op1=ALU.mult).then_inc(s_yc, 1)
                for s in range(2):
                    dve.wait_ge(s_gbc, s + 1)
                    dve.tensor_copy(gg[:, s, :], ps[:, 6:8, :].rearrange("p b n -> p (b n)")).then_inc(s_gcp, 1)
                for i in range(9):
                    b, slot = 2 * (i % 3), i % XO
                    dve.wait_ge(s_os, i + 1)
                    link(dve.reciprocal(rs2[:, i:i + 1], ss2[:, i:i + 1]))
                    dve.wait_ge(s_gcp, 2)
                    dve.scalar_tensor_tensor(out=gt2(i), in0=ps[:, b:b + 2, :].rearrange("p b n -> p (b n)"),
                                             scalar=rs2[:, i:i + 1], in1=gg[:, min(i, 1), :],
                                             op0=ALU.mult, op1=ALU.mult).then_inc(s_og, 1)
                    dve.wait_ge(s_og, i + 1)
                    dve.wait_ge(s_xr[slot], 16 * (i // XO + 1))
                    dve.tensor_tensor(xr[:, slot, :], xr[:, slot, :], gt2(i), ALU.add).then_inc(s_or, 1)


_INS = ["x_prompt", "x_sample", "c", "state_rwkv", "c_ctx", "ada_w", "ada_b", "g_pre", "g_post", "w_in",
        "conv_a", "conv_b", "conv_b_bias", "ln_b_g", "ln_b_b", "mu", "w0", "w2", "a0", "a2", "k_k", "k_a",
        "r_k", "gn_g", "gn_b", "w_out"]
_OUTS = [(1, SEQ, D_MODEL), (1, DEC_SEQ, D_MODEL), (1, 1, 2, 8, 64, 64)]


def kernel(**inputs):
    import numpy as _np
    import concourse.bacc as _bacc
    from concourse import mybir as _mybir
    from concourse.bass_utils import run_bass_kernel_spmd as _run

    nc = _bacc.Bacc("TRN2", target_bir_lowering=False, num_devices=1)
    arrays, args = {}, []
    for name in _INS:
        a = _np.ascontiguousarray(inputs[name])
        arrays[f"in_{name}"] = a
        args.append(nc.dram_tensor(f"in_{name}", a.shape, _mybir.dt.from_np(a.dtype), kind="ExternalInput").ap())
    for i, shape in enumerate(_OUTS):
        args.append(nc.dram_tensor(f"out_{i}", shape, _mybir.dt.float32, kind="ExternalOutput").ap())
    hybrid_step_kernel(nc, *args)
    r = _run(nc, [arrays], core_ids=[0])
    return tuple(r.results[0][f"out_{i}"] for i in range(len(_OUTS)))
```

```python
from contextlib import ExitStack

import concourse.bass as bass
from concourse import mybir

ALU = mybir.AluOpType
ACT = mybir.ActivationFunctionType
F32 = mybir.dt.float32
F32R = mybir.dt.float32r

P = 128
D_MODEL = 1024
KT = D_MODEL // P
SEQ, DEC_SEQ = 128, 1024
GRID_W = 64
ROWS = DEC_SEQ // GRID_W
TP, TS = 2, 132
W = TS + DEC_SEQ + 2
NB = 3
NC = W // NB
D_MIX = 1024
CONV_A, CONV_B = 3, 31
HEAD = 64
C = 64
PAIRS = 4
LEVELS = 6
UNROLL = 4
E_HALF = 0.6065306597126334
RMS_EPS, LN_EPS, GN_EPS, KK_EPS = 1e-6, 1e-5, 64e-5, 1e-12

VEC_ROWS = {}
_n = 0
for _name, _rows in (("c_ctx", 8), ("c", 8), ("g_pre", 8), ("conv_b_bias", 2), ("ln_b_g", 2), ("ln_b_b", 2),
                     ("mu", 14), ("w0", 8), ("a0", 8), ("k_k", 4), ("k_a", 4), ("r_k", 4), ("gn_g", 4),
                     ("gn_b", 4), ("conv_a", 6)):
    VEC_ROWS[_name] = (_n, _rows)
    _n += _rows
N_VEC = _n
N_CB = 2 * CONV_B


PIECES = [("gc", 14), ("gc", 15), ("u2", 5), ("u1", 4), ("gb", 6), ("xa", 0), ("cg", 2), ("bg", 1), ("ga", 3),
          ("mix", 7), ("mix", 8), ("mix", 9), ("mix", 10), ("mix", 11), ("mix", 12), ("mix", 13)]
TILES = [kind for kind, _ in PIECES for _ in range(2)]
MIX0 = TILES.index("mix")
MIXES = TILES.count("mix")
RING = 3
PIECE = 2048
N_ADA = KT
GATE_AFTER = 2
LOADS = [("ada", k) for k in range(KT)] + [("z", n) for n in range(GATE_AFTER)] + \
        [("gate", k) for k in range(KT // 2)] + [("z", n) for n in range(GATE_AFTER, len(PIECES))]
HT_BANKS = [(k, TP, P, 0, 0) for k in range(KT)] + \
           [(k, TS + 512 * g, 512, 1 + 4 * g, 1) for g in range(2) for k in range(KT)]


def hybrid_step_kernel(nc, x_prompt, x_sample, c, state_rwkv, c_ctx, ada_w, ada_b, g_pre, g_post, w_in,
                       conv_a, conv_b, conv_b_bias, ln_b_g, ln_b_b, mu, w0, w2, a0, a2, k_k, k_a,
                       r_k, gn_g, gn_b, w_out, y_prompt, y_sample, new_state):
    ctx = ExitStack()
    with ctx:
        def sb(name, *shape):
            return ctx.enter_context(nc.sbuf_tensor(name, [P, *shape], F32))

        def place(tensor):
            return nc.sbuf_base - tensor_bytes(tensor)

        def tensor_bytes(tensor):
            n = 4
            for size in tensor.shape[1:]:
                n *= size
            return n

        def rounded(name, at, *shape):
            return nc.alloc_sbuf_tensor_at(name, [P, *shape], F32R, offset=at)[:, :, :]

        def sem(name):
            return ctx.enter_context(nc.semaphore(name))

        ps = ctx.enter_context(nc.psum_tensor("ps", [P, 8, 512], F32))
        gate_dram = nc.dram_tensor("gate_scratch", [2, D_MODEL], F32, kind="Internal").ap()
        mix_dram = nc.dram_tensor("mix_scratch", [8, P, W], F32, kind="Internal").ap()

        hT = sb("hT", KT, W)
        hT_at = place(hT)
        y = hT[:, 0:4, :]
        q = hT[:, 4:8, :]
        zc = sb("zc", 18, W)
        zc_at = place(zc)
        vT, kT, rT, kkT = (zc[:, 4 * n:4 * n + 4, :] for n in range(4))
        lwT, laT = zc[:, 16, :], zc[:, 17, :]
        zflat = zc[:, :, :].rearrange("p a w -> p (a w)")
        xtok = zflat[:, 0:9 * D_MODEL].rearrange("p (i d) -> p i d", i=9)
        ARENA = 19520
        arena = sb("arena", ARENA)
        arena_at = place(arena)
        vec = sb("vec", N_VEC)
        cb = sb("cb", N_CB)
        cah = sb("cah", 6)
        smod = sb("smod", 16)
        hmu = sb("hmu", 14)
        omu = sb("omu", 14)
        shf = sb("shf", KT, 2)
        scl = sb("scl", KT, 2)
        small = sb("small", 36)
        epst = sb("epst", 4)
        lvl = sb("lvl", LEVELS, P)
        eye = sb("eye", P)
        heads = sb("heads", P)
        back = sb("back", P)
        ones = sb("ones", P)
        tri = sb("tri", 2, 3, C)
        w2s = sb("w2s", 512)
        a2s = sb("a2s", 512)

        def carve(start=0):
            at = [start]

            def take(*shape):
                n = 1
                for s in shape:
                    n *= s
                v = arena[:, at[0]:at[0] + n]
                at[0] += n
                assert at[0] <= ARENA, at[0]
                if len(shape) == 1:
                    return v
                names = "abcd"[:len(shape)]
                return v.rearrange(f"p ({' '.join(names)}) -> p {' '.join(names)}",
                                   **{names[i]: shape[i] for i in range(len(shape))})
            return take

        def cols(name):
            return vec[:, VEC_ROWS[name][0]:VEC_ROWS[name][0] + VEC_ROWS[name][1]]

        def col(name, i):
            return cols(name)[:, i:i + 1]


        DIRS = range(2)
        step_sems = []

        def ssem(name):
            s = sem(name)
            step_sems.append(s)
            return s

        l_stage = ssem("lora_input_staged")
        l_lora = ssem("lora_multiplied")
        l_x = ssem("lora_bias_added")
        l_tanh = ssem("gates_tanh_ready")
        l_dve = ssem("step_dve_chain")
        l_pool = ssem("step_pool_chain")
        l_q = ssem("bonus_key_summed")
        l_log = ssem("log_decay_ready")
        l_exp = ssem("decay_ready")
        l_end = ssem("chunk_decay_copied")
        l_kd = ssem("kd_over_decay_ready")
        l_kf = ssem("kd_ready")
        l_a = ssem("a_ready")
        l_b = ssem("b_ready")
        l_sum = ssem("state_summed")
        l_ops = [ssem(f"operands_ready_{d}") for d in DIRS]
        l_gram = [ssem(f"products_ready_{d}") for d in DIRS]
        l_vd = [ssem(f"v_doubled_{d}") for d in DIRS]
        l_vt = [ssem(f"v_transposed_{d}") for d in DIRS]
        l_kt = [ssem(f"keys_transposed_{d}") for d in DIRS]
        l_v = [ssem(f"v_by_token_{d}") for d in DIRS]
        l_kb = [ssem(f"keys_by_token_{d}") for d in DIRS]
        l_u = [ssem(f"m_b_masked_{d}") for d in DIRS]
        l_g = [ssem(f"products_masked_{d}") for d in DIRS]
        l_um0 = [ssem(f"first_levels_masked_{d}") for d in DIRS]
        l_um = [ssem(f"level_masked_{d}") for d in DIRS]
        l_Y0 = [ssem(f"inverse_of_twos_transposed_{d}") for d in DIRS]
        l_X0 = [ssem(f"inverse_of_twos_{d}") for d in DIRS]
        l_X = [ssem(f"inverse_ready_{d}") for d in DIRS]
        l_Y = [ssem(f"inverse_transposed_ready_{d}") for d in DIRS]
        l_P = [ssem(f"level_product_{d}") for d in DIRS]
        l_pc = [ssem(f"level_factor_ready_{d}") for d in DIRS]
        l_Q = [ssem(f"level_update_{d}") for d in DIRS]
        l_rhs = [ssem(f"rhs_multiplied_{d}") for d in DIRS]
        l_rh = [ssem(f"rhs_copied_{d}") for d in DIRS]
        l_U = [ssem(f"u_multiplied_{d}") for d in DIRS]
        l_uc = [ssem(f"u_copied_{d}") for d in DIRS]
        l_S = [ssem(f"outputs_multiplied_{d}") for d in DIRS]
        l_st = [ssem(f"state_ready_{d}") for d in DIRS]
        nums = [s.num for s in step_sems]
        assert nums == list(range(nums[0], nums[0] + len(nums)))

        take = carve()
        ring = take(RING, PIECE)
        take(2, PIECE)
        lo2 = take(4, W)
        raw = take(2, W)
        nsum = take(W)
        kn = take(W)
        w_rest = rounded("weights_rest", arena_at, RING, PIECE)
        w_round = rounded("weights_rounded", arena_at + 4 * RING * PIECE, 2, PIECE)
        lo2_r = rounded("input_rest_2", arena_at + 4 * (RING + 2) * PIECE, 4, W)
        kk_r = rounded("input_rest_1", zc_at + 4 * 12 * W, 4, W)
        hi_of_h = rounded("input_rounded", hT_at, KT, W)
        lo_full = [kkT[:, k, :] if k < 4 else lo2[:, k - 4, :] for k in range(KT)]
        lo_of_h = [kk_r[:, k, :] if k < 4 else lo2_r[:, k - 4, :] for k in range(KT)]
        T = zc[:, 0:8, :]
        xa, ya = rT, zc[:, 16:18, :]
        va, vb = raw[:, 0, 0:P], raw[:, 0, P:2 * P]
        junk = kn[:, 16:16 + D_MODEL]
        spare = rT.rearrange("p a w -> p (a w)")
        row, adab = spare[0:2, 0:2048], spare[0:2, 2048:4096]
        grow, gpost = zc[0:2, 16, 0:D_MODEL], zc[0:2, 17, 0:D_MODEL]
        blocks = raw[:, 1, 0:7 * P].rearrange("p (l j) -> p l j", l=7)
        triw = nsum[:, 0:4 * P].rearrange("p (l j) -> p l j", l=4)
        ss, rs = small[:, 0:9], small[:, 9:18]

        part1 = ExitStack()

        def sem1(name):
            s = part1.enter_context(nc.semaphore(name))
            sems1.append(s.num)
            return s

        sems1 = []
        s_vec = sem1("vectors_landed")
        s_w2 = sem1("lora_landed")
        s_x = [sem1(f"x_landed_{i}") for i in range(3)]
        s_adab = sem1("ada_b_landed")
        s_wl = [sem1(f"weights_landed_{i}") for i in range(RING)]
        s_wu = sem1("weights_used")
        s_wh = sem1("weights_rounded")
        s_wo1 = sem1("weights_rest_ready")
        s_hf = sem1("hT_copied_full")
        s_hs = [sem1("hT_rest_by_pool"), sem1("hT_rest_by_dve")]
        s_gu = sem1("gate_weights_used")
        s_gr = sem1("gate_row_ready")
        s_gst = sem1("gate_row_stored")
        s_const = sem1("constants_built")
        s_pool = sem1("pool_chain")
        s_dve = sem1("dve_chain")
        s_act = sem1("act_chain")
        s_vt = sem1("vectors_transposed")
        s_vc = sem1("vectors_copied")
        s_tm = sem1("tanh_of_modulation")
        s_smod = sem1("silu_of_modulation")
        s_row = sem1("ada_rows_copied")
        s_at = sem1("ada_transposed")
        s_sc = sem1("scale_shift_ready")
        s_ss = sem1("squares_summed")
        s_ms = sem1("mean_square_ready")
        s_sd = sem1("x_deviation_ready")
        s_xn = sem1("x_normalised")
        s_xt = sem1("x_transposed")
        s_ha = sem1("hT_written_by_act")
        s_z = sem1("tile_projected")
        s_th = sem1("tanh_ready")
        s_glu = sem1("glu_ready")
        s_gb = sem1("gate_b_ready")
        s_xa = sem1("xa_copied")
        s_cx = sem1("cg_times_xa_ready")
        s_bg = sem1("bg_applied")
        s_ya = sem1("ya_ready")
        s_raw = sem1("raw_copied")
        s_sum = sem1("neighbours_summed")
        s_mix = sem1("shift_mixed")
        s_lwt = sem1("lw_tanh_ready")
        s_cv = sem1("conv_b_done")
        s_lm = sem1("ln_mean_summed")
        s_lx = sem1("ln_centred")
        s_lq = sem1("ln_squared")
        s_lv = sem1("ln_variance_summed")
        s_ls = sem1("ln_deviation_ready")
        s_lr = sem1("ln_scaled")
        s_lt = sem1("ln_tanh_ready")
        s_yb = sem1("yb_ready")
        s_kq = sem1("kk_squared")
        s_ks = sem1("kk_square_summed")
        s_kd = sem1("kk_deviation_ready")
        s_kr = sem1("kk_deviation_inverted")
        s_kp = sem1("kk_deviation_spread")
        s_kn = sem1("kk_normalised")
        s_zero = sem1("scan_outputs_zero")
        s_gc = sem1("gate_c_ready")
        s_sa = sem1("ya_spilled")
        s_sb = sem1("yb_spilled")
        s_sg = sem1("gate_c_spilled")

        def dest(m):
            return zc[:, m + 8 if m < 4 else m if m < 8 else m - 8 if m < 12 else m + 4, :]

        def zbanks(j):
            return ps[:, NB * (j % 2):NB * (j % 2) + NB, 0:NC]

        def as3(a):
            return a.rearrange("p (n w) -> p n w", n=NB)

        def read_by(j):
            i = j - TILES.index(TILES[j])
            if TILES[j] == "u2":
                i += TILES.count("gc")
            return {"u2": s_th, "u1": s_glu, "gb": s_gb, "xa": s_xa, "cg": s_cx, "bg": s_bg, "ga": s_ya,
                    "mix": s_raw, "gc": s_gc}[TILES[j]], i + 1

        with nc.Block() as block:
            @block.sync
            def _(sp):
                def flat(a):
                    names = "abcd"[:len(a.shape)]
                    return a if len(names) == 1 else a.rearrange(f"{' '.join(names)} -> ({' '.join(names)})")

                given = {"c_ctx": c_ctx, "c": c, "g_pre": g_pre, "conv_b_bias": conv_b_bias, "ln_b_g": ln_b_g,
                         "ln_b_b": ln_b_b, "mu": mu, "w0": w0, "a0": a0, "k_k": k_k, "k_a": k_a, "r_k": r_k,
                         "gn_g": gn_g, "gn_b": gn_b, "conv_a": conv_a}
                for name, (r0, n) in VEC_ROWS.items():
                    sp.dma_start(va[r0:r0 + n, :], flat(given[name]).rearrange("(r p) -> r p", p=P)).then_inc(s_vec, 16)
                sp.dma_start(vb[0:N_CB, :], conv_b.rearrange("a j (h p) -> (a j h) p", p=P)).then_inc(s_vec, 16)

                def spill(first, tiles, ready, count, spilled):
                    sp.wait_ge(ready, count)
                    sp.dma_start(mix_dram[first:first + 2].rearrange("m p w -> p m w"), tiles).then_inc(spilled, 16)

                for n, (kind, k) in enumerate(LOADS):
                    if n >= RING:
                        before, m = LOADS[n - RING]
                        used, per = {"ada": (s_wu, 1), "gate": (s_gu, 1), "z": (s_z, 2)}[before]
                        sp.wait_ge(used, per * (m + 1))
                    slot = ring[:, n % RING, :]
                    if kind == "ada":
                        sp.dma_start(slot, ada_w[0, k * P:(k + 1) * P, 0:2048]).then_inc(s_wl[n % RING], 16)
                    elif kind == "gate":
                        sp.dma_start(slot.rearrange("p (k n) -> p k n", k=2),
                                     ada_w[0, 2 * k * P:2 * (k + 1) * P, 2048:3072].rearrange("(k p) n -> p k n", p=P)).then_inc(s_wl[n % RING], 16)
                    else:
                        at = 256 * PIECES[k][1]
                        sp.dma_start(slot.rearrange("p (k n) -> p k n", k=KT),
                                     w_in[0, :, at:at + 256].rearrange("(k p) n -> p k n", p=P)).then_inc(s_wl[n % RING], 16)
                    if n == 0:
                        for s in range(2):
                            sp.dma_start(adab[s:s + 1, :], ada_b[:, 0:2048]).then_inc(s_adab, 16)
                            sp.dma_start(grow[s:s + 1, :], ada_b[:, 2048:3072]).then_inc(s_adab, 16)
                            sp.dma_start(gpost[s:s + 1, :], g_post).then_inc(s_adab, 16)
                    if (kind, k) == ("z", GATE_AFTER + 1):
                        sp.wait_ge(s_gr, 1)
                        sp.dma_start(gate_dram, grow).then_inc(s_gst, 16)
                    if (kind, k) == ("z", 4):
                        spill(4, T[:, 4:6, :], s_gc, 2, s_sg)
                    if (kind, k) == ("z", 5):
                        spill(6, T[:, 6:8, :], s_gc, 4, s_sg)
                    if (kind, k) == ("z", MIX0 // 2 + RING):
                        spill(0, ya, s_ya, 2, s_sa)
                    if (kind, k) == ("z", MIX0 // 2 + RING + 1):
                        spill(2, T[:, 6:8, :], s_yb, 2, s_sb)
                sp.wait_ge(s_gst, 16)
                sp.wait_ge(s_sg, 32)
                sp.wait_ge(s_sa, 16)
                sp.wait_ge(s_sb, 16)

            @block.gpsimd
            def _(pool):
                n_pool = [0]

                def link(ins):
                    n_pool[0] += 1
                    ins.then_inc(s_pool, 1)
                    pool.wait_ge(s_pool, n_pool[0])

                link(pool.memset(blocks, 1.0))
                for l in range(7):
                    b = 1 << l
                    m = blocks[:, l, :].rearrange("p (n b) -> p n b", b=b)
                    link(pool.affine_select(out=m, in_=m, compare_op=ALU.is_ge, fill=0.0, base=0,
                                            pattern=[[-b, P // b], [0, b]], channel_multiplier=1))
                    link(pool.affine_select(out=m, in_=m, compare_op=ALU.is_ge, fill=0.0, base=b - 1,
                                            pattern=[[b, P // b], [0, b]], channel_multiplier=-1))
                    if l == 0:
                        pool.tensor_copy(eye[:, :], blocks[:, 0, :]).then_inc(s_const, 1)
                pool.tensor_copy(heads[:, :], blocks[:, 6, :])
                pool.tensor_tensor(lvl[:, :, :], blocks[:, 1:7, :], blocks[:, 0:6, :], ALU.subtract)
                pool.memset(ones[:, :], 1.0 / 256)
                link(pool.memset(triw, 1.0))
                for n, (sign, base) in enumerate(((1, -1), (1, 0), (-1, -1), (-1, 0))):
                    link(pool.affine_select(out=triw[:, n, :], in_=triw[:, n, :], compare_op=ALU.is_ge, fill=0.0,
                                            base=base, pattern=[[sign, P]], channel_multiplier=-sign))
                for d in range(2):
                    for half in range(2):
                        r = slice(64 * half, 64 * half + 64)
                        for slot, kind in enumerate((0, 1, 0)):
                            link(pool.tensor_copy(tri[r, d, slot, :], triw[r, 2 * d + kind, r]))
                for n, e in enumerate((RMS_EPS, LN_EPS, KK_EPS, GN_EPS)):
                    pool.memset(epst[:, n:n + 1], e)
                link(pool.memset(back[:, :], 0.0))
                for a in range(4):
                    link(pool.affine_select(out=back[:, :], in_=back[:, :], compare_op=ALU.not_equal, fill=1.0, base=-32 * a,
                                            pattern=[[-16, 2], [0, HEAD]], channel_multiplier=1))
                link(pool.memset(kn[:, 0:16], 0.0))
                for a in (0, TS - 2, W - 2):
                    for v, n in ((hi_of_h, KT), (kk_r, 4), (lo2_r, 4)):
                        last = pool.tensor_copy(v[:, :, a:a + 2], kn[:, 0:2 * n].rearrange("p (k c) -> p k c", c=2))
                last.then_inc(s_const, 1)
                for n in range(0, len(HT_BANKS), 2):
                    k, at, w, _, s = HT_BANKS[n]
                    pool.wait_ge(s_hf, n + 1)
                    pool.tensor_tensor(lo_of_h[k][:, at:at + w], lo_full[k][:, at:at + w], hi_of_h[:, k, at:at + w].bitcast(F32),
                                       ALU.subtract).then_inc(s_hs[0], 1)

                def split_rest(p):
                    slot = ring[:, LOADS.index(("z", p)) % RING, :]
                    pool.wait_ge(s_wh, p + 1)
                    pool.tensor_tensor(w_rest[:, LOADS.index(("z", p)) % RING, :], slot, w_round[:, p % 2, :].bitcast(F32), ALU.subtract).then_inc(s_wo1, 1)

                split_rest(0)
                for j in range(len(TILES)):
                    if j % 2 == 0 and j // 2 + 1 < len(PIECES):
                        split_rest(j // 2 + 1)
                    m = j - MIX0
                    if m >= 0:
                        if m:
                            pool.wait_ge(s_mix, m)
                        pool.wait_ge(s_raw, m + 1)
                        pool.tensor_tensor(nsum[:, 1:W - 1], raw[:, m % 2, 0:W - 2], raw[:, m % 2, 2:W], ALU.add).then_inc(s_sum, 1)
                pool.wait_ge(s_z, len(TILES))
                pool.memset(hT[:, :, :], 0.0).then_inc(s_zero, 1)

            @block.scalar
            def _(act):
                xs = x_sample[0].rearrange("(i p) d -> p i d", p=P)
                act.dma_start(xtok[:, 0, :], x_prompt[0]).then_inc(s_x[0], 16)
                act.dma_start(xtok[:, 1:5, :], xs[:, 0:4, :]).then_inc(s_x[1], 16)
                act.dma_start(xtok[:, 5:9, :], xs[:, 4:8, :]).then_inc(s_x[2], 16)
                act.dma_start(w2s[:, :], w2.rearrange("a n r d -> (a n r) d")).then_inc(s_w2, 16)
                act.dma_start(a2s[:, :], a2.rearrange("a n r d -> (a n r) d")).then_inc(s_w2, 16)
                act.wait_ge(s_vc, 1)
                act.activation(small[:, 18:34], vec[:, 0:16], ACT.Tanh, scale=0.5).then_inc(s_tm, 1)
                for i in range(9):
                    if i in (0, 1, 5):
                        act.wait_ge(s_x[(0, 1, 5).index(i)], 16)
                    if i:
                        act.wait_ge(s_ss, i)
                    act.activation(junk, xtok[:, i, :], ACT.Square, accum_out=ss[:, i:i + 1]).then_inc(s_ss, 1)
                act.wait_ge(s_ms, 1)
                act.activation(ss, ss, ACT.Sqrt).then_inc(s_sd, 1)
                act.wait_ge(s_sc, 1)
                for n in range(len(HT_BANKS)):
                    k, at, w, _, s = HT_BANKS[n]
                    act.wait_ge(s_xt, n + 1)
                    act.activation(hi_of_h[:, k, at:at + w], ps[:, n % 8, 0:w], ACT.Identity,
                                   bias=shf[:, k, s:s + 1], scale=scl[:, k, s:s + 1]).then_inc(s_ha, 1)

                def round_weights(p):
                    n = LOADS.index(("z", p))
                    act.wait_ge(s_wl[n % RING], 16 * (n // RING + 1))
                    if p >= 2:
                        act.wait_ge(s_z, 2 * (p - 1))
                    act.activation(w_round[:, p % 2, :], ring[:, n % RING, :], ACT.Copy).then_inc(s_wh, 1)

                def kk_norm(a):
                    act.wait_ge(s_mix, 5 + a)
                    act.wait_ge(s_sa, 16)
                    if a:
                        act.wait_ge(s_ks, NB * a)
                    act.activation(zc[:, 17, :], kT[:, a, :], ACT.Square, scale=col("k_k", a)).then_inc(s_kq, 1)
                    r = slice(32 * a, 32 * a + 32)
                    for n in range(NB):
                        act.wait_ge(s_ks, NB * a + n + 1)
                        act.activation(kn[r, n * NC:(n + 1) * NC], ps[r, 6 + n % 2, 0:NC], ACT.Sqrt,
                                       bias=epst[r, 2:3]).then_inc(s_kd, 1)

                def layer_norm():
                    for n in range(NB):
                        cut = slice(n * NC, (n + 1) * NC)
                        act.wait_ge(s_lx, n + 1)
                        act.activation(T[:, 2:4, cut], T[:, 0:2, cut], ACT.Square).then_inc(s_lq, 1)
                        act.wait_ge(s_lv, n + 1)
                        act.activation(raw[:, 0, cut], ps[:, 7, 0:NC], ACT.Sqrt, bias=epst[:, 1:2]).then_inc(s_ls, 1)
                    for g in range(2):
                        act.wait_ge(s_lr, g + 1)
                        act.activation(T[:, 2 + g, :], T[:, g, :], ACT.Tanh, scale=0.5).then_inc(s_lt, 1)

                round_weights(0)
                for j, kind in enumerate(TILES):
                    h, z = j % 2, zbanks(j)
                    i = j - TILES.index(kind)
                    if h == 0 and j // 2 + 1 < len(PIECES):
                        round_weights(j // 2 + 1)
                    if kind in ("u2", "gb", "ga", "gc", "xa", "mix"):
                        act.wait_ge(s_z, j + 1)
                    if kind == "u2":
                        act.activation(as3(T[:, h, :]), z, ACT.Tanh, scale=0.5).then_inc(s_th, 1)
                    elif kind == "gb":
                        if h == 0:
                            act.wait_ge(s_sg, 32)
                        act.activation(as3(T[:, 6 + h, :]), z, ACT.Tanh, scale=0.5).then_inc(s_th, 1)
                    elif kind == "xa":
                        act.activation(as3(xa[:, h, :]), z, ACT.Copy).then_inc(s_xa, 1)
                    elif kind == "ga":
                        act.activation(as3(xa[:, 2 + h, :]), z, ACT.Tanh, scale=0.5).then_inc(s_th, 1)
                    elif kind == "mix":
                        if i < 2:
                            act.wait_ge(s_ya, i + 1)
                        if i == 4:
                            act.wait_ge(s_yb, 2)
                        if i == 6:
                            act.wait_ge(s_sb, 16)
                        if i >= 2:
                            act.wait_ge(s_sum, i - 1)
                        act.activation(as3(dest(i)), z, ACT.Copy, scale=omu[:, i:i + 1])
                        act.activation(as3(raw[:, i % 2, :]), z, ACT.Copy).then_inc(s_raw, 1)
                    elif kind == "gc":
                        act.activation(as3(T[:, 4 + i, :]), z, ACT.Tanh, scale=0.5).then_inc(s_th, 1)
                    if j == MIX0 - 1:
                        layer_norm()
                    if MIX0 + 5 <= j <= MIX0 + 8:
                        kk_norm(j - MIX0 - 5)
                    if j == MIX0 + 13:
                        act.wait_ge(s_mix, 13)
                        act.activation(lwT, lwT, ACT.Tanh).then_inc(s_lwt, 1)

            @block.tensor
            def _(pe):
                pe.wait_ge(s_const, 1)
                pe.wait_ge(s_vec, 16 * (len(VEC_ROWS) + 1))
                pe.transpose(ps[:, 6, 0:N_VEC], va[0:N_VEC, :], eye[0:N_VEC, 0:N_VEC]).then_inc(s_vt, 1)
                pe.transpose(ps[:, 7, 0:N_CB], vb[0:N_CB, :], eye[0:N_CB, 0:N_CB]).then_inc(s_vt, 1)
                pe.wait_ge(s_smod, 1)
                mods = smod[:, :].rearrange("p (s k) -> p k s", k=KT)
                for k in range(KT):
                    pe.wait_ge(s_wl[k % RING], 16 * (k // RING + 1))
                    for b in range(4):
                        last = pe.matmul(ps[0:2, b, :], mods[:, k, :], ring[:, k % RING, 512 * b:512 * b + 512],
                                         start=(k == 0), stop=(k == KT - 1))
                    last.then_inc(s_wu, 1)
                pe.wait_ge(s_row, 1)
                for m in range(16):
                    last = pe.transpose(ps[:, 4, 2 * m:2 * m + 2], row[:, P * m:P * m + P], eye[0:2, 0:2])
                last.then_inc(s_at, 1)
                pe.wait_ge(s_xn, 9)
                for n, (k, at, w, i0, _) in enumerate(HT_BANKS):
                    if n == 4:
                        pe.wait_ge(s_sc, 1)
                    if n >= 8:
                        pe.wait_ge(s_hf, n - 7)
                    for i in range(w // P):
                        last = pe.transpose(ps[:, n % 8, P * i:P * i + P], xtok[:, i0 + i, P * k:P * k + P], eye[:, :])
                    last.then_inc(s_xt, 1)

                def layer_norm():
                    pe.wait_ge(s_cv, 2)
                    for n in range(NB):
                        cut = slice(n * NC, (n + 1) * NC)
                        if n:
                            pe.wait_ge(s_lx, n)
                        pe.matmul(ps[:, 6, 0:NC], ones[:, :], T[:, 4, cut], start=True, stop=False)
                        pe.matmul(ps[:, 6, 0:NC], ones[:, :], T[:, 5, cut], start=False, stop=True).then_inc(s_lm, 1)
                        pe.wait_ge(s_lq, n + 1)
                        if n:
                            pe.wait_ge(s_ls, n)
                        pe.matmul(ps[:, 7, 0:NC], ones[:, :], T[:, 2, cut], start=True, stop=False)
                        pe.matmul(ps[:, 7, 0:NC], ones[:, :], T[:, 3, cut], start=False, stop=True).then_inc(s_lv, 1)

                def kk_norm(a):
                    pe.wait_ge(s_kq, a + 1)
                    for n in range(NB):
                        if n == 2:
                            pe.wait_ge(s_kd, NB * a + 1)
                        elif a:
                            pe.wait_ge(s_kd, NB * a)
                        pe.matmul(ps[32 * a:32 * a + 32, 6 + n % 2, 0:NC], heads[:, 48:80], zc[:, 17, n * NC:(n + 1) * NC],
                                  start=True, stop=True).then_inc(s_ks, 1)

                pe.wait_ge(s_const, 2)
                pe.wait_ge(s_w2, 32)
                for by in range(2):
                    pe.wait_ge(s_hs[by], len(HT_BANKS) // 2)
                for j in range(len(TILES)):
                    p = j // 2
                    cut = slice(P * (j % 2), P * (j % 2) + P)
                    w_hi = w_round[:, p % 2, :].rearrange("p (k n) -> p k n", k=KT)
                    w_lo = w_rest[:, LOADS.index(("z", p)) % RING, :].rearrange("p (k n) -> p k n", k=KT)
                    if j % 2 == 0:
                        pe.wait_ge(s_wh, p + 1)
                        pe.wait_ge(s_wo1, p + 1)
                    if j >= 2:
                        pe.wait_ge(*read_by(j - 2))
                    for b in range(NB):
                        o, cols_b = ps[:, NB * (j % 2) + b, 0:NC], slice(NC * b, NC * (b + 1))
                        for k in range(KT):
                            pe.matmul(o, w_hi[:, k, cut], hi_of_h[:, k, cols_b], start=(k == 0), stop=False)
                            pe.matmul(o, w_hi[:, k, cut], lo_of_h[k][:, cols_b], start=False, stop=False)
                            last = pe.matmul(o, w_lo[:, k, cut], hi_of_h[:, k, cols_b], start=False, stop=(k == KT - 1))
                    last.then_inc(s_z, 1)
                    if j == 2 * GATE_AFTER - 1:
                        for k in range(KT):
                            n = LOADS.index(("gate", k // 2))
                            if k % 2 == 0:
                                pe.wait_ge(s_wl[n % RING], 16 * (n // RING + 1))
                            for b in range(2):
                                at = D_MODEL * (k % 2) + 512 * b
                                last = pe.matmul(ps[0:2, 6 + b, :], mods[:, k, :], ring[:, n % RING, at:at + 512],
                                                 start=(k == 0), stop=(k == KT - 1))
                            if k % 2:
                                last.then_inc(s_gu, 1)
                    if j == MIX0:
                        layer_norm()
                    if MIX0 + 5 <= j <= MIX0 + 8:
                        kk_norm(j - MIX0 - 5)
                pe.wait_ge(s_kr, 1)
                for a in range(PAIRS):
                    r = slice(32 * a, 32 * a + 32)
                    for n in range(NB):
                        at = NB * a + n
                        if at >= 2:
                            pe.wait_ge(s_kn, at - 1)
                        pe.matmul(ps[:, 6 + at % 2, 0:NC], back[r, :], kn[r, n * NC:(n + 1) * NC],
                                  start=True, stop=True).then_inc(s_kp, 1)

            @block.vector
            def _(dve):
                n_dve = [0]

                def link(ins):
                    n_dve[0] += 1
                    ins.then_inc(s_dve, 1)
                    dve.wait_ge(s_dve, n_dve[0])

                dve.wait_ge(s_vt, 1)
                dve.tensor_copy(vec[:, :], ps[:, 6, 0:N_VEC]).then_inc(s_vc, 1)
                dve.wait_ge(s_vt, 2)
                dve.tensor_scalar(cb[:, :], ps[:, 7, 0:N_CB], 0.5, None, ALU.mult)
                dve.wait_ge(s_vc, 1)
                dve.tensor_scalar(cah[:, :], cols("conv_a"), 0.5, None, ALU.mult)
                dve.tensor_scalar(hmu[:, :], cols("mu"), 0.5, None, ALU.mult)
                dve.tensor_scalar(omu[:, :], cols("mu"), -1.0, 1.0, ALU.mult, ALU.add)
                dve.wait_ge(s_tm, 1)
                link(dve.scalar_tensor_tensor(out=smod[:, :], in0=small[:, 18:34], scalar=1.0, in1=vec[:, 0:16],
                                              op0=ALU.add, op1=ALU.mult))
                dve.tensor_scalar(smod[:, :], smod[:, :], 0.5, None, ALU.mult).then_inc(s_smod, 1)
                dve.wait_ge(s_ss, 9)
                dve.tensor_scalar(ss, ss, 1.0 / D_MODEL, RMS_EPS, ALU.mult, ALU.add).then_inc(s_ms, 1)
                dve.wait_ge(s_sd, 1)
                link(dve.reciprocal(rs, ss))
                for i in range(9):
                    dve.tensor_scalar(xtok[:, i, :], xtok[:, i, :], rs[:, i:i + 1], None, ALU.mult).then_inc(s_xn, 1)
                dve.wait_ge(s_wu, KT)
                dve.wait_ge(s_adab, 96)
                dve.tensor_tensor(row, ps[0:2, 0:4, :].rearrange("p b n -> p (b n)"), adab, ALU.add).then_inc(s_row, 1)
                dve.wait_ge(s_at, 1)
                cols4 = ps[:, 4, 0:32].rearrange("p (m s) -> p m s", s=2)
                dve.tensor_copy(shf[:, :, :], cols4[:, 0:KT, :])
                dve.scalar_tensor_tensor(out=scl[:, :, :], in0=cols4[:, KT:, :], scalar=1.0,
                                         in1=cols("g_pre").unsqueeze(2).to_broadcast([P, KT, 2]),
                                         op0=ALU.add, op1=ALU.mult).then_inc(s_sc, 1)
                dve.wait_ge(s_sc, 1)
                for n in range(len(HT_BANKS)):
                    k, at, w, _, s = HT_BANKS[n]
                    dve.wait_ge(s_ha, n + 1)
                    dve.tensor_scalar(lo_full[k][:, at:at + w], ps[:, n % 8, 0:w], scl[:, k, s:s + 1], shf[:, k, s:s + 1],
                                      ALU.mult, ALU.add).then_inc(s_hf, 1)
                    if n % 2:
                        dve.wait_ge(s_hf, n + 1)
                        dve.tensor_tensor(lo_of_h[k][:, at:at + w], lo_full[k][:, at:at + w], hi_of_h[:, k, at:at + w].bitcast(F32),
                                          ALU.subtract).then_inc(s_hs[1], 1)

                def conv_taps(g, first, last):
                    x, o = T[:, 2 + g, :], T[:, 4 + g, :]
                    order = [CONV_B // 2] + [t for t in range(CONV_B) if t != CONV_B // 2]
                    for t in order[first:last]:
                        w = cb[:, 2 * t + g:2 * t + g + 1]
                        off = t - CONV_B // 2
                        if off == 0:
                            link(dve.tensor_scalar(o, x, w, col("conv_b_bias", g), ALU.mult, ALU.add))
                            continue
                        for at, n, step in ((TP, SEQ, 1), (TS, ROWS, GRID_W)):
                            lo, hi = max(0, -off), min(n, n - off)
                            if hi <= lo:
                                continue
                            a, b = at + lo * step, at + hi * step
                            done = dve.scalar_tensor_tensor(out=o[:, a:b], in0=x[:, a + off * step:b + off * step], scalar=w,
                                                            in1=o[:, a:b], op0=ALU.mult, op1=ALU.add)
                        if t == order[-1]:
                            done.then_inc(s_cv, 1)
                        else:
                            link(done)

                def conv_a_half(g):
                    x, o = xa[:, g, :], ya[:, g, :]
                    link(dve.tensor_scalar(o, x, cah[:, 2 + g:3 + g], None, ALU.mult))
                    xg, og = (a[:, TS:TS + DEC_SEQ].rearrange("p (r w) -> p r w", w=GRID_W) for a in (x, o))
                    for t, off in ((0, -1), (2, 1)):
                        w = cah[:, 2 * t + g:2 * t + g + 1]
                        dve.scalar_tensor_tensor(out=o[:, TP:TP + SEQ], in0=x[:, TP + off:TP + SEQ + off], scalar=w,
                                                 in1=o[:, TP:TP + SEQ], op0=ALU.mult, op1=ALU.add)
                        lo, hi = max(0, -off), GRID_W - max(0, off)
                        link(dve.scalar_tensor_tensor(out=og[:, :, lo:hi], in0=xg[:, :, lo + off:hi + off], scalar=w,
                                                      in1=og[:, :, lo:hi], op0=ALU.mult, op1=ALU.add))

                def layer_norm():
                    for n in range(NB):
                        cut = slice(n * NC, (n + 1) * NC)
                        dve.wait_ge(s_lm, n + 1)
                        dve.tensor_tensor(T[:, 0:2, cut], T[:, 4:6, cut],
                                          ps[:, 6, 0:NC].unsqueeze(1).to_broadcast([P, 2, NC]), ALU.subtract).then_inc(s_lx, 1)
                        dve.wait_ge(s_ls, n + 1)
                        link(dve.reciprocal(raw[:, 0, cut], raw[:, 0, cut]))
                        link(dve.tensor_tensor(T[:, 0:2, cut], T[:, 0:2, cut],
                                               raw[:, 0, cut].unsqueeze(1).to_broadcast([P, 2, NC]), ALU.mult))
                    for g in range(2):
                        dve.tensor_scalar(T[:, g, :], T[:, g, :], col("ln_b_g", g), col("ln_b_b", g),
                                          ALU.mult, ALU.add).then_inc(s_lr, 1)
                    for g in range(2):
                        dve.wait_ge(s_lt, g + 1)
                        link(dve.scalar_tensor_tensor(out=T[:, 2 + g, :], in0=T[:, 2 + g, :], scalar=1.0, in1=T[:, g, :],
                                                      op0=ALU.add, op1=ALU.mult))
                        dve.scalar_tensor_tensor(out=T[:, 6 + g, :], in0=T[:, 2 + g, :], scalar=0.25, in1=T[:, 6 + g, :],
                                                 op0=ALU.mult, op1=ALU.mult).then_inc(s_yb, 1)

                for j, kind in enumerate(TILES):
                    h, z = j % 2, zbanks(j)
                    i = j - TILES.index(kind)
                    if j == 2 * GATE_AFTER + 1:
                        dve.wait_ge(s_gu, KT // 2)
                        link(dve.tensor_tensor(grow, ps[0:2, 6:8, :].rearrange("p b n -> p (b n)"), grow, ALU.add))
                        dve.tensor_tensor(grow, grow, gpost, ALU.mult).then_inc(s_gr, 1)
                    if kind in ("u1", "gb", "cg", "bg", "ga", "gc"):
                        dve.wait_ge(s_z, j + 1)
                    if kind == "u1":
                        dve.wait_ge(s_th, 5 + h)
                        dve.scalar_tensor_tensor(out=as3(T[:, 2 + h, :]), in0=as3(T[:, h, :]), scalar=1.0, in1=z,
                                                 op0=ALU.add, op1=ALU.mult).then_inc(s_glu, 1)
                        dve.wait_ge(s_glu, h + 1)
                        dve.wait_ge(s_sg, 32)
                        conv_taps(h, 0, 12)
                    elif kind == "gb":
                        dve.wait_ge(s_th, 7 + h)
                        dve.scalar_tensor_tensor(out=as3(T[:, 6 + h, :]), in0=as3(T[:, 6 + h, :]), scalar=1.0, in1=z,
                                                 op0=ALU.add, op1=ALU.mult).then_inc(s_gb, 1)
                        conv_taps(0, 12 + 10 * h, 22 + 9 * h)
                    elif kind == "cg":
                        dve.wait_ge(s_xa, h + 1)
                        dve.tensor_tensor(as3(xa[:, h, :]), as3(xa[:, h, :]), z, ALU.mult).then_inc(s_cx, 1)
                        dve.wait_ge(s_cx, h + 1)
                        dve.wait_ge(s_gst, 16)
                        conv_a_half(h)
                        conv_taps(1, 12 + 6 * h, 18 + 6 * h)
                    elif kind == "bg":
                        dve.tensor_tensor(as3(ya[:, h, :]), as3(ya[:, h, :]), z, ALU.mult).then_inc(s_bg, 1)
                        if h:
                            conv_taps(1, 24, 31)
                    elif kind == "ga":
                        dve.wait_ge(s_th, 9 + h)
                        link(dve.scalar_tensor_tensor(out=as3(xa[:, 2 + h, :]), in0=as3(xa[:, 2 + h, :]), scalar=1.0, in1=z,
                                                      op0=ALU.add, op1=ALU.mult))
                        dve.wait_ge(s_bg, h + 1)
                        dve.tensor_tensor(ya[:, h, :], ya[:, h, :], xa[:, 2 + h, :], ALU.mult).then_inc(s_ya, 1)
                        if h:
                            layer_norm()
                    elif kind == "mix":
                        dve.wait_ge(s_sum, i + 1)
                        o = dest(i)[:, 1:W - 1]
                        dve.scalar_tensor_tensor(out=o, in0=nsum[:, 1:W - 1], scalar=hmu[:, i:i + 1], in1=o,
                                                 op0=ALU.mult, op1=ALU.add).then_inc(s_mix, 1)
                        if i == 9:
                            dve.wait_ge(s_kd, NB * PAIRS)
                            dve.reciprocal(kn, kn).then_inc(s_kr, 1)
                    elif kind == "gc":
                        dve.wait_ge(s_th, i + 1)
                        dve.scalar_tensor_tensor(out=as3(T[:, 4 + i, :]), in0=as3(T[:, 4 + i, :]), scalar=1.0, in1=z,
                                                 op0=ALU.add, op1=ALU.mult).then_inc(s_gc, 1)
                for at in range(NB * PAIRS):
                    a, cut = at // NB, slice(at % NB * NC, at % NB * NC + NC)
                    dve.wait_ge(s_kp, at + 1)
                    dve.scalar_tensor_tensor(out=kkT[:, a, cut], in0=kT[:, a, cut], scalar=col("k_k", a),
                                             in1=ps[:, 6 + at % 2, 0:NC], op0=ALU.mult, op1=ALU.mult).then_inc(s_kn, 1)

        assert sems1 == list(range(sems1[0], sems1[0] + len(sems1)))
        nc.all_engine_barrier(sems_to_clear=range(sems1[0], sems1[-1] + 1))
        part1.close()

        take = carve()
        LEV = range(1, LEVELS)
        ls = take(2, P)
        xw = take(PAIRS, 2, C)
        av = take(PAIRS, 2, C)
        LA = take(PAIRS, 2, C)
        LB = take(PAIRS, 2, C)
        eA, eB, eN = take(PAIRS, 2, C), LB, LA
        kd = take(2, PAIRS, C)
        keep = take(512)
        dend = take(2, 2, PAIRS)
        GL = [take(PAIRS, 3, C) for _ in DIRS]
        GR = [[take(PAIRS, 4, C) for _ in DIRS] for _ in range(2)]
        AB = [[take(PAIRS, C) for _ in DIRS] for _ in range(2)]
        Ub = [take(PAIRS, P) for _ in DIRS]
        Um = [take(PAIRS, P) for _ in DIRS]
        X = [take(PAIRS, P) for _ in DIRS]
        Y = [take(PAIRS, P) for _ in DIRS]
        PX = [take(PAIRS, P) for _ in DIRS]
        KB = [take(PAIRS, 2, C) for _ in DIRS]
        SU = [take(2, PAIRS, 2, C) for _ in DIRS]
        RH = [take(PAIRS, C) for _ in DIRS]
        VD = [xw, av]
        stin = [v.rearrange("p a b c -> p (a b c)") for v in KB]
        sout = PX

        s_set = sem("scan_buffers_set")
        s_so = sem("final_state_transposed")
        s_sc2 = sem("final_state_copied")
        s_sz = sem("state_staging_zero")
        s_sl = sem("state_landed")
        s_st = sem("state_transposed")
        s_ns = sem("new_state_stored")

        with nc.Block() as block:
            @block.vector
            def _(dve):
                for d in DIRS:
                    dve.memset(Ub[d], 0.0)
                    dve.memset(SU[d], 0.0)
                dve.memset(ls, 0.0)
                dve.memset(keep, 1.0).then_inc(s_set, 1)
                dve.wait_ge(s_set, 1)
                dve.memset(keep.rearrange("p (n c) -> p n c", c=C)[:, :, 0:1], 0.0)

        lo, hi = slice(0, 64), slice(64, 128)

        def pairs(bank, w):
            return ps[:, bank, 0:PAIRS * w].rearrange("p (a b) -> p a b", a=PAIRS)

        def chunk(tiles, col):
            return tiles[:, :, bass.ds(col, C)]

        def steps(solve, prepare, start=0):
            N = len(solve)

            def earlier(e, s, value):
                if value > 0:
                    e.wait_ge(s, value)

            with nc.Block() as block:
                @block.scalar
                def _(act):
                    for t in range(N):
                        so, pr = solve[t], prepare[t]
                        nxt = (start + t + 1) % 2

                        def stage_lora():
                            earlier(act, l_lora, 2 * t)
                            for n, src in enumerate((lwT, laT)):
                                for d in DIRS:
                                    r = slice(64 * d, 64 * d + 64)
                                    act.activation(ls[r, n, r], src[r, bass.ds(pr[d], C)], ACT.Copy).then_inc(l_stage, 1)

                        def v_by_token(d):
                            earlier(act, l_S[d], t)
                            act.wait_ge(l_vt[d], t + 1)
                            vt = ps[:, 6 + d, :].rearrange("p (a h c) -> p a h c", a=PAIRS, h=2)
                            for g, r in ((0, hi), (1, lo)):
                                act.activation(SU[d][r, :, :, g, :],
                                               vt[r, :, g, :].unsqueeze(1).to_broadcast([64, 2, PAIRS, C]),
                                               ACT.Copy).then_inc(l_v[d], 1)

                        def tanh():
                            for n, x in enumerate((xw, av)):
                                act.wait_ge(l_x, 2 * t + n + 1)
                                act.activation(x, x, ACT.Tanh, scale=0.5).then_inc(l_tanh, 1)

                        def sigmoid():
                            act.wait_ge(l_tanh, 2 * t + 2)
                            act.activation(av, av, ACT.Copy, bias=0.5, scale=0.5).then_inc(l_a, 1)

                        def copy_y(d, l):
                            if l < LEVELS - 1:
                                act.wait_ge(l_X[d], 4 * t + l)
                            else:
                                act.wait_ge(l_Q[d], 5 * t + l)
                            act.activation(Y[d], pairs(2 * d + 1, P), ACT.Copy).then_inc(l_Y[d], 1)

                        def keys_by_token(d):
                            for g in range(2):
                                act.wait_ge(l_kt[d], 2 * t + g + 1)
                                act.activation(KB[d][:, :, g, :], pairs((6, 4)[d] + g, P)[:, :, 64 * g:64 * g + 64],
                                               ACT.Copy).then_inc(l_kb[d], 1)

                        def exps():
                            act.wait_ge(l_log, 2 * t + 2)
                            act.activation(eA, LA, ACT.Exp).then_inc(l_exp, 1)
                            act.activation(eB, LB, ACT.Exp).then_inc(l_exp, 1)
                            act.wait_ge(l_exp, 3 * t + 1)
                            act.activation(eN, LA, ACT.Exp, scale=-1.0).then_inc(l_exp, 1)
                            earlier(act, l_st[1], 2 * t)
                            for d in DIRS:
                                end = C - 1 if d == 0 else 0
                                act.activation(dend[:, nxt, d, :], eA[:, :, d, end], ACT.Copy).then_inc(l_end, 1)

                        def negate_rhs(d):
                            act.wait_ge(l_rhs[d], t + 1)
                            act.activation(RH[d], pairs(6 + d, C), ACT.Copy, scale=-1.0).then_inc(l_rh[d], 1)

                        def double_v(d):
                            act.wait_ge((l_kf, l_b)[d], 2 * t + 2)
                            if d == 1:
                                act.wait_ge(l_kf, 2 * t + 2)
                            act.activation(VD[d], chunk(vT, pr[d]).unsqueeze(2).to_broadcast([P, PAIRS, 2, C]),
                                           ACT.Copy).then_inc(l_vd[d], 1)

                        def copy_u(d):
                            act.wait_ge(l_U[d], t + 1)
                            u = pairs(2 * d, C)
                            for g, r in ((0, lo), (1, hi)):
                                act.activation(SU[d][r, 1, :, g, :], u[r], ACT.Copy).then_inc(l_uc[d], 1)

                        if pr:
                            stage_lora()
                        if so:
                            v_by_token(0)
                        if pr:
                            tanh()
                        if so:
                            v_by_token(1)
                            copy_y(0, 1)
                        if pr:
                            sigmoid()
                        if so:
                            copy_y(1, 1)
                            keys_by_token(0)
                            copy_y(0, 2)
                        if pr:
                            exps()
                        if so:
                            copy_y(1, 2)
                            keys_by_token(1)
                            copy_y(0, 3)
                            negate_rhs(0)
                            negate_rhs(1)
                            copy_y(1, 3)
                        if pr:
                            double_v(0)
                            double_v(1)
                        if so:
                            for l in (4, 5):
                                for d in DIRS:
                                    copy_y(d, l)
                            copy_u(0)
                            copy_u(1)

                @block.tensor
                def _(pe):
                    for t in range(N):
                        so, pr = solve[t], prepare[t]
                        now, nxt = (start + t) % 2, (start + t + 1) % 2

                        def level_product(d, l):
                            if l == 1:
                                earlier(pe, l_um0[d], 2 * t)
                                earlier(pe, l_X0[d], t)
                                earlier(pe, l_uc[d], 2 * t)
                            else:
                                pe.wait_ge(l_um[d], 4 * t + l - 1)
                                pe.wait_ge(l_X[d], 4 * t + l - 1)
                            for a in range(PAIRS):
                                last = pe.matmul(pairs(2 * d, P)[:, a, :], Um[d][:, a, :], X[d][:, a, :], start=True, stop=True)
                            last.then_inc(l_P[d], 1)

                        def level_update(d, l):
                            pe.wait_ge(l_pc[d], 5 * t + l)
                            if l == 1:
                                earlier(pe, l_st[d], 2 * t)
                            else:
                                pe.wait_ge(l_Y[d], 5 * t + l - 1)
                            for a in range(PAIRS):
                                last = pe.matmul(pairs(2 * d + 1, P)[:, a, :], PX[d][:, a, :], Y[d][:, a, :], start=True, stop=True)
                            last.then_inc(l_Q[d], 1)

                        def transpose_v():
                            for d in DIRS:
                                earlier(pe, l_vd[d], t)
                                earlier(pe, l_g[1], t)
                                for a in range(PAIRS):
                                    last = pe.transpose(pairs(6 + d, P)[:, a, :], VD[d][:, a].rearrange("p b c -> p (b c)"), eye[:, :])
                                last.then_inc(l_vt[d], 1)

                        def lora():
                            earlier(pe, l_g[0], t)
                            for n, w in enumerate((w2s, a2s)):
                                pe.wait_ge(l_stage, 4 * t + 2 * n + 2)
                                for a in range(PAIRS):
                                    last = pe.matmul(pairs(4 + n, P)[:, a, :], w[:, P * a:P * a + P], ls[:, n, :],
                                                     start=True, stop=True)
                                last.then_inc(l_lora, 1)

                        def transpose_keys(d):
                            if d == 0:
                                pe.wait_ge(l_v[0], 2 * t + 2)
                                pe.wait_ge(l_v[1], 2 * t + 2)
                            elif pr:
                                pe.wait_ge(l_x, 2 * t + 2)
                            for g in range(2):
                                for a in range(PAIRS):
                                    last = pe.transpose(pairs((6, 4)[d] + g, P)[:, a, :],
                                                        GL[d][:, a, g:g + 2, :].rearrange("p b c -> p (b c)"), eye[:, :])
                                last.then_inc(l_kt[d], 1)

                        def rhs():
                            pe.wait_ge(l_kb[0], 2 * t + 2)
                            for d in DIRS:
                                earlier(pe, l_st[d], 2 * t)
                                for a in range(PAIRS):
                                    for g in range(2):
                                        last = pe.matmul(pairs(6 + d, C)[64 * g:64 * g + 64, a, :], GR[now][d][:, a, 3 * g, :],
                                                         SU[d][:, 0, a, g, :], start=True, stop=True)
                                last.then_inc(l_rhs[d], 1)

                        def gram(d):
                            pe.wait_ge(l_ops[d], t + 1)
                            if so and d == 0:
                                pe.wait_ge(l_kb[1], 2 * t + 2)
                            if so and d == 1:
                                pe.wait_ge(l_rh[0], t + 1)
                                pe.wait_ge(l_rh[1], t + 1)
                            for g in range(2):
                                r = slice(64 * g, 64 * g + 64)
                                for a in range(PAIRS):
                                    last = pe.matmul(pairs(4 + 2 * d + g, P)[:, a, :], GL[d][r, a, g:g + 2, :],
                                                     GR[nxt][d][r, a, 2 * g:2 * g + 2, :], start=True, stop=True)
                                last.then_inc(l_gram[d], 1)

                        if so:
                            level_product(0, 1)
                            transpose_v()
                        if pr:
                            lora()
                        if so:
                            level_update(0, 1)
                            level_product(1, 1)
                            level_product(0, 2)
                            level_update(1, 1)
                            transpose_keys(0)
                            level_update(0, 2)
                            level_product(1, 2)
                            transpose_keys(1)
                            level_product(0, 3)
                            level_update(1, 2)
                            rhs()
                            level_update(0, 3)
                            level_product(1, 3)
                            level_product(0, 4)
                            level_update(1, 3)
                        if pr:
                            gram(0)
                        if so:
                            level_update(0, 4)
                            level_product(1, 4)
                            level_product(0, 5)
                            level_update(1, 4)
                        if pr:
                            gram(1)
                        if so:
                            level_update(0, 5)
                            level_product(1, 5)
                            level_update(1, 5)
                        if so:
                            for d in DIRS:
                                pe.wait_ge(l_Y[d], 5 * t + 5)
                                pe.wait_ge(l_rh[d], t + 1)
                                for a in range(PAIRS):
                                    last = pe.matmul(pairs(2 * d, C)[:, a, :], Y[d][:, a, :], RH[d][:, a, :],
                                                     start=True, stop=True)
                                last.then_inc(l_U[d], 1)
                            pe.wait_ge(l_kb[1], 2 * t + 2)
                            for d in DIRS:
                                pe.wait_ge(l_uc[d], 2 * t + 2)
                                for a in range(PAIRS):
                                    for g in range(2):
                                        r = slice(64 * g, 64 * g + 64)
                                        o = pairs(2 * d + 1, C)[r, a, :]
                                        pe.matmul(o, SU[d][:, 0, a, g, :], GR[now][d][:, a, 1 + g, :], start=True, stop=False)
                                        pe.matmul(o, SU[d][r, 1, a, g, :], AB[now][d][r, a, :], start=False, stop=True)
                                for a in range(PAIRS):
                                    for g in range(2):
                                        last = pe.matmul(ps[64 * g:64 * g + 64, 2 * d + 1, 256 + C * a:256 + C * a + C],
                                                         KB[d][:, a, g, :], SU[d][:, 1, a, g, :], start=True, stop=True)
                                last.then_inc(l_S[d], 1)

                @block.gpsimd
                def _(pool):
                    n_pool = [0]

                    def link(ins):
                        n_pool[0] += 1
                        ins.then_inc(l_pool, 1)
                        pool.wait_ge(l_pool, n_pool[0])

                    def mask_level(d, l):
                        return pool.tensor_tensor(Um[d], Ub[d], lvl[:, l, :].unsqueeze(1).to_broadcast([P, PAIRS, P]), ALU.mult)

                    for t in range(N):
                        so, pr = solve[t], prepare[t]

                        def next_level(d, l):
                            pool.wait_ge(l_P[d], 5 * t + l - 1)
                            mask_level(d, l).then_inc(l_um[d], 1)

                        def b_keys(d):
                            if so:
                                pool.wait_ge(l_kt[d], 2 * t + 2)
                            pool.wait_ge(l_a, t + 1)
                            pool.tensor_tensor(GL[d][:, :, 0, :], chunk(kkT, pr[d]), av[:, :, d], ALU.mult).then_inc(l_b, 1)

                        def bonus_keys(d):
                            pool.wait_ge(l_kd, 2 * t + d + 1)
                            link(pool.tensor_tensor(kd[:, d], kd[:, d], chunk(rT, pr[d]), ALU.mult))
                            pool.tensor_tensor(chunk(q, pr[d]), chunk(q, pr[d]), kd[:, d], ALU.add).then_inc(l_q, 1)
                            pool.wait_ge(l_q, 2 * t + d + 1)

                        if so:
                            for l in (2, 3):
                                for d in DIRS:
                                    next_level(d, l)
                        if pr:
                            b_keys(0)
                            b_keys(1)
                        if so:
                            for l in (4, 5):
                                for d in DIRS:
                                    next_level(d, l)
                        if pr:
                            bonus_keys(0)
                            bonus_keys(1)
                            for d in DIRS:
                                if so:
                                    pool.wait_ge(l_P[d], 5 * t + 5)
                                pool.wait_ge(l_u[d], 2 * t + 2)
                                mask_level(d, 0).then_inc(l_um0[d], 1)
                            for d in DIRS:
                                pool.wait_ge(l_Y0[d], t + 1)
                                mask_level(d, 1).then_inc(l_um0[d], 1)

                @block.vector
                def _(dve):
                    n_dve = [0]

                    def link(ins):
                        n_dve[0] += 1
                        ins.then_inc(l_dve, 1)
                        dve.wait_ge(l_dve, n_dve[0])

                    def wide(name):
                        return cols(name).rearrange("p (d a) -> p a d", d=2).unsqueeze(3).to_broadcast([P, PAIRS, 2, C])

                    def mask(d, r, slots):
                        return tri[r, d, slots, :].unsqueeze(1).to_broadcast([64, PAIRS, slots.stop - slots.start, C])

                    eyes = eye[:, :].unsqueeze(1).to_broadcast([P, PAIRS, P])
                    for t in range(N):
                        so, pr = solve[t], prepare[t]
                        now, nxt = (start + t) % 2, (start + t + 1) % 2

                        def transpose_x(d, l):
                            dve.wait_ge(l_Q[d], 5 * t + l)
                            dve.transpose(X[d], pairs(2 * d + 1, P)).then_inc(l_X[d], 1)

                        def add_bias():
                            for n, (x, bias) in enumerate(((xw, "w0"), (av, "a0"))):
                                dve.wait_ge(l_lora, 2 * t + n + 1)
                                if so:
                                    dve.wait_ge(l_vt[n], t + 1)
                                dve.tensor_tensor(x, ps[:, 4 + n, :].rearrange("p (a d c) -> p a d c", a=PAIRS, d=2),
                                                  wide(bias), ALU.add).then_inc(l_x, 1)

                        def log_decays():
                            dve.wait_ge(l_tanh, 2 * t + 1)
                            link(dve.tensor_scalar(xw, xw, -E_HALF / 2, -E_HALF / 2, ALU.mult, ALU.add))
                            link(dve.tensor_tensor_scan(LA.rearrange("p a d c -> p (a d c)"), keep,
                                                        xw.rearrange("p a d c -> p (a d c)"), 0.0, ALU.mult, ALU.add))

                        def split_decays():
                            dve.tensor_tensor(LB[:, :, 0], LA[:, :, 0], xw[:, :, 0], ALU.subtract)
                            link(dve.tensor_tensor(LB[:, :, 1], LA[:, :, 1, C - 1:C].to_broadcast([P, PAIRS, C]),
                                                   LA[:, :, 1], ALU.subtract))
                            dve.tensor_tensor(LA[:, :, 1], LB[:, :, 1], xw[:, :, 1], ALU.add).then_inc(l_log, 2)
                            dve.wait_ge(l_log, 2 * t + 2)

                        def keys():
                            dve.wait_ge(l_a, t + 1)
                            m1, a2d = (v.rearrange("p a d c -> p a (d c)") for v in (xw, av))
                            link(dve.scalar_tensor_tensor(out=m1, in0=a2d, scalar=-1.0,
                                                          in1=cols("k_a").unsqueeze(2).to_broadcast([P, PAIRS, P]),
                                                          op0=ALU.add, op1=ALU.mult))
                            earlier(dve, l_q, 2 * t)
                            for d in DIRS:
                                dve.scalar_tensor_tensor(out=kd[:, d], in0=xw[:, :, d], scalar=1.0, in1=chunk(kT, pr[d]),
                                                         op0=ALU.add, op1=ALU.mult).then_inc(l_kf, 1)

                        def queries(d):
                            kk2 = chunk(kkT, pr[d]).unsqueeze(2).to_broadcast([P, PAIRS, 2, C])
                            r2 = chunk(rT, pr[d]).unsqueeze(2).to_broadcast([P, PAIRS, 2, C])
                            earlier(dve, l_S[d], t)
                            dve.wait_ge(l_exp, 3 * t + 3)
                            dve.tensor_tensor(GR[nxt][d][:, :, 0:4:3, :], kk2,
                                              eB[:, :, d].unsqueeze(2).to_broadcast([P, PAIRS, 2, C]), ALU.mult)
                            dve.tensor_tensor(GR[nxt][d][:, :, 1:3, :], r2,
                                              eA[:, :, d].unsqueeze(2).to_broadcast([P, PAIRS, 2, C]), ALU.mult)

                        def keys_over_decay(d):
                            dve.wait_ge(l_kf, 2 * t + 2)
                            dve.tensor_tensor(GL[d][:, :, 1, :], kd[:, d], eN[:, :, d], ALU.mult).then_inc(l_kd, 1)
                            dve.wait_ge(l_b, 2 * t + 2)
                            dve.tensor_tensor(GL[d][:, :, 2, :], GL[d][:, :, 0, :], eN[:, :, d], ALU.mult)
                            dve.tensor_tensor(GL[d][:, :, 0, :], GL[d][:, :, 0, :], eN[:, :, d], ALU.mult).then_inc(l_ops[d], 1)

                        def masks(d):
                            ga, gb = (ps[:, 4 + 2 * d + g, :].rearrange("p (a s c) -> p a s c", a=PAIRS, s=2) for g in range(2))
                            if so:
                                dve.wait_ge(l_um[d], 4 * t + 4)
                            dve.wait_ge(l_gram[d], 2 * t + 1)
                            dve.tensor_tensor(Ub[d][lo, :, 0:64], ga[lo, :, 0], mask(d, lo, slice(0, 1))[:, :, 0], ALU.mult).then_inc(l_u[d], 1)
                            dve.wait_ge(l_gram[d], 2 * t + 2)
                            dve.tensor_tensor(Ub[d][hi, :, 64:128], gb[hi, :, 1], mask(d, hi, slice(0, 1))[:, :, 0], ALU.mult).then_inc(l_u[d], 1)
                            dve.tensor_tensor(GR[nxt][d][hi, :, 0:2, :], ga[hi], mask(d, hi, slice(0, 2)), ALU.mult)
                            dve.tensor_tensor(GR[nxt][d][lo, :, 2:4, :], gb[lo], mask(d, lo, slice(1, 3)), ALU.mult)
                            dve.tensor_tensor(AB[nxt][d][lo], ga[lo, :, 1], mask(d, lo, slice(1, 2))[:, :, 0], ALU.mult)
                            dve.tensor_tensor(AB[nxt][d][hi], gb[hi, :, 0], mask(d, hi, slice(1, 2))[:, :, 0], ALU.mult).then_inc(l_g[d], 1)

                        def factor(d, l):
                            dve.wait_ge(l_P[d], 5 * t + l)
                            dve.tensor_tensor(PX[d], eyes, pairs(2 * d, P), ALU.subtract).then_inc(l_pc[d], 1)

                        if so:
                            factor(0, 1)
                        if pr:
                            add_bias()
                        if so:
                            transpose_x(0, 1)
                            factor(1, 1)
                        if pr:
                            log_decays()
                        if so:
                            factor(0, 2)
                            transpose_x(1, 1)
                        if pr:
                            split_decays()
                        if so:
                            transpose_x(0, 2)
                            factor(1, 2)
                        if pr:
                            keys()
                        if so:
                            factor(0, 3)
                            transpose_x(1, 2)
                        if pr:
                            queries(0)
                        if so:
                            transpose_x(0, 3)
                            factor(1, 3)
                        if pr:
                            keys_over_decay(0)
                        if so:
                            factor(0, 4)
                            transpose_x(1, 3)
                        if pr:
                            queries(1)
                        if so:
                            transpose_x(0, 4)
                            factor(1, 4)
                        if pr:
                            keys_over_decay(1)
                        if so:
                            factor(0, 5)
                            transpose_x(1, 4)
                        if pr:
                            masks(0)
                        if so:
                            factor(1, 5)
                        if pr:
                            masks(1)
                            for d in DIRS:
                                dve.wait_ge(l_um0[d], 2 * t + 1)
                                if so:
                                    dve.wait_ge(l_U[d], t + 1)
                                dve.tensor_tensor(Y[d], eyes, Um[d], ALU.subtract).then_inc(l_Y0[d], 1)
                                dve.wait_ge(l_Y0[d], t + 1)
                                dve.transpose(X[d], Y[d]).then_inc(l_X0[d], 1)
                        if so:
                            for d in DIRS:
                                dve.wait_ge(l_S[d], t + 1)
                                yc = chunk(y, so[d])
                                link(dve.tensor_tensor(yc, yc, pairs(2 * d + 1, C), ALU.add))
                                s = ps[:, 2 * d + 1, 256:512].rearrange("p (a c) -> p a c", a=PAIRS)
                                for g, r in ((0, lo), (1, hi)):
                                    dve.tensor_tensor(SU[d][r, 0, :, g, :], SU[d][r, 0, :, g, :], s[r], ALU.add).then_inc(l_sum, 1)
                                dve.wait_ge(l_sum, 4 * t + 2 * d + 2)
                                for g, r in ((0, lo), (1, hi)):
                                    dve.tensor_tensor(SU[d][r, 0, :, g, :], SU[d][r, 0, :, g, :],
                                                      dend[r, now, d, :].unsqueeze(2).to_broadcast([64, PAIRS, C]),
                                                      ALU.mult).then_inc(l_st[d], 1)
            nc.all_engine_barrier(sems_to_clear=range(nums[0], nums[-1] + 1))

        def first_columns(base, chunks, i):
            return base + C * i, base + C * (chunks - 1) - C * i

        PC, SC = SEQ // C, DEC_SEQ // C
        prompt = [first_columns(TP, PC, i) for i in range(PC)]
        steps([None], [prompt[0]], start=1)
        steps(prompt, prompt[1:] + [first_columns(TS, SC, 0)])

        state_in = state_rwkv[0, 0].rearrange("d (a g) v k -> d g v a k", g=2)
        state_out = new_state[0, 0].rearrange("d (a g) v k -> d g v a k", g=2)
        with nc.Block() as block:
            @block.sync
            def _(sp):
                sp.wait_ge(s_sz, 1)
                for d in DIRS:
                    for g in range(2):
                        r = slice(64 * g, 64 * g + 64)
                        sp.dma_start(stin[d].rearrange("p (a k) -> p a k", a=PAIRS)[r, :, r], state_in[d, g]).then_inc(s_sl, 16)
                sp.wait_ge(s_sc2, 1)
                for d in DIRS:
                    for g in range(2):
                        r = slice(64 * g, 64 * g + 64)
                        sp.dma_start(state_out[d, g], sout[d][r, :, r]).then_inc(s_ns, 16)
                sp.wait_ge(s_ns, 64)

            @block.tensor
            def _(pe):
                for d in DIRS:
                    for a in range(PAIRS):
                        last = pe.transpose(pairs(d, P)[:, a, :], SU[d][:, 0, a].rearrange("p b c -> p (b c)"), eye[:, :])
                last.then_inc(s_so, 1)
                pe.wait_ge(s_sl, 64)
                for d in DIRS:
                    for a in range(PAIRS):
                        last = pe.transpose(pairs(2 + d, P)[:, a, :], stin[d][:, P * a:P * a + P], eye[:, :])
                last.then_inc(s_st, 1)

            @block.vector
            def _(dve):
                dve.memset(stin[0], 0.0)
                dve.memset(stin[1], 0.0).then_inc(s_sz, 1)
                dve.wait_ge(s_so, 1)
                dve.tensor_copy(sout[0], pairs(0, P))
                dve.tensor_copy(sout[1], pairs(1, P)).then_inc(s_sc2, 1)
                dve.wait_ge(s_st, 1)
                for d in DIRS:
                    dve.tensor_copy(SU[d][:, 0].rearrange("p a b c -> p a (b c)"), pairs(2 + d, P))

        with nc.Fori(0, SC // UNROLL - 1) as i:
            at = [first_columns(TS, SC, UNROLL * i + n) for n in range(UNROLL + 1)]
            steps(at[:-1], at[1:])
        last = [first_columns(TS, SC, n) for n in range(SC - UNROLL, SC)]
        steps(last, last[1:] + [None])

        take = carve()
        gt = take(4, W)
        sq = take(2, NC)
        sd = take(NC)
        XO = 3
        xr = take(XO, D_MODEL)
        gout = take(2, D_MODEL)
        gg = take(2, D_MODEL)
        jk = take(D_MODEL)
        yab = kkT
        wo = zflat[:, 4 * W:4 * W + 8 * D_MODEL].rearrange("p (k n) -> p k n", k=8)
        ss2, rs2 = small[:, 0:9], small[:, 9:18]
        BLOCKS = [(a, slice(b * NC, (b + 1) * NC)) for b in range(NB) for a in range(4)]
        GT_PARTS = [slice(b * NC, (b + 1) * NC) for b in range(NB)]
        first_col = [TP if i == 0 else TS + P * (i - 1) for i in range(9)]
        needs = [4 * ((at + P - 1) // NC + 1) for at in first_col]

        s_gl = sem("gate_c_landed")
        s_wo = sem("w_out_landed")
        s_ab = sem("branches_landed")
        s_gg = sem("gate_rows_landed")
        f_dve = sem("final_dve_chain")
        f_pm = sem("gn_mean_summed")
        f_xc = sem("gn_centred")
        f_sq = sem("gn_squared")
        f_pv = sem("gn_variance_summed")
        f_sd = sem("gn_deviation_ready")
        f_rs = sem("gn_deviation_inverted")
        f_pr = sem("gn_deviation_spread")
        f_n = sem("gn_normalised")
        f_af = sem("gn_scaled")
        f_bo = sem("gn_bonus_added")
        f_yc = sem("yc_ready")
        f_bq = sem("bonus_scaled")
        f_pb = sem("bonus_summed")
        f_bd = sem("bonus_ready")
        s_xr = [sem(f"residual_landed_{i}") for i in range(XO)]
        s_o = sem("output_multiplied")
        s_oq = sem("output_squared")
        s_os = sem("output_deviation_ready")
        s_og = sem("output_gated")
        s_or = sem("output_ready")
        s_st2 = [sem(f"output_stored_{i}") for i in range(XO)]

        with nc.Block() as block:
            @block.sync
            def _(sp):
                def store(i):
                    sp.wait_ge(s_or, i + 1)
                    sp.dma_start(y_prompt[0] if i == 0 else y_sample[0, P * (i - 1):P * i, :],
                                 xr[:, i % XO, :]).then_inc(s_st2[i % XO], 16)

                for n, cut in enumerate(GT_PARTS):
                    sp.dma_start(gt[:, :, cut], mix_dram[4:8, :, cut].rearrange("m p w -> p m w")).then_inc(s_gl, 16)
                    sp.wait_ge(s_gl, 16 * (n + 1))
                    if n == 0:
                        sp.dma_start(yab, mix_dram[0:4].rearrange("m p w -> p m w")).then_inc(s_ab, 16)
                        sp.dma_start(wo, w_out[0].rearrange("(k p) n -> p k n", p=P)).then_inc(s_wo, 16)
                sp.dma_start(gg, gate_dram[:, :].unsqueeze(0).to_broadcast([P, 2, D_MODEL])).then_inc(s_gg, 16)
                for i in range(9):
                    if i >= XO:
                        sp.wait_ge(s_st2[i % XO], 16 * (i // XO))
                    sp.dma_start(xr[:, i % XO, :], x_prompt[0] if i == 0 else x_sample[0, P * (i - 1):P * i, :]).then_inc(s_xr[i % XO], 16)
                    if i >= XO - 1:
                        store(i - XO + 1)
                for i in range(9 - XO + 1, 9):
                    store(i)
                for i in range(XO):
                    sp.wait_ge(s_st2[i], 16 * 3)

            @block.tensor
            def _(pe):
                def mean_and_bonus(n):
                    a, cut = BLOCKS[n]
                    if n:
                        pe.wait_ge(f_xc, n)
                    if n and a == 0:
                        pe.wait_ge(f_n, n)
                    pe.matmul(ps[:, 4, 0:NC], heads[:, :], y[:, a, cut], start=True, stop=True).then_inc(f_pm, 1)
                    pe.wait_ge(f_bq, min(n, 3) + 1)
                    if n:
                        pe.wait_ge(f_bd, n)
                    pe.matmul(ps[:, 5, 0:NC], heads[:, :], q[:, a, cut], start=True, stop=True).then_inc(f_pb, 1)

                def variance(n):
                    a = BLOCKS[n][0]
                    pe.wait_ge(f_sq, n + 1)
                    if a == 0 and n:
                        pe.wait_ge(f_sd, n // 4)
                    pe.matmul(ps[32 * a:32 * a + 32, 6, 0:NC], heads[:, 48:80], sq[:, n % 2, :],
                              start=True, stop=True).then_inc(f_pv, 1)

                def spread(n):
                    a = BLOCKS[n][0]
                    r = slice(32 * a, 32 * a + 32)
                    pe.wait_ge(f_rs, n // 4 + 1)
                    if a >= 2:
                        pe.wait_ge(f_n, n - 1)
                    elif a == 1:
                        pe.wait_ge(f_xc, n + 3)
                    elif n:
                        pe.wait_ge(f_n, n)
                    pe.matmul(ps[:, (7, 4)[a % 2], 0:NC], back[r, :], sd[r, :], start=True, stop=True).then_inc(f_pr, 1)

                def statistics(b):
                    for n in range(4 * b, 4 * b + 4):
                        mean_and_bonus(n)
                        if n > 4 * b:
                            variance(n - 1)
                    variance(4 * b + 3)

                def spreads(b):
                    for n in range(4 * b, 4 * b + 4):
                        spread(n)

                def output(i):
                    if i == 0:
                        pe.wait_ge(s_ab, 16)
                        pe.wait_ge(s_wo, 16)
                    pe.wait_ge(f_yc, needs[i])
                    at = first_col[i]
                    if i >= 2:
                        pe.wait_ge(s_og, i - 1)
                    for k in range(8):
                        src = yab[:, k, at:at + P] if k < 4 else y[:, k - 4, at:at + P]
                        for b in range(2):
                            last = pe.matmul(ps[:, 2 * (i % 2) + b, :], src, wo[:, k, 512 * b:512 * b + 512],
                                             start=(k == 0), stop=(k == 7))
                    last.then_inc(s_o, 1)

                statistics(0)
                spreads(0)
                statistics(1)
                output(0)
                spreads(1)
                statistics(2)
                output(1)
                spreads(2)
                for i in range(2, 9):
                    output(i)

            @block.scalar
            def _(act):
                def bonus_keys(a):
                    act.activation(q[:, a, :], q[:, a, :], ACT.Copy, scale=col("r_k", a)).then_inc(f_bq, 1)

                def deviation(b):
                    act.wait_ge(f_pv, 4 * b + 4)
                    if b:
                        act.wait_ge(f_pr, 4 * b)
                    act.activation(sd, ps[:, 6, 0:NC], ACT.Sqrt, bias=epst[:, 3:4], scale=1.0 / HEAD).then_inc(f_sd, 1)

                def affine(n):
                    a, cut = BLOCKS[n]
                    act.wait_ge(f_n, n + 1)
                    act.activation(y[:, a, cut], y[:, a, cut], ACT.Identity, bias=col("gn_b", a), scale=col("gn_g", a)).then_inc(f_af, 1)

                def mean_square(i):
                    b = 2 * (i % 2)
                    act.wait_ge(s_o, i + 1)
                    act.activation(jk, ps[:, b:b + 2, :].rearrange("p b n -> p (b n)"), ACT.Square,
                                   accum_out=ss2[:, i:i + 1]).then_inc(s_oq, 1)
                    act.wait_ge(s_oq, i + 1)
                    act.activation(ss2[:, i:i + 1], ss2[:, i:i + 1], ACT.Sqrt, bias=epst[:, 0:1], scale=1.0 / D_MODEL).then_inc(s_os, 1)

                def square(n):
                    a, cut = BLOCKS[n]
                    act.wait_ge(f_xc, n + 1)
                    if n >= 2:
                        act.wait_ge(f_pv, n - 1)
                    act.activation(sq[:, n % 2, :], y[:, a, cut], ACT.Square).then_inc(f_sq, 1)

                bonus_keys(0)
                for n in range(4):
                    square(n)
                    if n < 3:
                        bonus_keys(n + 1)
                for b in range(NB):
                    deviation(b)
                    for n in range(4 * b, 4 * b + 4):
                        affine(n)
                    if b < NB - 1:
                        for n in range(4 * b + 4, 4 * b + 8):
                            square(n)
                for i in range(9):
                    mean_square(i)

            @block.gpsimd
            def _(pool):
                for n, (a, cut) in enumerate(BLOCKS):
                    pool.wait_ge(f_af, n + 1)
                    pool.wait_ge(f_bd, n + 1)
                    pool.tensor_tensor(y[:, a, cut], y[:, a, cut], vT[:, a, cut], ALU.add).then_inc(f_bo, 1)

            @block.vector
            def _(dve):
                def centre(n):
                    a, cut = BLOCKS[n]
                    dve.wait_ge(f_pm, n + 1)
                    dve.scalar_tensor_tensor(out=y[:, a, cut], in0=ps[:, 4, 0:NC], scalar=-1.0 / HEAD, in1=y[:, a, cut],
                                             op0=ALU.mult, op1=ALU.add).then_inc(f_xc, 1)
                    dve.wait_ge(f_pb, n + 1)
                    dve.tensor_tensor(vT[:, a, cut], vT[:, a, cut], ps[:, 5, 0:NC], ALU.mult).then_inc(f_bd, 1)

                def invert(b):
                    dve.wait_ge(f_sd, b + 1)
                    dve.reciprocal(sd, sd).then_inc(f_rs, 1)

                def normalise(n):
                    a, cut = BLOCKS[n]
                    dve.wait_ge(f_pr, n + 1)
                    dve.tensor_tensor(y[:, a, cut], y[:, a, cut], ps[:, (7, 4)[a % 2], 0:NC], ALU.mult).then_inc(f_n, 1)

                def gate(n):
                    a, cut = BLOCKS[n]
                    dve.wait_ge(f_bo, n + 1)
                    dve.wait_ge(s_gl, 16 * (n // 4 + 1))
                    dve.scalar_tensor_tensor(out=y[:, a, cut], in0=gt[:, a, cut], scalar=0.5, in1=y[:, a, cut],
                                             op0=ALU.mult, op1=ALU.mult).then_inc(f_yc, 1)

                for b in range(NB):
                    group = range(4 * b, 4 * b + 4)
                    for n in group:
                        centre(n)
                    invert(b)
                    for n in group:
                        normalise(n)
                        if n >= 4 * b + 2:
                            gate(n - 2)
                    gate(4 * b + 2)
                    gate(4 * b + 3)
                dve.wait_ge(s_gg, 16)
                for i in range(9):
                    b, slot = 2 * (i % 2), i % XO
                    dve.wait_ge(s_os, i + 1)
                    dve.reciprocal(rs2[:, i:i + 1], ss2[:, i:i + 1]).then_inc(f_dve, 1)
                    dve.wait_ge(f_dve, i + 1)
                    dve.scalar_tensor_tensor(out=gout[:, i % 2, :], in0=ps[:, b:b + 2, :].rearrange("p b n -> p (b n)"),
                                             scalar=rs2[:, i:i + 1], in1=gg[:, min(i, 1), :],
                                             op0=ALU.mult, op1=ALU.mult).then_inc(s_og, 1)
                    dve.wait_ge(s_og, i + 1)
                    dve.wait_ge(s_xr[slot], 16 * (i // XO + 1))
                    dve.tensor_tensor(xr[:, slot, :], xr[:, slot, :], gout[:, i % 2, :], ALU.add).then_inc(s_or, 1)


_INS = ["x_prompt", "x_sample", "c", "state_rwkv", "c_ctx", "ada_w", "ada_b", "g_pre", "g_post", "w_in",
        "conv_a", "conv_b", "conv_b_bias", "ln_b_g", "ln_b_b", "mu", "w0", "w2", "a0", "a2", "k_k", "k_a",
        "r_k", "gn_g", "gn_b", "w_out"]
_OUTS = [(1, SEQ, D_MODEL), (1, DEC_SEQ, D_MODEL), (1, 1, 2, 8, 64, 64)]


def kernel(**inputs):
    import numpy as _np
    import concourse.bacc as _bacc
    from concourse import mybir as _mybir
    from concourse.bass_utils import run_bass_kernel_spmd as _run

    nc = _bacc.Bacc("TRN2", target_bir_lowering=False, num_devices=1)
    arrays, args = {}, []
    for name in _INS:
        a = _np.ascontiguousarray(inputs[name])
        arrays[f"in_{name}"] = a
        args.append(nc.dram_tensor(f"in_{name}", a.shape, _mybir.dt.from_np(a.dtype), kind="ExternalInput").ap())
    for i, shape in enumerate(_OUTS):
        args.append(nc.dram_tensor(f"out_{i}", shape, _mybir.dt.float32, kind="ExternalOutput").ap())
    hybrid_step_kernel(nc, *args)
    r = _run(nc, [arrays], core_ids=[0])
    return tuple(r.results[0][f"out_{i}"] for i in range(len(_OUTS)))
```

```python
from contextlib import ExitStack

import concourse.bass as bass
from concourse import mybir

ALU = mybir.AluOpType
ACT = mybir.ActivationFunctionType
F32 = mybir.dt.float32
F32R = mybir.dt.float32r

P = 128
D_MODEL = 1024
KT = D_MODEL // P
SEQ, DEC_SEQ = 128, 1024
GRID_W = 64
ROWS = DEC_SEQ // GRID_W
TP, TS = 2, 132
W = TS + DEC_SEQ + 2
NB = 3
NC = W // NB
D_MIX = 1024
CONV_A, CONV_B = 3, 31
HEAD = 64
C = 64
PAIRS = 4
LEVELS = 6
POOL_CLEARS = 3
UNROLL = 6
E_HALF = 0.6065306597126334
RMS_EPS, LN_EPS, GN_EPS, KK_EPS = 1e-6, 1e-5, 64e-5, 1e-12

VEC_ROWS = {}
_n = 0
for _name, _rows in (("c_ctx", 8), ("c", 8), ("g_pre", 8), ("conv_b_bias", 2), ("ln_b_g", 2), ("ln_b_b", 2),
                     ("mu", 14), ("w0", 8), ("a0", 8), ("k_k", 4), ("k_a", 4), ("r_k", 4), ("gn_g", 4),
                     ("gn_b", 4), ("conv_a", 6)):
    VEC_ROWS[_name] = (_n, _rows)
    _n += _rows
N_VEC = _n
N_CB = 2 * CONV_B
N_C = VEC_ROWS["c_ctx"][1] + VEC_ROWS["c"][1]


PIECES = [("gc", 14), ("gc", 15), ("u2", 5), ("u1", 4), ("gb", 6), ("xa", 0), ("cg", 2), ("bg", 1), ("ga", 3),
          ("mix", 7), ("mix", 8), ("mix", 9), ("mix", 10), ("mix", 11), ("mix", 12), ("mix", 13)]
TILES = [kind for kind, _ in PIECES for _ in range(2)]
MIX0 = TILES.index("mix")
MIXES = TILES.count("mix")
RING = 3
PIECE = 2048
N_ADA = KT
GATE_AFTER = 1
GATES = KT // 2
LOADS = [("ada", k) for k in range(KT)]
for _n in range(len(PIECES)):
    LOADS.append(("z", _n))
    if 0 <= _n - GATE_AFTER < GATES:
        LOADS.append(("gate", _n - GATE_AFTER))
HT_BANKS = [(k, TP, P, 0, 0) for k in range(KT)] + \
           [(k, TS + 512 * g, 512, 1 + 4 * g, 1) for g in range(2) for k in range(KT)]
REST_BY = [1 if n % 5 in (1, 3) else 0 for n in range(len(HT_BANKS))]


def rests(by, n):
    return REST_BY[:n].count(by)


def hybrid_step_kernel(nc, x_prompt, x_sample, c, state_rwkv, c_ctx, ada_w, ada_b, g_pre, g_post, w_in,
                       conv_a, conv_b, conv_b_bias, ln_b_g, ln_b_b, mu, w0, w2, a0, a2, k_k, k_a,
                       r_k, gn_g, gn_b, w_out, y_prompt, y_sample, new_state):
    ctx = ExitStack()
    with ctx:
        def sb(name, *shape):
            return ctx.enter_context(nc.sbuf_tensor(name, [P, *shape], F32))

        def place(tensor):
            return nc.sbuf_base - tensor_bytes(tensor)

        def tensor_bytes(tensor):
            n = 4
            for size in tensor.shape[1:]:
                n *= size
            return n

        def rounded(name, at, *shape):
            return nc.alloc_sbuf_tensor_at(name, [P, *shape], F32R, offset=at)[:, :, :]

        def sem(name):
            return ctx.enter_context(nc.semaphore(name))

        ps = ctx.enter_context(nc.psum_tensor("ps", [P, 8, 512], F32))
        gate_dram = nc.dram_tensor("gate_scratch", [2, D_MODEL], F32, kind="Internal").ap()
        mix_dram = nc.dram_tensor("mix_scratch", [8, P, W], F32, kind="Internal").ap()

        hT = sb("hT", KT, W)
        hT_at = place(hT)
        y = hT[:, 0:4, :]
        q = hT[:, 4:8, :]
        zc = sb("zc", 18, W)
        zc_at = place(zc)
        vT, kT, rT, kkT = (zc[:, 4 * n:4 * n + 4, :] for n in range(4))
        lwT, laT = zc[:, 16, :], zc[:, 17, :]
        zflat = zc[:, :, :].rearrange("p a w -> p (a w)")
        xtok = zflat[:, 0:9 * D_MODEL].rearrange("p (i d) -> p i d", i=9)
        ARENA = 20240
        arena = sb("arena", ARENA)
        arena_at = place(arena)
        vec = sb("vec", N_VEC)
        cb = sb("cb", N_CB)
        cah = sb("cah", 6)
        smod = sb("smod", 16)
        hmu = sb("hmu", 14)
        omu = sb("omu", 14)
        shf = sb("shf", KT, 2)
        scl = sb("scl", KT, 2)
        small = sb("small", 36)
        epst = sb("epst", 4)
        lvl = sb("lvl", LEVELS, P)
        eye = sb("eye", P)
        heads = sb("heads", P)
        tri = sb("tri", 2, 3, C)
        w2s = sb("w2s", 512)
        a2s = sb("a2s", 512)

        def carve(start=0):
            at = [start]

            def take(*shape):
                n = 1
                for s in shape:
                    n *= s
                v = arena[:, at[0]:at[0] + n]
                at[0] += n
                assert at[0] <= ARENA, at[0]
                if len(shape) == 1:
                    return v
                names = "abcd"[:len(shape)]
                return v.rearrange(f"p ({' '.join(names)}) -> p {' '.join(names)}",
                                   **{names[i]: shape[i] for i in range(len(shape))})
            return take

        def cols(name):
            return vec[:, VEC_ROWS[name][0]:VEC_ROWS[name][0] + VEC_ROWS[name][1]]

        def col(name, i):
            return cols(name)[:, i:i + 1]


        DIRS = range(2)
        s_sl = sem("state_landed")

        state_in = state_rwkv[0, 0].rearrange("d (a g) v k -> d g v a k", g=2)

        step_sems = []

        def ssem(name):
            s = sem(name)
            step_sems.append(s)
            return s

        l_stage = ssem("lora_input_staged")
        l_lora = ssem("lora_multiplied")
        l_x = ssem("lora_bias_added")
        l_tanh = ssem("gates_tanh_ready")
        l_dve = ssem("step_dve_chain")
        l_pool = ssem("step_pool_chain")
        l_q = ssem("bonus_key_summed")
        l_log = ssem("log_decay_ready")
        l_exp = ssem("decay_ready")
        l_end = ssem("chunk_decay_copied")
        l_kd = ssem("kd_over_decay_ready")
        l_kf = ssem("kd_ready")
        l_a = ssem("a_ready")
        l_b = ssem("b_ready")
        l_sum = ssem("state_summed")
        l_ops = [ssem(f"operands_ready_{d}") for d in DIRS]
        l_gram = [ssem(f"products_ready_{d}") for d in DIRS]
        l_vd = [ssem(f"v_doubled_{d}") for d in DIRS]
        l_vt = [ssem(f"v_transposed_{d}") for d in DIRS]
        l_kt = [ssem(f"keys_transposed_{d}") for d in DIRS]
        l_v = [ssem(f"v_by_token_{d}") for d in DIRS]
        l_kb = [ssem(f"keys_by_token_{d}") for d in DIRS]
        l_u = [ssem(f"m_b_masked_{d}") for d in DIRS]
        l_g = [ssem(f"products_masked_{d}") for d in DIRS]
        l_um0 = [ssem(f"first_levels_masked_{d}") for d in DIRS]
        l_um = [ssem(f"level_masked_{d}") for d in DIRS]
        l_Y0 = [ssem(f"inverse_of_twos_transposed_{d}") for d in DIRS]
        l_X0 = [ssem(f"inverse_of_twos_{d}") for d in DIRS]
        l_X = [ssem(f"inverse_ready_{d}") for d in DIRS]
        l_Y = [ssem(f"inverse_transposed_ready_{d}") for d in DIRS]
        l_P = [ssem(f"level_product_{d}") for d in DIRS]
        l_pc = [ssem(f"level_factor_ready_{d}") for d in DIRS]
        l_Q = [ssem(f"level_update_{d}") for d in DIRS]
        l_rhs = [ssem(f"rhs_multiplied_{d}") for d in DIRS]
        l_rh = [ssem(f"rhs_copied_{d}") for d in DIRS]
        l_U = [ssem(f"u_multiplied_{d}") for d in DIRS]
        l_uc = [ssem(f"u_copied_{d}") for d in DIRS]
        l_S = [ssem(f"outputs_multiplied_{d}") for d in DIRS]
        l_st = [ssem(f"state_ready_{d}") for d in DIRS]
        nums = [s.num for s in step_sems]
        assert nums == list(range(nums[0], nums[0] + len(nums)))

        take = carve()
        ls = take(2, P)
        xw = take(PAIRS, 2, C)
        av = take(PAIRS, 2, C)
        LA = take(PAIRS, 2, C)
        LB = take(PAIRS, 2, C)
        eA, eB, eN = take(PAIRS, 2, C), LB, LA
        kd = take(2, PAIRS, C)
        keep = take(512)
        stin = [take(512) for _ in DIRS]
        SU = [take(2, PAIRS, 2, C) for _ in DIRS]
        dend = take(2, 2, PAIRS)
        GL = [take(PAIRS, 3, C) for _ in DIRS]
        GR = [[take(PAIRS, 4, C) for _ in DIRS] for _ in range(2)]
        AB = [[take(PAIRS, C) for _ in DIRS] for _ in range(2)]
        Ub = [take(PAIRS, P) for _ in DIRS]
        Um = [take(PAIRS, P) for _ in DIRS]
        X = [take(PAIRS, P) for _ in DIRS]
        Y = [take(PAIRS, P) for _ in DIRS]
        PX = [take(PAIRS, P) for _ in DIRS]
        KB = [take(PAIRS, 2, C) for _ in DIRS]
        RH = [take(PAIRS, C) for _ in DIRS]
        VD = [xw, av]
        sout = [v.rearrange("p (a k) -> p a k", a=PAIRS) for v in stin]

        take = carve()
        ring = take(RING, PIECE)
        take(2, PIECE)
        lo2 = take(4, W)
        raw = take(2, W)
        nsum = take(W)
        ones = take(P)
        back = take(4, P)
        kn = take(W)
        w_rest = rounded("weights_rest", arena_at, RING, PIECE)
        w_round = rounded("weights_rounded", arena_at + 4 * RING * PIECE, 2, PIECE)
        lo2_r = rounded("input_rest_2", arena_at + 4 * (RING + 2) * PIECE, 4, W)
        kk_r = rounded("input_rest_1", zc_at + 4 * 12 * W, 4, W)
        hi_of_h = rounded("input_rounded", hT_at, KT, W)
        lo_full = [kkT[:, k, :] if k < 4 else lo2[:, k - 4, :] for k in range(KT)]
        lo_of_h = [kk_r[:, k, :] if k < 4 else lo2_r[:, k - 4, :] for k in range(KT)]
        T = zc[:, 0:8, :]
        xa, ya = rT, zc[:, 16:18, :]
        va, vb = raw[:, 0, 0:P], raw[:, 0, P:2 * P]
        junk = kn[:, 16:16 + D_MODEL]
        spare = rT.rearrange("p a w -> p (a w)")
        row, adab = spare[0:2, 0:2048], spare[0:2, 2048:4096]
        grow, gpost = zc[0:2, 16, 0:D_MODEL], zc[0:2, 17, 0:D_MODEL]
        blocks = raw[:, 1, 0:7 * P].rearrange("p (l j) -> p l j", l=7)
        triw = nsum[:, 0:4 * P].rearrange("p (l j) -> p l j", l=4)
        ss, rs = small[:, 0:9], small[:, 9:18]

        part1 = ExitStack()

        def sem1(name):
            s = part1.enter_context(nc.semaphore(name))
            sems1.append(s.num)
            return s

        sems1 = []
        s_vec = sem1("vectors_landed")
        s_w2 = sem1("lora_landed")
        s_x = [sem1(f"x_landed_{i}") for i in range(3)]
        s_adab = sem1("ada_b_landed")
        s_wl = [sem1(f"weights_landed_{i}") for i in range(RING)]
        s_wu = sem1("weights_used")
        s_wh = sem1("weights_rounded")
        s_wo1 = sem1("weights_rest_ready")
        s_hf = sem1("hT_copied_full")
        s_hs = [sem1("hT_rest_by_pool"), sem1("hT_rest_by_dve")]
        s_gu = sem1("gate_weights_used")
        s_gr = sem1("gate_row_ready")
        s_gst = sem1("gate_row_stored")
        s_const = sem1("constants_built")
        s_pool = sem1("pool_chain")
        s_dve = sem1("dve_chain")
        s_c = sem1("modulation_landed")
        s_ct = sem1("modulation_transposed")
        s_vt = sem1("vectors_transposed")
        s_vc = sem1("vectors_copied")
        s_tm = sem1("tanh_of_modulation")
        s_smod = sem1("silu_of_modulation")
        s_row = sem1("ada_rows_copied")
        s_at = sem1("ada_transposed")
        s_sc = sem1("scale_shift_ready")
        s_ss = sem1("squares_summed")
        s_ms = sem1("mean_square_ready")
        s_sd = sem1("x_deviation_ready")
        s_xn = sem1("x_normalised")
        s_xt = sem1("x_transposed")
        s_ha = sem1("hT_written_by_act")
        s_z = sem1("tile_projected")
        s_th = sem1("tanh_ready")
        s_glu = sem1("glu_ready")
        s_gb = sem1("gate_b_ready")
        s_xa = sem1("xa_copied")
        s_cx = sem1("cg_times_xa_ready")
        s_bg = sem1("bg_applied")
        s_ya = sem1("ya_ready")
        s_raw = sem1("raw_copied")
        s_sum = sem1("neighbours_summed")
        s_mix = sem1("shift_mixed")
        s_lwt = sem1("lw_tanh_ready")
        s_cv = sem1("conv_b_done")
        s_lm = sem1("ln_mean_summed")
        s_lx = sem1("ln_centred")
        s_lq = sem1("ln_squared")
        s_lv = sem1("ln_variance_summed")
        s_ls = sem1("ln_deviation_ready")
        s_lr = sem1("ln_scaled")
        s_lt = sem1("ln_tanh_ready")
        s_yb = sem1("yb_ready")
        s_kq = sem1("kk_squared")
        s_ks = sem1("kk_square_summed")
        s_kd = sem1("kk_deviation_ready")
        s_kr = sem1("kk_deviation_inverted")
        s_kp = sem1("kk_deviation_spread")
        s_kn = sem1("kk_normalised")
        s_zero = sem1("state_staging_zero")
        s_gc = sem1("gate_c_ready")
        s_sa = sem1("ya_spilled")
        s_sb = sem1("yb_spilled")
        s_sg = sem1("gate_c_spilled")

        def dest(m):
            return zc[:, m + 8 if m < 4 else m if m < 8 else m - 8 if m < 12 else m + 4, :]

        def zbanks(j):
            return ps[:, NB * (j % 2):NB * (j % 2) + NB, 0:NC]

        def as3(a):
            return a.rearrange("p (n w) -> p n w", n=NB)

        def read_by(j):
            i = j - TILES.index(TILES[j])
            if TILES[j] == "u2":
                i += TILES.count("gc")
            return {"u2": s_th, "u1": s_glu, "gb": s_gb, "xa": s_xa, "cg": s_cx, "bg": s_bg, "ga": s_ya,
                    "mix": s_raw, "gc": s_gc}[TILES[j]], i + 1

        with nc.Block() as block:
            @block.sync
            def _(sp):
                def flat(a):
                    names = "abcd"[:len(a.shape)]
                    return a if len(names) == 1 else a.rearrange(f"{' '.join(names)} -> ({' '.join(names)})")

                def load_ada(k):
                    sp.dma_start(ring[:, k % RING, :], ada_w[0, k * P:(k + 1) * P, 0:2048]).then_inc(s_wl[k % RING], 16)

                given = {"c_ctx": c_ctx, "c": c, "g_pre": g_pre, "conv_b_bias": conv_b_bias, "ln_b_g": ln_b_g,
                         "ln_b_b": ln_b_b, "mu": mu, "w0": w0, "a0": a0, "k_k": k_k, "k_a": k_a, "r_k": r_k,
                         "gn_g": gn_g, "gn_b": gn_b, "conv_a": conv_a}
                for name, (r0, n) in VEC_ROWS.items():
                    sp.dma_start(va[r0:r0 + n, :], flat(given[name]).rearrange("(r p) -> r p", p=P)).then_inc(
                        s_c if name in ("c_ctx", "c") else s_vec, 16)
                    if name == "c":
                        for k in range(RING):
                            load_ada(k)
                sp.dma_start(vb[0:N_CB, :], conv_b.rearrange("a j (h p) -> (a j h) p", p=P)).then_inc(s_vec, 16)

                def spill(first, tiles, ready, count, spilled):
                    sp.wait_ge(ready, count)
                    sp.dma_start(mix_dram[first:first + 2].rearrange("m p w -> p m w"), tiles).then_inc(spilled, 16)

                for n, (kind, k) in enumerate(LOADS):
                    if n >= RING:
                        before, m = LOADS[n - RING]
                        used, per = {"ada": (s_wu, 1), "gate": (s_gu, 1), "z": (s_z, 2)}[before]
                        sp.wait_ge(used, per * (m + 1))
                    slot = ring[:, n % RING, :]
                    if kind == "ada":
                        if k >= RING:
                            load_ada(k)
                    elif kind == "gate":
                        sp.dma_start(slot.rearrange("p (k n) -> p k n", k=2),
                                     ada_w[0, 2 * k * P:2 * (k + 1) * P, 2048:3072].rearrange("(k p) n -> p k n", p=P)).then_inc(s_wl[n % RING], 16)
                    else:
                        at = 256 * PIECES[k][1]
                        sp.dma_start(slot.rearrange("p (k n) -> p k n", k=KT),
                                     w_in[0, :, at:at + 256].rearrange("(k p) n -> p k n", p=P)).then_inc(s_wl[n % RING], 16)
                    if n == 0:
                        for s in range(2):
                            sp.dma_start(adab[s:s + 1, :], ada_b[:, 0:2048]).then_inc(s_adab, 16)
                            sp.dma_start(grow[s:s + 1, :], ada_b[:, 2048:3072]).then_inc(s_adab, 16)
                            sp.dma_start(gpost[s:s + 1, :], g_post).then_inc(s_adab, 16)
                    if (kind, k) == ("z", GATE_AFTER + GATES + 2):
                        sp.wait_ge(s_gr, 1)
                        sp.dma_start(gate_dram, grow).then_inc(s_gst, 16)
                    if (kind, k) == ("z", 4):
                        spill(4, T[:, 4:6, :], s_gc, 2, s_sg)
                    if (kind, k) == ("z", 5):
                        spill(6, T[:, 6:8, :], s_gc, 4, s_sg)
                    if (kind, k) == ("z", MIX0 // 2 + RING):
                        spill(0, ya, s_ya, 2, s_sa)
                    if (kind, k) == ("z", MIX0 // 2 + RING + 1):
                        spill(2, T[:, 6:8, :], s_yb, 2, s_sb)
                sp.wait_ge(s_zero, 1)
                for d in DIRS:
                    for g in range(2):
                        r = slice(64 * g, 64 * g + 64)
                        sp.dma_start(stin[d].rearrange("p (a k) -> p a k", a=PAIRS)[r, :, r], state_in[d, g]).then_inc(s_sl, 16)
                sp.wait_ge(s_gst, 16)
                sp.wait_ge(s_sg, 32)
                sp.wait_ge(s_sa, 16)
                sp.wait_ge(s_sb, 16)

            @block.gpsimd
            def _(pool):
                n_pool = [0]

                def link(ins):
                    n_pool[0] += 1
                    ins.then_inc(s_pool, 1)
                    pool.wait_ge(s_pool, n_pool[0])

                link(pool.memset(blocks, 1.0))
                for l in range(7):
                    b = 1 << l
                    m = blocks[:, l, :].rearrange("p (n b) -> p n b", b=b)
                    link(pool.affine_select(out=m, in_=m, compare_op=ALU.is_ge, fill=0.0, base=0,
                                            pattern=[[-b, P // b], [0, b]], channel_multiplier=1))
                    link(pool.affine_select(out=m, in_=m, compare_op=ALU.is_ge, fill=0.0, base=b - 1,
                                            pattern=[[b, P // b], [0, b]], channel_multiplier=-1))
                    if l == 0:
                        pool.tensor_copy(eye[:, :], blocks[:, 0, :]).then_inc(s_const, 1)
                pool.tensor_copy(heads[:, :], blocks[:, 6, :])
                pool.tensor_tensor(lvl[:, :, :], blocks[:, 1:7, :], blocks[:, 0:6, :], ALU.subtract)
                pool.memset(ones[:, :], 1.0 / 256)
                link(pool.memset(triw, 1.0))
                for n, (sign, base) in enumerate(((1, -1), (1, 0), (-1, -1), (-1, 0))):
                    link(pool.affine_select(out=triw[:, n, :], in_=triw[:, n, :], compare_op=ALU.is_ge, fill=0.0,
                                            base=base, pattern=[[sign, P]], channel_multiplier=-sign))
                for d in range(2):
                    for half in range(2):
                        r = slice(64 * half, 64 * half + 64)
                        for slot, kind in enumerate((0, 1, 0)):
                            link(pool.tensor_copy(tri[r, d, slot, :], triw[r, 2 * d + kind, r]))
                for n, e in enumerate((RMS_EPS, LN_EPS, KK_EPS, GN_EPS)):
                    pool.memset(epst[:, n:n + 1], e)
                link(pool.memset(back, 0.0))
                link(pool.affine_select(out=back, in_=back, compare_op=ALU.not_equal, fill=1.0, base=0,
                                        pattern=[[-32, 4], [-16, 2], [0, HEAD]], channel_multiplier=1))
                link(pool.memset(kn[:, 0:16], 0.0))
                for a in (0, TS - 2, W - 2):
                    for v, n in ((hi_of_h, KT), (kk_r, 4), (lo2_r, 4)):
                        last = pool.tensor_copy(v[:, :, a:a + 2], kn[:, 0:2 * n].rearrange("p (k c) -> p k c", c=2))
                last.then_inc(s_const, 1)
                def split_rest(p):
                    slot = ring[:, LOADS.index(("z", p)) % RING, :]
                    pool.wait_ge(s_wh, p + 1)
                    pool.tensor_tensor(w_rest[:, LOADS.index(("z", p)) % RING, :], slot,
                                       w_round[:, p % 2, :].bitcast(F32), ALU.subtract).then_inc(s_wo1, 1)

                for n, (k, at, w, _, s) in enumerate(HT_BANKS):
                    if n == KT + 2:
                        split_rest(0)
                    if REST_BY[n] != 0:
                        continue
                    pool.wait_ge(s_hf, n + 1)
                    pool.tensor_tensor(lo_of_h[k][:, at:at + w], lo_full[k][:, at:at + w], hi_of_h[:, k, at:at + w].bitcast(F32),
                                       ALU.subtract).then_inc(s_hs[0], 1)

                for j in range(len(TILES)):
                    if j % 2 == 0 and j // 2 + 1 < len(PIECES):
                        split_rest(j // 2 + 1)
                    if j == len(TILES) - 1:
                        pool.wait_ge(s_z, len(TILES))
                        for v in (*stin, *Ub):
                            last = pool.memset(v, 0.0)
                        last.then_inc(s_zero, 1)
                    m = j - MIX0
                    if m >= 0:
                        if m:
                            pool.wait_ge(s_mix, m)
                        pool.wait_ge(s_raw, m + 1)
                        pool.tensor_tensor(nsum[:, 1:W - 1], raw[:, m % 2, 0:W - 2], raw[:, m % 2, 2:W], ALU.add).then_inc(s_sum, 1)
                for v in (*SU, ls, keep):
                    pool.memset(v, 1.0 if v is keep else 0.0)
                link(pool.memset(hT[:, 0:POOL_CLEARS, :], 0.0))
                pool.memset(keep.rearrange("p (n c) -> p n c", c=C)[:, :, 0:1], 0.0)

            @block.scalar
            def _(act):
                xs = x_sample[0].rearrange("(i p) d -> p i d", p=P)
                act.dma_start(xtok[:, 0, :], x_prompt[0]).then_inc(s_x[0], 16)
                act.dma_start(xtok[:, 1:5, :], xs[:, 0:4, :]).then_inc(s_x[1], 16)
                act.dma_start(xtok[:, 5:9, :], xs[:, 4:8, :]).then_inc(s_x[2], 16)
                act.dma_start(w2s[:, :], w2.rearrange("a n r d -> (a n r) d")).then_inc(s_w2, 16)
                act.dma_start(a2s[:, :], a2.rearrange("a n r d -> (a n r) d")).then_inc(s_w2, 16)
                act.wait_ge(s_vc, 1)
                act.activation(small[:, 18:34], vec[:, 0:16], ACT.Tanh, scale=0.5).then_inc(s_tm, 1)
                for i in range(9):
                    if i in (0, 1, 5):
                        act.wait_ge(s_x[(0, 1, 5).index(i)], 16)
                    if i:
                        act.wait_ge(s_ss, i)
                    act.activation(junk, xtok[:, i, :], ACT.Square, accum_out=ss[:, i:i + 1]).then_inc(s_ss, 1)
                act.wait_ge(s_ms, 1)
                act.activation(ss, ss, ACT.Sqrt).then_inc(s_sd, 1)
                act.wait_ge(s_sc, 1)
                def round_weights(p):
                    n = LOADS.index(("z", p))
                    act.wait_ge(s_wl[n % RING], 16 * (n // RING + 1))
                    if p >= 2:
                        act.wait_ge(s_z, 2 * (p - 1))
                    act.activation(w_round[:, p % 2, :], ring[:, n % RING, :], ACT.Copy).then_inc(s_wh, 1)

                for n in range(len(HT_BANKS)):
                    if n == KT:
                        round_weights(0)
                    k, at, w, _, s = HT_BANKS[n]
                    act.wait_ge(s_xt, n + 1)
                    act.activation(hi_of_h[:, k, at:at + w], ps[:, n % 8, 0:w], ACT.Identity,
                                   bias=shf[:, k, s:s + 1], scale=scl[:, k, s:s + 1]).then_inc(s_ha, 1)

                def kk_norm(a):
                    act.wait_ge(s_mix, 5 + a)
                    act.wait_ge(s_sa, 16)
                    if a:
                        act.wait_ge(s_ks, NB * a)
                    act.activation(zc[:, 17, :], kT[:, a, :], ACT.Square, scale=col("k_k", a)).then_inc(s_kq, 1)
                    r = slice(32 * a, 32 * a + 32)
                    for n in range(NB):
                        act.wait_ge(s_ks, NB * a + n + 1)
                        act.activation(kn[r, n * NC:(n + 1) * NC], ps[r, 6 + n % 2, 0:NC], ACT.Sqrt,
                                       bias=epst[r, 2:3]).then_inc(s_kd, 1)

                def layer_norm():
                    for n in range(NB):
                        cut = slice(n * NC, (n + 1) * NC)
                        act.wait_ge(s_lx, n + 1)
                        act.activation(T[:, 2:4, cut], T[:, 0:2, cut], ACT.Square).then_inc(s_lq, 1)
                        act.wait_ge(s_lv, n + 1)
                        act.activation(raw[:, 0, cut], ps[:, 7, 0:NC], ACT.Sqrt, bias=epst[:, 1:2]).then_inc(s_ls, 1)
                    for g in range(2):
                        act.wait_ge(s_lr, g + 1)
                        act.activation(T[:, 2 + g, :], T[:, g, :], ACT.Tanh, scale=0.5).then_inc(s_lt, 1)

                round_weights(1)
                for j, kind in enumerate(TILES):
                    h, z = j % 2, zbanks(j)
                    i = j - TILES.index(kind)
                    if kind in ("u2", "gb", "ga", "gc", "xa", "mix"):
                        act.wait_ge(s_z, j + 1)
                    if kind == "u2":
                        act.activation(as3(T[:, h, :]), z, ACT.Tanh, scale=0.5).then_inc(s_th, 1)
                    elif kind == "gb":
                        if h == 0:
                            act.wait_ge(s_sg, 32)
                        act.activation(as3(T[:, 6 + h, :]), z, ACT.Tanh, scale=0.5).then_inc(s_th, 1)
                    elif kind == "xa":
                        act.activation(as3(xa[:, h, :]), z, ACT.Copy).then_inc(s_xa, 1)
                    elif kind == "ga":
                        act.activation(as3(xa[:, 2 + h, :]), z, ACT.Tanh, scale=0.5).then_inc(s_th, 1)
                    elif kind == "mix":
                        if i < 2:
                            act.wait_ge(s_ya, i + 1)
                        if i == 4:
                            act.wait_ge(s_yb, 2)
                        if i == 6:
                            act.wait_ge(s_sb, 16)
                        if i >= 2:
                            act.wait_ge(s_sum, i - 1)
                        act.activation(as3(dest(i)), z, ACT.Copy, scale=omu[:, i:i + 1])
                        act.activation(as3(raw[:, i % 2, :]), z, ACT.Copy).then_inc(s_raw, 1)
                    elif kind == "gc":
                        act.activation(as3(T[:, 4 + i, :]), z, ACT.Tanh, scale=0.5).then_inc(s_th, 1)
                    if h and (j + 3) // 2 < len(PIECES):
                        round_weights((j + 3) // 2)
                    if j == MIX0 - 1:
                        layer_norm()
                    if MIX0 + 5 <= j <= MIX0 + 8:
                        kk_norm(j - MIX0 - 5)
                    if j == MIX0 + 13:
                        act.wait_ge(s_mix, 13)
                        act.activation(lwT, lwT, ACT.Tanh).then_inc(s_lwt, 1)
                act.wait_ge(s_zero, 1)
                act.activation(hT[:, POOL_CLEARS:, :], Ub[0][:, 0, 0:1].unsqueeze(2).to_broadcast([P, KT - POOL_CLEARS, W]), ACT.Copy)

            @block.tensor
            def _(pe):
                pe.wait_ge(s_const, 1)
                pe.wait_ge(s_c, 32)
                pe.transpose(ps[:, 5, 0:N_C], va[0:N_C, :], eye[0:N_C, 0:N_C]).then_inc(s_ct, 1)
                pe.wait_ge(s_smod, 1)
                mods = smod[:, :].rearrange("p (s k) -> p k s", k=KT)
                for k in range(KT):
                    pe.wait_ge(s_wl[k % RING], 16 * (k // RING + 1))
                    for b in range(4):
                        last = pe.matmul(ps[0:2, b, :], mods[:, k, :], ring[:, k % RING, 512 * b:512 * b + 512],
                                         start=(k == 0), stop=(k == KT - 1))
                    last.then_inc(s_wu, 1)
                pe.wait_ge(s_vec, 16 * (len(VEC_ROWS) - 1))
                pe.transpose(ps[:, 6, 0:N_VEC], va[0:N_VEC, :], eye[0:N_VEC, 0:N_VEC]).then_inc(s_vt, 1)
                pe.transpose(ps[:, 7, 0:N_CB], vb[0:N_CB, :], eye[0:N_CB, 0:N_CB]).then_inc(s_vt, 1)
                pe.wait_ge(s_row, 1)
                for m in range(16):
                    last = pe.transpose(ps[:, 4, 2 * m:2 * m + 2], row[:, P * m:P * m + P], eye[0:2, 0:2])
                last.then_inc(s_at, 1)
                pe.wait_ge(s_xn, 9)
                for n, (k, at, w, i0, _) in enumerate(HT_BANKS):
                    if n == 4:
                        pe.wait_ge(s_sc, 1)
                    if n >= 8:
                        pe.wait_ge(s_hf, n - 7)
                    for i in range(w // P):
                        last = pe.transpose(ps[:, n % 8, P * i:P * i + P], xtok[:, i0 + i, P * k:P * k + P], eye[:, :])
                    last.then_inc(s_xt, 1)

                def layer_norm(step):
                    if step < NB:
                        n = step
                        cut = slice(n * NC, (n + 1) * NC)
                        if n == 0:
                            pe.wait_ge(s_cv, 2)
                        else:
                            pe.wait_ge(s_lx, n)
                        pe.matmul(ps[:, 6, 0:NC], ones[:, :], T[:, 4, cut], start=True, stop=False)
                        pe.matmul(ps[:, 6, 0:NC], ones[:, :], T[:, 5, cut], start=False, stop=True).then_inc(s_lm, 1)
                    if step > 0:
                        n = step - 1
                        cut = slice(n * NC, (n + 1) * NC)
                        pe.wait_ge(s_lq, n + 1)
                        if n:
                            pe.wait_ge(s_ls, n)
                        pe.matmul(ps[:, 7, 0:NC], ones[:, :], T[:, 2, cut], start=True, stop=False)
                        pe.matmul(ps[:, 7, 0:NC], ones[:, :], T[:, 3, cut], start=False, stop=True).then_inc(s_lv, 1)

                def kk_norm(a):
                    pe.wait_ge(s_kq, a + 1)
                    for n in range(NB):
                        if n == 2:
                            pe.wait_ge(s_kd, NB * a + 1)
                        elif a:
                            pe.wait_ge(s_kd, NB * a)
                        pe.matmul(ps[32 * a:32 * a + 32, 6 + n % 2, 0:NC], heads[:, 48:80], zc[:, 17, n * NC:(n + 1) * NC],
                                  start=True, stop=True).then_inc(s_ks, 1)

                pe.wait_ge(s_const, 2)
                pe.wait_ge(s_w2, 32)
                for j in range(len(TILES)):
                    p = j // 2
                    cut = slice(P * (j % 2), P * (j % 2) + P)
                    w_hi = w_round[:, p % 2, :].rearrange("p (k n) -> p k n", k=KT)
                    w_lo = w_rest[:, LOADS.index(("z", p)) % RING, :].rearrange("p (k n) -> p k n", k=KT)
                    if j % 2 == 0:
                        pe.wait_ge(s_wh, p + 1)
                        pe.wait_ge(s_wo1, p + 1)
                    if j >= 2:
                        pe.wait_ge(*read_by(j - 2))
                    for b in range(NB):
                        o, cols_b = ps[:, NB * (j % 2) + b, 0:NC], slice(NC * b, NC * (b + 1))
                        if j == 0 and b < 2:
                            pe.wait_ge(s_hf, (2 * KT + 1, len(HT_BANKS))[b])
                            for by in range(2):
                                pe.wait_ge(s_hs[by], rests(by, (2 * KT, len(HT_BANKS))[b]))
                        for k in range(KT):
                            pe.matmul(o, w_hi[:, k, cut], hi_of_h[:, k, cols_b], start=(k == 0), stop=False)
                            pe.matmul(o, w_hi[:, k, cut], lo_of_h[k][:, cols_b], start=False, stop=False)
                            last = pe.matmul(o, w_lo[:, k, cut], hi_of_h[:, k, cols_b], start=False, stop=(k == KT - 1))
                        if b == NB - 1:
                            last.then_inc(s_z, 1)
                        if j == MIX0 or (j == MIX0 + 1 and b == 0):
                            layer_norm(NB * (j - MIX0) + b)
                        if MIX0 + 6 <= j <= MIX0 + 9 and b == 0:
                            kk_norm(j - MIX0 - 6)
                    g = p - GATE_AFTER
                    if j % 2 and 0 <= g < GATES:
                        n = LOADS.index(("gate", g))
                        pe.wait_ge(s_wl[n % RING], 16 * (n // RING + 1))
                        for k in (2 * g, 2 * g + 1):
                            for b in range(2):
                                at = D_MODEL * (k % 2) + 512 * b
                                last = pe.matmul(ps[0:2, 6 + b, :], mods[:, k, :], ring[:, n % RING, at:at + 512],
                                                 start=(k == 0), stop=(k == KT - 1))
                        last.then_inc(s_gu, 1)
                pe.wait_ge(s_kr, 1)
                for a in range(PAIRS):
                    for n in range(NB):
                        at = NB * a + n
                        if at >= 2:
                            pe.wait_ge(s_kn, at - 1)
                        pe.matmul(ps[:, 6 + at % 2, 0:NC], back[:, a, :], kn[:, n * NC:(n + 1) * NC],
                                  start=True, stop=True).then_inc(s_kp, 1)

            @block.vector
            def _(dve):
                n_dve = [0]

                def link(ins):
                    n_dve[0] += 1
                    ins.then_inc(s_dve, 1)
                    dve.wait_ge(s_dve, n_dve[0])

                dve.wait_ge(s_ct, 1)
                dve.tensor_copy(vec[:, 0:N_C], ps[:, 5, 0:N_C]).then_inc(s_vc, 1)
                dve.wait_ge(s_vc, 1)
                dve.wait_ge(s_tm, 1)
                link(dve.scalar_tensor_tensor(out=smod[:, :], in0=small[:, 18:34], scalar=1.0, in1=vec[:, 0:16],
                                              op0=ALU.add, op1=ALU.mult))
                dve.tensor_scalar(smod[:, :], smod[:, :], 0.5, None, ALU.mult).then_inc(s_smod, 1)
                dve.wait_ge(s_ss, 9)
                dve.tensor_scalar(ss, ss, 1.0 / D_MODEL, RMS_EPS, ALU.mult, ALU.add).then_inc(s_ms, 1)
                dve.wait_ge(s_sd, 1)
                link(dve.reciprocal(rs, ss))
                for i in range(9):
                    dve.tensor_scalar(xtok[:, i, :], xtok[:, i, :], rs[:, i:i + 1], None, ALU.mult).then_inc(s_xn, 1)
                dve.wait_ge(s_vt, 1)
                dve.tensor_copy(vec[:, N_C:], ps[:, 6, N_C:N_VEC]).then_inc(s_vc, 1)
                dve.wait_ge(s_vt, 2)
                dve.tensor_scalar(cb[:, :], ps[:, 7, 0:N_CB], 0.5, None, ALU.mult)
                dve.wait_ge(s_vc, 2)
                dve.tensor_scalar(cah[:, :], cols("conv_a"), 0.5, None, ALU.mult)
                dve.tensor_scalar(hmu[:, :], cols("mu"), 0.5, None, ALU.mult)
                dve.tensor_scalar(omu[:, :], cols("mu"), -1.0, 1.0, ALU.mult, ALU.add)
                dve.wait_ge(s_wu, KT)
                dve.wait_ge(s_adab, 96)
                dve.tensor_tensor(row, ps[0:2, 0:4, :].rearrange("p b n -> p (b n)"), adab, ALU.add).then_inc(s_row, 1)
                dve.wait_ge(s_at, 1)
                cols4 = ps[:, 4, 0:32].rearrange("p (m s) -> p m s", s=2)
                dve.tensor_copy(shf[:, :, :], cols4[:, 0:KT, :])
                dve.scalar_tensor_tensor(out=scl[:, :, :], in0=cols4[:, KT:, :], scalar=1.0,
                                         in1=cols("g_pre").unsqueeze(2).to_broadcast([P, KT, 2]),
                                         op0=ALU.add, op1=ALU.mult).then_inc(s_sc, 1)
                dve.wait_ge(s_sc, 1)
                for n in range(len(HT_BANKS)):
                    k, at, w, _, s = HT_BANKS[n]
                    dve.wait_ge(s_ha, n + 1)
                    dve.tensor_scalar(lo_full[k][:, at:at + w], ps[:, n % 8, 0:w], scl[:, k, s:s + 1], shf[:, k, s:s + 1],
                                      ALU.mult, ALU.add).then_inc(s_hf, 1)
                    if REST_BY[n] == 1:
                        dve.wait_ge(s_hf, n + 1)
                        dve.tensor_tensor(lo_of_h[k][:, at:at + w], lo_full[k][:, at:at + w], hi_of_h[:, k, at:at + w].bitcast(F32),
                                          ALU.subtract).then_inc(s_hs[1], 1)

                U1 = TILES.index("u1")
                taps_after = dict(zip(range(U1, MIX0), (5, 6, 6, 6, 7, 7, 3, 3, 6, 6, 4, 3)))
                assert sum(taps_after.values()) == 2 * CONV_B
                taps_done = [0]

                def conv_some(n):
                    for _ in range(n):
                        g, tap = divmod(taps_done[0], CONV_B)
                        if tap == 0:
                            dve.wait_ge(s_glu, g + 1)
                            dve.wait_ge(s_sg, 32)
                        conv_taps(g, tap, tap + 1)
                        taps_done[0] += 1

                def conv_taps(g, first, last):
                    x, o = T[:, 2 + g, :], T[:, 4 + g, :]
                    order = [CONV_B // 2] + [t for t in range(CONV_B) if t != CONV_B // 2]
                    for t in order[first:last]:
                        w = cb[:, 2 * t + g:2 * t + g + 1]
                        off = t - CONV_B // 2
                        if off == 0:
                            link(dve.tensor_scalar(o, x, w, col("conv_b_bias", g), ALU.mult, ALU.add))
                            continue
                        for at, n, step in ((TP, SEQ, 1), (TS, ROWS, GRID_W)):
                            lo, hi = max(0, -off), min(n, n - off)
                            if hi <= lo:
                                continue
                            a, b = at + lo * step, at + hi * step
                            done = dve.scalar_tensor_tensor(out=o[:, a:b], in0=x[:, a + off * step:b + off * step], scalar=w,
                                                            in1=o[:, a:b], op0=ALU.mult, op1=ALU.add)
                        if t == order[-1]:
                            done.then_inc(s_cv, 1)
                        else:
                            link(done)

                def conv_a_half(g):
                    x, o = xa[:, g, :], ya[:, g, :]
                    link(dve.tensor_scalar(o, x, cah[:, 2 + g:3 + g], None, ALU.mult))
                    xg, og = (a[:, TS:TS + DEC_SEQ].rearrange("p (r w) -> p r w", w=GRID_W) for a in (x, o))
                    for t, off in ((0, -1), (2, 1)):
                        w = cah[:, 2 * t + g:2 * t + g + 1]
                        dve.scalar_tensor_tensor(out=o[:, TP:TP + SEQ], in0=x[:, TP + off:TP + SEQ + off], scalar=w,
                                                 in1=o[:, TP:TP + SEQ], op0=ALU.mult, op1=ALU.add)
                        lo, hi = max(0, -off), GRID_W - max(0, off)
                        link(dve.scalar_tensor_tensor(out=og[:, :, lo:hi], in0=xg[:, :, lo + off:hi + off], scalar=w,
                                                      in1=og[:, :, lo:hi], op0=ALU.mult, op1=ALU.add))

                def layer_norm():
                    for n in range(NB):
                        cut = slice(n * NC, (n + 1) * NC)
                        dve.wait_ge(s_lm, n + 1)
                        dve.tensor_tensor(T[:, 0:2, cut], T[:, 4:6, cut],
                                          ps[:, 6, 0:NC].unsqueeze(1).to_broadcast([P, 2, NC]), ALU.subtract).then_inc(s_lx, 1)
                        dve.wait_ge(s_ls, n + 1)
                        link(dve.reciprocal(raw[:, 0, cut], raw[:, 0, cut]))
                        link(dve.tensor_tensor(T[:, 0:2, cut], T[:, 0:2, cut],
                                               raw[:, 0, cut].unsqueeze(1).to_broadcast([P, 2, NC]), ALU.mult))
                    for g in range(2):
                        dve.tensor_scalar(T[:, g, :], T[:, g, :], col("ln_b_g", g), col("ln_b_b", g),
                                          ALU.mult, ALU.add).then_inc(s_lr, 1)
                    for g in range(2):
                        dve.wait_ge(s_lt, g + 1)
                        link(dve.scalar_tensor_tensor(out=T[:, 2 + g, :], in0=T[:, 2 + g, :], scalar=1.0, in1=T[:, g, :],
                                                      op0=ALU.add, op1=ALU.mult))
                        dve.scalar_tensor_tensor(out=T[:, 6 + g, :], in0=T[:, 2 + g, :], scalar=0.25, in1=T[:, 6 + g, :],
                                                 op0=ALU.mult, op1=ALU.mult).then_inc(s_yb, 1)

                def kk_ready():
                    for at in range(NB * PAIRS):
                        a, cut = at // NB, slice(at % NB * NC, at % NB * NC + NC)
                        dve.wait_ge(s_kp, at + 1)
                        dve.scalar_tensor_tensor(out=kkT[:, a, cut], in0=kT[:, a, cut], scalar=col("k_k", a),
                                                 in1=ps[:, 6 + at % 2, 0:NC], op0=ALU.mult, op1=ALU.mult).then_inc(s_kn, 1)

                for j, kind in enumerate(TILES):
                    h, z = j % 2, zbanks(j)
                    i = j - TILES.index(kind)
                    if j == 2 * (GATE_AFTER + GATES):
                        dve.wait_ge(s_gu, GATES)
                        link(dve.tensor_tensor(grow, ps[0:2, 6:8, :].rearrange("p b n -> p (b n)"), grow, ALU.add))
                        dve.tensor_tensor(grow, grow, gpost, ALU.mult).then_inc(s_gr, 1)
                    if kind in ("u1", "gb", "cg", "bg", "ga", "gc"):
                        dve.wait_ge(s_z, j + 1)
                    if kind == "u1":
                        dve.wait_ge(s_th, 5 + h)
                        dve.scalar_tensor_tensor(out=as3(T[:, 2 + h, :]), in0=as3(T[:, h, :]), scalar=1.0, in1=z,
                                                 op0=ALU.add, op1=ALU.mult).then_inc(s_glu, 1)
                    elif kind == "gb":
                        dve.wait_ge(s_th, 7 + h)
                        dve.scalar_tensor_tensor(out=as3(T[:, 6 + h, :]), in0=as3(T[:, 6 + h, :]), scalar=1.0, in1=z,
                                                 op0=ALU.add, op1=ALU.mult).then_inc(s_gb, 1)
                    elif kind == "cg":
                        dve.wait_ge(s_xa, h + 1)
                        dve.tensor_tensor(as3(xa[:, h, :]), as3(xa[:, h, :]), z, ALU.mult).then_inc(s_cx, 1)
                        dve.wait_ge(s_cx, h + 1)
                        dve.wait_ge(s_gst, 16)
                        conv_a_half(h)
                    elif kind == "bg":
                        dve.tensor_tensor(as3(ya[:, h, :]), as3(ya[:, h, :]), z, ALU.mult).then_inc(s_bg, 1)
                    elif kind == "ga":
                        dve.wait_ge(s_th, 9 + h)
                        link(dve.scalar_tensor_tensor(out=as3(xa[:, 2 + h, :]), in0=as3(xa[:, 2 + h, :]), scalar=1.0, in1=z,
                                                      op0=ALU.add, op1=ALU.mult))
                        dve.wait_ge(s_bg, h + 1)
                        dve.tensor_tensor(ya[:, h, :], ya[:, h, :], xa[:, 2 + h, :], ALU.mult).then_inc(s_ya, 1)
                    elif kind == "mix":
                        if i == MIXES - 1:
                            kk_ready()
                        dve.wait_ge(s_sum, i + 1)
                        o = dest(i)[:, 1:W - 1]
                        dve.scalar_tensor_tensor(out=o, in0=nsum[:, 1:W - 1], scalar=hmu[:, i:i + 1], in1=o,
                                                 op0=ALU.mult, op1=ALU.add).then_inc(s_mix, 1)
                        if i == 11:
                            dve.wait_ge(s_kd, NB * PAIRS)
                            dve.reciprocal(kn, kn).then_inc(s_kr, 1)
                    elif kind == "gc":
                        dve.wait_ge(s_th, i + 1)
                        dve.scalar_tensor_tensor(out=as3(T[:, 4 + i, :]), in0=as3(T[:, 4 + i, :]), scalar=1.0, in1=z,
                                                 op0=ALU.add, op1=ALU.mult).then_inc(s_gc, 1)
                    conv_some(taps_after.get(j, 0))
                    if j == MIX0 - 1:
                        layer_norm()

        assert sems1 == list(range(sems1[0], sems1[0] + len(sems1)))
        nc.all_engine_barrier(sems_to_clear=range(sems1[0], sems1[-1] + 1))
        part1.close()

        s_sc2 = sem("final_state_copied")
        s_st = sem("state_transposed")
        s_ns = sem("new_state_stored")

        lo, hi = slice(0, 64), slice(64, 128)

        def pairs(bank, w):
            return ps[:, bank, 0:PAIRS * w].rearrange("p (a b) -> p a b", a=PAIRS)

        def chunk(tiles, col):
            return tiles[:, :, bass.ds(col, C)]

        def steps(solve, prepare, start=0, stored=None):
            N = len(solve)

            def earlier(e, s, value):
                if value > 0:
                    e.wait_ge(s, value)

            with nc.Block() as block:
                if stored:
                    @block.sync
                    def _(sp):
                        sp.wait_ge(*stored)

                @block.scalar
                def _(act):
                    for t in range(N):
                        so, pr = solve[t], prepare[t]
                        nxt = (start + t + 1) % 2

                        def stage_lora():
                            earlier(act, l_lora, 2 * t)
                            for n, src in enumerate((lwT, laT)):
                                for d in DIRS:
                                    r = slice(64 * d, 64 * d + 64)
                                    act.activation(ls[r, n, r], src[r, bass.ds(pr[d], C)], ACT.Copy).then_inc(l_stage, 1)

                        def v_by_token(d):
                            earlier(act, l_S[d], t)
                            act.wait_ge(l_vt[d], t + 1)
                            vt = ps[:, 6 + d, :].rearrange("p (a h c) -> p a h c", a=PAIRS, h=2)
                            for g, r in ((0, hi), (1, lo)):
                                act.activation(SU[d][r, :, :, g, :],
                                               vt[r, :, g, :].unsqueeze(1).to_broadcast([64, 2, PAIRS, C]),
                                               ACT.Copy).then_inc(l_v[d], 1)

                        def tanh():
                            for n, x in enumerate((xw, av)):
                                act.wait_ge(l_x, 2 * t + n + 1)
                                act.activation(x, x, ACT.Tanh, scale=0.5).then_inc(l_tanh, 1)

                        def sigmoid():
                            act.wait_ge(l_tanh, 2 * t + 2)
                            act.activation(av, av, ACT.Copy, bias=0.5, scale=0.5).then_inc(l_a, 1)

                        def copy_y(d, l):
                            if l < LEVELS - 1:
                                act.wait_ge(l_X[d], 4 * t + l)
                            else:
                                act.wait_ge(l_Q[d], 5 * t + l)
                            act.activation(Y[d], pairs(2 * d + 1, P), ACT.Copy).then_inc(l_Y[d], 1)

                        def keys_by_token(d):
                            for g in range(2):
                                act.wait_ge(l_kt[d], 2 * t + g + 1)
                                act.activation(KB[d][:, :, g, :], pairs((6, 4)[d] + g, P)[:, :, 64 * g:64 * g + 64],
                                               ACT.Copy).then_inc(l_kb[d], 1)

                        def exps():
                            act.wait_ge(l_log, 2 * t + 2)
                            act.activation(eA, LA, ACT.Exp).then_inc(l_exp, 1)
                            act.activation(eB, LB, ACT.Exp).then_inc(l_exp, 1)
                            act.wait_ge(l_exp, 3 * t + 1)
                            act.activation(eN, LA, ACT.Exp, scale=-1.0).then_inc(l_exp, 1)
                            earlier(act, l_st[1], 2 * t)
                            for d in DIRS:
                                end = C - 1 if d == 0 else 0
                                act.activation(dend[:, nxt, d, :], eA[:, :, d, end], ACT.Copy).then_inc(l_end, 1)

                        def negate_rhs(d):
                            act.wait_ge(l_rhs[d], t + 1)
                            act.activation(RH[d], pairs(6 + d, C), ACT.Copy, scale=-1.0).then_inc(l_rh[d], 1)

                        def double_v(d):
                            act.wait_ge((l_kf, l_b)[d], 2 * t + 2)
                            if d == 1:
                                act.wait_ge(l_kf, 2 * t + 2)
                            act.activation(VD[d], chunk(vT, pr[d]).unsqueeze(2).to_broadcast([P, PAIRS, 2, C]),
                                           ACT.Copy).then_inc(l_vd[d], 1)

                        def copy_u(d):
                            act.wait_ge(l_U[d], t + 1)
                            u = pairs(2 * d, C)
                            for g, r in ((0, lo), (1, hi)):
                                act.activation(SU[d][r, 1, :, g, :], u[r], ACT.Copy).then_inc(l_uc[d], 1)

                        if pr:
                            stage_lora()
                        if so:
                            v_by_token(0)
                        if pr:
                            tanh()
                        if so:
                            v_by_token(1)
                            copy_y(0, 1)
                        if pr:
                            sigmoid()
                        if so:
                            copy_y(1, 1)
                            keys_by_token(0)
                            copy_y(0, 2)
                        if pr:
                            exps()
                        if so:
                            copy_y(1, 2)
                            keys_by_token(1)
                            copy_y(0, 3)
                            negate_rhs(0)
                            negate_rhs(1)
                            copy_y(1, 3)
                        if pr:
                            double_v(0)
                            double_v(1)
                        if so:
                            copy_y(0, 4)
                            copy_y(1, 4)
                            copy_y(0, 5)
                            copy_u(0)
                            copy_y(1, 5)
                            copy_u(1)

                @block.tensor
                def _(pe):
                    for t in range(N):
                        so, pr = solve[t], prepare[t]
                        now, nxt = (start + t) % 2, (start + t + 1) % 2

                        def level_product(d, l):
                            if l == 1:
                                earlier(pe, l_um0[d], 2 * t)
                                earlier(pe, l_X0[d], t)
                                earlier(pe, l_uc[d], 2 * t)
                            else:
                                pe.wait_ge(l_um[d], 4 * t + l - 1)
                                pe.wait_ge(l_X[d], 4 * t + l - 1)
                            for a in range(PAIRS):
                                last = pe.matmul(pairs(2 * d, P)[:, a, :], Um[d][:, a, :], X[d][:, a, :], start=True, stop=True)
                            last.then_inc(l_P[d], 1)

                        def level_update(d, l):
                            pe.wait_ge(l_pc[d], 5 * t + l)
                            if l == 1:
                                earlier(pe, l_st[d], 2 * t)
                            else:
                                pe.wait_ge(l_Y[d], 5 * t + l - 1)
                            for a in range(PAIRS):
                                last = pe.matmul(pairs(2 * d + 1, P)[:, a, :], PX[d][:, a, :], Y[d][:, a, :], start=True, stop=True)
                            last.then_inc(l_Q[d], 1)

                        def transpose_v():
                            for d in DIRS:
                                earlier(pe, l_vd[d], t)
                                earlier(pe, l_g[1], t)
                                for a in range(PAIRS):
                                    last = pe.transpose(pairs(6 + d, P)[:, a, :], VD[d][:, a].rearrange("p b c -> p (b c)"), eye[:, :])
                                last.then_inc(l_vt[d], 1)

                        def lora():
                            earlier(pe, l_g[0], t)
                            for n, w in enumerate((w2s, a2s)):
                                pe.wait_ge(l_stage, 4 * t + 2 * n + 2)
                                for a in range(PAIRS):
                                    last = pe.matmul(pairs(4 + n, P)[:, a, :], w[:, P * a:P * a + P], ls[:, n, :],
                                                     start=True, stop=True)
                                last.then_inc(l_lora, 1)

                        def transpose_keys(d):
                            if d == 0:
                                pe.wait_ge(l_v[0], 2 * t + 2)
                                pe.wait_ge(l_v[1], 2 * t + 2)
                            elif pr:
                                pe.wait_ge(l_x, 2 * t + 2)
                            for g in range(2):
                                for a in range(PAIRS):
                                    last = pe.transpose(pairs((6, 4)[d] + g, P)[:, a, :],
                                                        GL[d][:, a, g:g + 2, :].rearrange("p b c -> p (b c)"), eye[:, :])
                                last.then_inc(l_kt[d], 1)

                        def rhs():
                            pe.wait_ge(l_kb[0], 2 * t + 2)
                            for d in DIRS:
                                earlier(pe, l_st[d], 2 * t)
                                for a in range(PAIRS):
                                    for g in range(2):
                                        last = pe.matmul(pairs(6 + d, C)[64 * g:64 * g + 64, a, :], GR[now][d][:, a, 3 * g, :],
                                                         SU[d][:, 0, a, g, :], start=True, stop=True)
                                last.then_inc(l_rhs[d], 1)

                        def gram(d):
                            pe.wait_ge(l_ops[d], t + 1)
                            if so and d == 0:
                                pe.wait_ge(l_kb[1], 2 * t + 2)
                            if so and d == 1:
                                pe.wait_ge(l_rh[0], t + 1)
                                pe.wait_ge(l_rh[1], t + 1)
                            for g in range(2):
                                r = slice(64 * g, 64 * g + 64)
                                for a in range(PAIRS):
                                    last = pe.matmul(pairs(4 + 2 * d + g, P)[:, a, :], GL[d][r, a, g:g + 2, :],
                                                     GR[nxt][d][r, a, 2 * g:2 * g + 2, :], start=True, stop=True)
                                last.then_inc(l_gram[d], 1)

                        def solve_u(d):
                            pe.wait_ge(l_Y[d], 5 * t + 5)
                            pe.wait_ge(l_rh[d], t + 1)
                            for a in range(PAIRS):
                                last = pe.matmul(pairs(2 * d, C)[:, a, :], Y[d][:, a, :], RH[d][:, a, :],
                                                 start=True, stop=True)
                            last.then_inc(l_U[d], 1)

                        def outputs(d):
                            pe.wait_ge(l_kb[d], 2 * t + 2)
                            pe.wait_ge(l_uc[d], 2 * t + 2)
                            for a in range(PAIRS):
                                for g in range(2):
                                    r = slice(64 * g, 64 * g + 64)
                                    o = pairs(2 * d + 1, C)[r, a, :]
                                    pe.matmul(o, SU[d][:, 0, a, g, :], GR[now][d][:, a, 1 + g, :], start=True, stop=False)
                                    pe.matmul(o, SU[d][r, 1, a, g, :], AB[now][d][r, a, :], start=False, stop=True)
                            for a in range(PAIRS):
                                for g in range(2):
                                    last = pe.matmul(ps[64 * g:64 * g + 64, 2 * d + 1, 256 + C * a:256 + C * a + C],
                                                     KB[d][:, a, g, :], SU[d][:, 1, a, g, :], start=True, stop=True)
                            last.then_inc(l_S[d], 1)

                        if so:
                            level_product(0, 1)
                            transpose_v()
                        if pr:
                            lora()
                        if so:
                            level_update(0, 1)
                            level_product(1, 1)
                            level_product(0, 2)
                            level_update(1, 1)
                            transpose_keys(0)
                            level_update(0, 2)
                            level_product(1, 2)
                            transpose_keys(1)
                            level_product(0, 3)
                            level_update(1, 2)
                            rhs()
                            level_update(0, 3)
                            level_product(1, 3)
                            level_product(0, 4)
                            level_update(1, 3)
                        if pr:
                            gram(0)
                        if so:
                            level_update(0, 4)
                            level_product(1, 4)
                            level_product(0, 5)
                            level_update(1, 4)
                        if pr:
                            gram(1)
                        if so:
                            level_update(0, 5)
                            level_product(1, 5)
                            solve_u(0)
                            level_update(1, 5)
                            outputs(0)
                            solve_u(1)
                            outputs(1)

                @block.gpsimd
                def _(pool):
                    n_pool = [0]

                    def link(ins):
                        n_pool[0] += 1
                        ins.then_inc(l_pool, 1)
                        pool.wait_ge(l_pool, n_pool[0])

                    def mask_level(d, l):
                        return pool.tensor_tensor(Um[d], Ub[d], lvl[:, l, :].unsqueeze(1).to_broadcast([P, PAIRS, P]), ALU.mult)

                    for t in range(N):
                        so, pr = solve[t], prepare[t]

                        def next_level(d, l):
                            pool.wait_ge(l_P[d], 5 * t + l - 1)
                            mask_level(d, l).then_inc(l_um[d], 1)

                        def b_keys(d):
                            if so:
                                pool.wait_ge(l_kt[d], 2 * t + 2)
                            pool.wait_ge(l_a, t + 1)
                            pool.tensor_tensor(GL[d][:, :, 0, :], chunk(kkT, pr[d]), av[:, :, d], ALU.mult).then_inc(l_b, 1)

                        def bonus_keys(d):
                            pool.wait_ge(l_kd, 2 * t + d + 1)
                            link(pool.tensor_tensor(kd[:, d], kd[:, d], chunk(rT, pr[d]), ALU.mult))
                            pool.tensor_tensor(chunk(q, pr[d]), chunk(q, pr[d]), kd[:, d], ALU.add).then_inc(l_q, 1)
                            pool.wait_ge(l_q, 2 * t + d + 1)

                        if so:
                            for l in (2, 3):
                                for d in DIRS:
                                    next_level(d, l)
                        if pr:
                            b_keys(0)
                            b_keys(1)
                        if so:
                            for l in (4, 5):
                                for d in DIRS:
                                    next_level(d, l)
                        if pr:
                            bonus_keys(0)
                            bonus_keys(1)
                            for d in DIRS:
                                if so:
                                    pool.wait_ge(l_P[d], 5 * t + 5)
                                pool.wait_ge(l_u[d], 2 * t + 2)
                                mask_level(d, 0).then_inc(l_um0[d], 1)
                            for d in DIRS:
                                pool.wait_ge(l_Y0[d], t + 1)
                                mask_level(d, 1).then_inc(l_um0[d], 1)

                @block.vector
                def _(dve):
                    n_dve = [0]

                    def link(ins):
                        n_dve[0] += 1
                        ins.then_inc(l_dve, 1)
                        dve.wait_ge(l_dve, n_dve[0])

                    def wide(name):
                        return cols(name).rearrange("p (d a) -> p a d", d=2).unsqueeze(3).to_broadcast([P, PAIRS, 2, C])

                    def mask(d, r, slots):
                        return tri[r, d, slots, :].unsqueeze(1).to_broadcast([64, PAIRS, slots.stop - slots.start, C])

                    eyes = eye[:, :].unsqueeze(1).to_broadcast([P, PAIRS, P])
                    for t in range(N):
                        so, pr = solve[t], prepare[t]
                        now, nxt = (start + t) % 2, (start + t + 1) % 2

                        def transpose_x(d, l):
                            dve.wait_ge(l_Q[d], 5 * t + l)
                            dve.transpose(X[d], pairs(2 * d + 1, P)).then_inc(l_X[d], 1)

                        def add_bias():
                            for n, (x, bias) in enumerate(((xw, "w0"), (av, "a0"))):
                                dve.wait_ge(l_lora, 2 * t + n + 1)
                                if so:
                                    dve.wait_ge(l_vt[n], t + 1)
                                dve.tensor_tensor(x, ps[:, 4 + n, :].rearrange("p (a d c) -> p a d c", a=PAIRS, d=2),
                                                  wide(bias), ALU.add).then_inc(l_x, 1)

                        def log_decays():
                            dve.wait_ge(l_tanh, 2 * t + 1)
                            link(dve.tensor_scalar(xw, xw, -E_HALF / 2, -E_HALF / 2, ALU.mult, ALU.add))
                            link(dve.tensor_tensor_scan(LA.rearrange("p a d c -> p (a d c)"), keep,
                                                        xw.rearrange("p a d c -> p (a d c)"), 0.0, ALU.mult, ALU.add))

                        def split_decays():
                            dve.tensor_tensor(LB[:, :, 0], LA[:, :, 0], xw[:, :, 0], ALU.subtract)
                            link(dve.tensor_tensor(LB[:, :, 1], LA[:, :, 1, C - 1:C].to_broadcast([P, PAIRS, C]),
                                                   LA[:, :, 1], ALU.subtract))
                            dve.tensor_tensor(LA[:, :, 1], LB[:, :, 1], xw[:, :, 1], ALU.add).then_inc(l_log, 2)
                            dve.wait_ge(l_log, 2 * t + 2)

                        def keys():
                            dve.wait_ge(l_a, t + 1)
                            m1, a2d = (v.rearrange("p a d c -> p a (d c)") for v in (xw, av))
                            link(dve.scalar_tensor_tensor(out=m1, in0=a2d, scalar=-1.0,
                                                          in1=cols("k_a").unsqueeze(2).to_broadcast([P, PAIRS, P]),
                                                          op0=ALU.add, op1=ALU.mult))
                            earlier(dve, l_q, 2 * t)
                            for d in DIRS:
                                dve.scalar_tensor_tensor(out=kd[:, d], in0=xw[:, :, d], scalar=1.0, in1=chunk(kT, pr[d]),
                                                         op0=ALU.add, op1=ALU.mult).then_inc(l_kf, 1)

                        def queries(d):
                            kk2 = chunk(kkT, pr[d]).unsqueeze(2).to_broadcast([P, PAIRS, 2, C])
                            r2 = chunk(rT, pr[d]).unsqueeze(2).to_broadcast([P, PAIRS, 2, C])
                            earlier(dve, l_S[d], t)
                            dve.wait_ge(l_exp, 3 * t + 3)
                            dve.tensor_tensor(GR[nxt][d][:, :, 0:4:3, :], kk2,
                                              eB[:, :, d].unsqueeze(2).to_broadcast([P, PAIRS, 2, C]), ALU.mult)
                            dve.tensor_tensor(GR[nxt][d][:, :, 1:3, :], r2,
                                              eA[:, :, d].unsqueeze(2).to_broadcast([P, PAIRS, 2, C]), ALU.mult)

                        def keys_over_decay(d):
                            dve.wait_ge(l_kf, 2 * t + 2)
                            dve.tensor_tensor(GL[d][:, :, 1, :], kd[:, d], eN[:, :, d], ALU.mult).then_inc(l_kd, 1)
                            dve.wait_ge(l_b, 2 * t + 2)
                            dve.tensor_tensor(GL[d][:, :, 2, :], GL[d][:, :, 0, :], eN[:, :, d], ALU.mult)
                            dve.tensor_tensor(GL[d][:, :, 0, :], GL[d][:, :, 0, :], eN[:, :, d], ALU.mult).then_inc(l_ops[d], 1)

                        def masks(d):
                            ga, gb = (ps[:, 4 + 2 * d + g, :].rearrange("p (a s c) -> p a s c", a=PAIRS, s=2) for g in range(2))
                            if so:
                                dve.wait_ge(l_um[d], 4 * t + 4)
                            dve.wait_ge(l_gram[d], 2 * t + 1)
                            dve.tensor_tensor(Ub[d][lo, :, 0:64], ga[lo, :, 0], mask(d, lo, slice(0, 1))[:, :, 0], ALU.mult).then_inc(l_u[d], 1)
                            dve.wait_ge(l_gram[d], 2 * t + 2)
                            dve.tensor_tensor(Ub[d][hi, :, 64:128], gb[hi, :, 1], mask(d, hi, slice(0, 1))[:, :, 0], ALU.mult).then_inc(l_u[d], 1)
                            dve.tensor_tensor(GR[nxt][d][hi, :, 0:2, :], ga[hi], mask(d, hi, slice(0, 2)), ALU.mult)
                            dve.tensor_tensor(GR[nxt][d][lo, :, 2:4, :], gb[lo], mask(d, lo, slice(1, 3)), ALU.mult)
                            dve.tensor_tensor(AB[nxt][d][lo], ga[lo, :, 1], mask(d, lo, slice(1, 2))[:, :, 0], ALU.mult)
                            dve.tensor_tensor(AB[nxt][d][hi], gb[hi, :, 0], mask(d, hi, slice(1, 2))[:, :, 0], ALU.mult).then_inc(l_g[d], 1)

                        def factor(d, l):
                            dve.wait_ge(l_P[d], 5 * t + l)
                            dve.tensor_tensor(PX[d], eyes, pairs(2 * d, P), ALU.subtract).then_inc(l_pc[d], 1)

                        if so:
                            factor(0, 1)
                        if pr:
                            add_bias()
                        if so:
                            transpose_x(0, 1)
                            factor(1, 1)
                        if pr:
                            log_decays()
                        if so:
                            factor(0, 2)
                            transpose_x(1, 1)
                        if pr:
                            split_decays()
                        if so:
                            transpose_x(0, 2)
                            factor(1, 2)
                        if pr:
                            keys()
                        if so:
                            factor(0, 3)
                            transpose_x(1, 2)
                        if pr:
                            queries(0)
                        if so:
                            transpose_x(0, 3)
                            factor(1, 3)
                        if pr:
                            keys_over_decay(0)
                        if so:
                            factor(0, 4)
                            transpose_x(1, 3)
                        if pr:
                            queries(1)
                        if so:
                            transpose_x(0, 4)
                            factor(1, 4)
                        if pr:
                            keys_over_decay(1)
                        if so:
                            factor(0, 5)
                            transpose_x(1, 4)
                        if pr:
                            masks(0)
                        if so:
                            factor(1, 5)
                        if pr:
                            masks(1)
                            for d in DIRS:
                                dve.wait_ge(l_um0[d], 2 * t + 1)
                                if so:
                                    dve.wait_ge(l_U[d], t + 1)
                                dve.tensor_tensor(Y[d], eyes, Um[d], ALU.subtract).then_inc(l_Y0[d], 1)
                                dve.wait_ge(l_Y0[d], t + 1)
                                dve.transpose(X[d], Y[d]).then_inc(l_X0[d], 1)
                        if so:
                            for d in DIRS:
                                dve.wait_ge(l_S[d], t + 1)
                                yc = chunk(y, so[d])
                                link(dve.tensor_tensor(yc, yc, pairs(2 * d + 1, C), ALU.add))
                                s = ps[:, 2 * d + 1, 256:512].rearrange("p (a c) -> p a c", a=PAIRS)
                                for g, r in ((0, lo), (1, hi)):
                                    dve.tensor_tensor(SU[d][r, 0, :, g, :], SU[d][r, 0, :, g, :], s[r], ALU.add).then_inc(l_sum, 1)
                                dve.wait_ge(l_sum, 4 * t + 2 * d + 2)
                                for g, r in ((0, lo), (1, hi)):
                                    dve.tensor_tensor(SU[d][r, 0, :, g, :], SU[d][r, 0, :, g, :],
                                                      dend[r, now, d, :].unsqueeze(2).to_broadcast([64, PAIRS, C]),
                                                      ALU.mult).then_inc(l_st[d], 1)
            nc.all_engine_barrier(sems_to_clear=range(nums[0], nums[-1] + 1))

        def first_columns(base, chunks, i):
            return base + C * i, base + C * (chunks - 1) - C * i

        PC, SC = SEQ // C, DEC_SEQ // C
        prompt = [first_columns(TP, PC, i) for i in range(PC)]
        steps([None], [prompt[0]], start=1)
        steps(prompt, prompt[1:] + [first_columns(TS, SC, 0)])

        state_out = new_state[0, 0].rearrange("d (a g) v k -> d g v a k", g=2)
        with nc.Block() as block:
            @block.sync
            def _(sp):
                for d in DIRS:
                    sp.wait_ge(s_sc2, d + 1)
                    for g in range(2):
                        r = slice(64 * g, 64 * g + 64)
                        sp.dma_start(state_out[d, g], sout[d][r, :, r]).then_inc(s_ns, 16)

            @block.tensor
            def _(pe):
                pe.wait_ge(s_sl, 64)
                for d in DIRS:
                    for a in range(PAIRS):
                        last = pe.transpose(pairs(2 * d, P)[:, a, :], stin[d][:, P * a:P * a + P], eye[:, :])
                    for a in range(PAIRS):
                        last = pe.transpose(pairs(2 * d + 1, P)[:, a, :], SU[d][:, 0, a].rearrange("p b c -> p (b c)"), eye[:, :])
                    last.then_inc(s_st, 1)

            @block.scalar
            def _(act):
                for d in DIRS:
                    act.wait_ge(s_st, d + 1)
                    act.activation(sout[d], pairs(2 * d + 1, P), ACT.Copy).then_inc(s_sc2, 1)

            @block.vector
            def _(dve):
                for d in DIRS:
                    dve.wait_ge(s_st, d + 1)
                    dve.tensor_copy(SU[d][:, 0].rearrange("p a b c -> p a (b c)"), pairs(2 * d, P))

        loops = (SC - 1) // UNROLL
        with nc.Fori(0, loops) as i:
            at = [first_columns(TS, SC, UNROLL * i + n) for n in range(UNROLL + 1)]
            steps(at[:-1], at[1:])
        last = [first_columns(TS, SC, n) for n in range(UNROLL * loops, SC)]
        steps(last, last[1:] + [None], stored=(s_ns, 64))

        BLOCK_ENDS = (0, TS + 2 * P, TS + 5 * P, W)
        BLOCK_W = max(b - a for a, b in zip(BLOCK_ENDS, BLOCK_ENDS[1:]))
        take = carve()
        take(8 * D_MODEL - 2 * W)
        gt = take(4, W)
        sq = take(2, BLOCK_W)
        sd = take(BLOCK_W)
        back = take(4, P)
        XO = 3
        xr = take(XO, D_MODEL)
        gout = take(2, D_MODEL)
        gg = take(2, D_MODEL)
        yab = kkT
        wo = zflat[:, 4 * W:4 * W + 8 * D_MODEL].rearrange("p (k n) -> p k n", k=8)
        wo_hi = rounded("w_out_rounded", zc_at + 4 * 16 * W, 8, D_MODEL)
        wo_lo = rounded("w_out_rest", zc_at + 4 * 4 * W, 8, D_MODEL)
        y_hi = rounded("yc_rounded", hT_at + 4 * 4 * W, 4, W)
        y_lo = rounded("yc_rest", hT_at, 4, W)
        yab_hi = rounded("branches_rounded", zc_at, 4, W)
        yab_lo = rounded("branches_rest", zc_at + 4 * 12 * W, 4, W)
        WO_PARTS = 4
        WO_ORDER = (2, 3, 0, 1)
        REST_OF_WO_BY = (0, 1, 1, 1)
        ss2, rs2 = small[:, 0:9], small[:, 9:18]
        CUTS = [slice(a, b) for a, b in zip(BLOCK_ENDS, BLOCK_ENDS[1:])]
        BLOCKS = [(a, cut) for cut in CUTS for a in range(4)]
        first_col = [TP if i == 0 else TS + P * (i - 1) for i in range(9)]
        needs = [4 * (i // 3 + 1) for i in range(9)]

        s_gl = [sem(f"gate_c_landed_{b}") for b in range(NB)]
        s_wo = [sem(f"w_out_landed_{c}") for c in range(WO_PARTS)]
        f_wh = sem("w_out_rounded")
        f_wr = [sem("w_out_rest_by_pool"), sem("w_out_rest_by_dve")]
        f_ah = sem("branches_rounded")
        f_al = sem("branches_rest_ready")
        f_yh = sem("yc_rounded")
        f_yl = sem("yc_rest_ready")
        s_ab = sem("branches_landed")
        s_gg = sem("gate_rows_landed")
        f_dve = sem("final_dve_chain")
        f_pm = sem("gn_mean_summed")
        f_xc = sem("gn_centred")
        f_sq = sem("gn_squared")
        f_pv = sem("gn_variance_summed")
        f_sd = sem("gn_deviation_ready")
        f_rs = sem("gn_deviation_inverted")
        f_bk = sem("spread_matrix_built")
        f_pr = sem("gn_deviation_spread")
        f_n = sem("gn_normalised")
        f_af = sem("gn_scaled")
        f_bo = sem("gn_bonus_added")
        f_yc = sem("yc_ready")
        f_bq = sem("bonus_scaled")
        f_pb = sem("bonus_summed")
        f_bd = sem("bonus_ready")
        s_xr = [sem(f"residual_landed_{i}") for i in range(XO)]
        s_o = sem("output_multiplied")
        s_oq = sem("output_squared")
        s_os = sem("output_deviation_ready")
        s_og = sem("output_gated")
        s_or = sem("output_ready")
        s_st2 = [sem(f"output_stored_{i}") for i in range(XO)]

        def width(cut):
            return cut.stop - cut.start

        def wo_part(c):
            return slice(2 * WO_ORDER[c], 2 * WO_ORDER[c] + 2)

        def rest_of_w_out(e, c):
            part = wo_part(c)
            e.wait_ge(f_wh, c + 1)
            e.tensor_tensor(wo_lo[:, part, :], wo[:, part, :], wo_hi[:, part, :].bitcast(F32),
                            ALU.subtract).then_inc(f_wr[REST_OF_WO_BY[c]], 1)

        with nc.Block() as block:
            @block.sync
            def _(sp):
                def store(i):
                    sp.wait_ge(s_or, i + 1)
                    sp.dma_start(y_prompt[0] if i == 0 else y_sample[0, P * (i - 1):P * i, :],
                                 xr[:, i % XO, :]).then_inc(s_st2[i % XO], 16)

                def load_gate(b):
                    cut = CUTS[b]
                    sp.dma_start(gt[:, :, cut], mix_dram[4:8, :, cut].rearrange("m p w -> p m w")).then_inc(s_gl[b], 16)

                for c in range(WO_PARTS):
                    at = 2 * P * WO_ORDER[c]
                    sp.dma_start(wo[:, wo_part(c), :],
                                 w_out[0, at:at + 2 * P, :].rearrange("(k p) n -> p k n", p=P)).then_inc(s_wo[c], 16)
                load_gate(0)
                sp.dma_start(yab, mix_dram[0:4].rearrange("m p w -> p m w")).then_inc(s_ab, 16)
                load_gate(1)
                load_gate(2)
                sp.dma_start(gg, gate_dram[:, :].unsqueeze(0).to_broadcast([P, 2, D_MODEL])).then_inc(s_gg, 16)
                for i in range(9):
                    if i >= XO:
                        sp.wait_ge(s_st2[i % XO], 16 * (i // XO))
                    sp.dma_start(xr[:, i % XO, :], x_prompt[0] if i == 0 else x_sample[0, P * (i - 1):P * i, :]).then_inc(s_xr[i % XO], 16)
                    if i >= XO - 1:
                        store(i - XO + 1)
                for i in range(9 - XO + 1, 9):
                    store(i)
                for i in range(XO):
                    sp.wait_ge(s_st2[i], 16 * 3)

            @block.tensor
            def _(pe):
                def mean_and_bonus(n):
                    a, cut = BLOCKS[n]
                    if n:
                        pe.wait_ge(f_xc, n)
                    if n and a == 0:
                        pe.wait_ge(f_n, n)
                    pe.matmul(ps[:, 4, 0:width(cut)], heads[:, :], y[:, a, cut], start=True, stop=True).then_inc(f_pm, 1)
                    pe.wait_ge(f_bq, n + 1)
                    if n:
                        pe.wait_ge(f_bd, n)
                    pe.matmul(ps[:, 5, 0:width(cut)], heads[:, :], q[:, a, cut], start=True, stop=True).then_inc(f_pb, 1)

                def variance(n):
                    a, cut = BLOCKS[n]
                    pe.wait_ge(f_sq, n + 1)
                    if a == 0 and n:
                        pe.wait_ge(f_sd, n // 4)
                    pe.matmul(ps[32 * a:32 * a + 32, 6, 0:width(cut)], heads[:, 48:80], sq[:, n % 2, 0:width(cut)],
                              start=True, stop=True).then_inc(f_pv, 1)

                def spread(n):
                    a, cut = BLOCKS[n]
                    pe.wait_ge(f_bk, 2)
                    pe.wait_ge(f_rs, n // 4 + 1)
                    if a >= 2:
                        pe.wait_ge(f_n, n - 1)
                    elif a == 1:
                        pe.wait_ge(f_xc, n + 3)
                    elif n:
                        pe.wait_ge(f_n, n)
                    pe.matmul(ps[:, (7, 4)[a % 2], 0:width(cut)], back[:, a, :], sd[:, 0:width(cut)], start=True, stop=True).then_inc(f_pr, 1)

                def statistics(b):
                    for n in range(4 * b, 4 * b + 4):
                        mean_and_bonus(n)
                        if n > 4 * b:
                            variance(n - 1)
                    variance(4 * b + 3)

                def spreads(b):
                    for n in range(4 * b, 4 * b + 4):
                        spread(n)

                def output(i):
                    pe.wait_ge(f_yl, needs[i])
                    at = first_col[i]
                    if i >= 2:
                        pe.wait_ge(s_og, i - 1)
                    for n in range(8):
                        k = 2 * WO_ORDER[n // 2] + n % 2
                        if i == 0 and n % 2 == 0:
                            by = REST_OF_WO_BY[n // 2]
                            pe.wait_ge(f_wr[by], REST_OF_WO_BY[:n // 2 + 1].count(by))
                        if n == 4:
                            pe.wait_ge(f_al, needs[i] // 4)
                        hi, rest = (yab_hi, yab_lo) if k < 4 else (y_hi, y_lo)
                        hi, rest = (v[:, k % 4, at:at + P] for v in (hi, rest))
                        for b in range(2):
                            o, cut = ps[:, 2 * (i % 2) + b, :], slice(512 * b, 512 * b + 512)
                            pe.matmul(o, hi, wo_hi[:, k, cut], start=(n == 0), stop=False)
                            pe.matmul(o, hi, wo_lo[:, k, cut], start=False, stop=False)
                            last = pe.matmul(o, rest, wo_hi[:, k, cut], start=False, stop=(n == 7))
                    last.then_inc(s_o, 1)

                statistics(0)
                spreads(0)
                output(0)
                statistics(1)
                output(1)
                spreads(1)
                output(2)
                statistics(2)
                output(3)
                spreads(2)
                for i in range(4, 9):
                    output(i)

            @block.scalar
            def _(act):
                def bonus_keys(n):
                    a, cut = BLOCKS[n]
                    act.activation(q[:, a, cut], q[:, a, cut], ACT.Copy, scale=col("r_k", a)).then_inc(f_bq, 1)

                def deviation(b):
                    act.wait_ge(f_pv, 4 * b + 4)
                    if b:
                        act.wait_ge(f_pr, 4 * b)
                    n = width(CUTS[b])
                    act.activation(sd[:, 0:n], ps[:, 6, 0:n], ACT.Sqrt, bias=epst[:, 3:4], scale=1.0 / HEAD).then_inc(f_sd, 1)

                def affine(n):
                    a, cut = BLOCKS[n]
                    act.wait_ge(f_n, n + 1)
                    act.activation(y[:, a, cut], y[:, a, cut], ACT.Identity, bias=col("gn_b", a), scale=col("gn_g", a)).then_inc(f_af, 1)

                def mean_square(i):
                    b = 2 * (i % 2)
                    act.wait_ge(s_o, i + 1)
                    if i >= 2:
                        act.wait_ge(s_or, i - 1)
                    act.activation(gout[:, i % 2, :], ps[:, b:b + 2, :].rearrange("p b n -> p (b n)"), ACT.Square,
                                   accum_out=ss2[:, i:i + 1]).then_inc(s_oq, 1)
                    act.wait_ge(s_oq, i + 1)
                    act.activation(ss2[:, i:i + 1], ss2[:, i:i + 1], ACT.Sqrt, bias=epst[:, 0:1], scale=1.0 / D_MODEL).then_inc(s_os, 1)

                def square(n):
                    a, cut = BLOCKS[n]
                    act.wait_ge(f_xc, n + 1)
                    if n >= 2:
                        act.wait_ge(f_pv, n - 1)
                    act.activation(sq[:, n % 2, 0:width(cut)], y[:, a, cut], ACT.Square).then_inc(f_sq, 1)

                def round_w_out(c):
                    act.wait_ge(s_wo[c], 16)
                    act.activation(wo_hi[:, wo_part(c), :], wo[:, wo_part(c), :], ACT.Copy).then_inc(f_wh, 1)

                def round_inputs(b):
                    cut = BLOCKS[4 * b][1]
                    for n in range(4 * b, 4 * b + 4):
                        act.wait_ge(f_yc, n + 1)
                        act.activation(y_hi[:, n % 4, cut], y[:, n % 4, cut], ACT.Copy).then_inc(f_yh, 1)
                    if b == 0:
                        act.wait_ge(s_ab, 16)
                    act.wait_ge(f_bo, 4 * b + 4)
                    act.activation(yab_hi[:, :, cut], yab[:, :, cut], ACT.Copy).then_inc(f_ah, 1)

                bonus_keys(0)
                for n in range(4):
                    square(n)
                    if n < 3:
                        bonus_keys(n + 1)
                for b in range(NB):
                    deviation(b)
                    if b == 0:
                        for c in range(WO_PARTS - 1):
                            round_w_out(c)
                    for n in range(4 * b, 4 * b + 4):
                        affine(n)
                    round_inputs(b)
                    if b == 0:
                        round_w_out(WO_PARTS - 1)
                    if b == 1:
                        mean_square(1)
                    if b < NB - 1:
                        for n in range(4 * b + 4, 4 * b + 8):
                            bonus_keys(n)
                            square(n)
                        mean_square(2 * b)
                for i in range(NB, 9):
                    mean_square(i)

            @block.gpsimd
            def _(pool):
                pool.memset(back, 0.0).then_inc(f_bk, 1)
                pool.wait_ge(f_bk, 1)
                pool.affine_select(out=back, in_=back, compare_op=ALU.not_equal, fill=1.0, base=0,
                                   pattern=[[-32, 4], [-16, 2], [0, HEAD]], channel_multiplier=1).then_inc(f_bk, 1)
                rest_of_w_out(pool, 0)
                for n, (a, cut) in enumerate(BLOCKS):
                    pool.wait_ge(f_af, n + 1)
                    pool.wait_ge(f_bd, n + 1)
                    pool.tensor_tensor(y[:, a, cut], y[:, a, cut], vT[:, a, cut], ALU.add).then_inc(f_bo, 1)
                    if a == 3:
                        pool.wait_ge(f_ah, n // 4 + 1)
                        pool.tensor_tensor(yab_lo[:, :, cut], yab[:, :, cut], yab_hi[:, :, cut].bitcast(F32),
                                           ALU.subtract).then_inc(f_al, 1)

            @block.vector
            def _(dve):
                def centre(n):
                    a, cut = BLOCKS[n]
                    dve.wait_ge(f_pm, n + 1)
                    dve.scalar_tensor_tensor(out=y[:, a, cut], in0=ps[:, 4, 0:width(cut)], scalar=-1.0 / HEAD, in1=y[:, a, cut],
                                             op0=ALU.mult, op1=ALU.add).then_inc(f_xc, 1)
                    dve.wait_ge(f_pb, n + 1)
                    dve.tensor_tensor(vT[:, a, cut], vT[:, a, cut], ps[:, 5, 0:width(cut)], ALU.mult).then_inc(f_bd, 1)

                def invert(b):
                    dve.wait_ge(f_sd, b + 1)
                    n = width(CUTS[b])
                    dve.reciprocal(sd[:, 0:n], sd[:, 0:n]).then_inc(f_rs, 1)

                def normalise(n):
                    a, cut = BLOCKS[n]
                    dve.wait_ge(f_pr, n + 1)
                    dve.tensor_tensor(y[:, a, cut], y[:, a, cut], ps[:, (7, 4)[a % 2], 0:width(cut)], ALU.mult).then_inc(f_n, 1)

                def gate(n):
                    a, cut = BLOCKS[n]
                    dve.wait_ge(f_bo, n + 1)
                    dve.wait_ge(s_gl[n // 4], 16)
                    dve.scalar_tensor_tensor(out=y[:, a, cut], in0=gt[:, a, cut], scalar=0.5, in1=y[:, a, cut],
                                             op0=ALU.mult, op1=ALU.mult).then_inc(f_yc, 1)

                def finish(i):
                    b, slot = 2 * (i % 2), i % XO
                    dve.wait_ge(s_os, i + 1)
                    dve.reciprocal(rs2[:, i:i + 1], ss2[:, i:i + 1]).then_inc(f_dve, 1)
                    dve.wait_ge(f_dve, i + 1)
                    dve.scalar_tensor_tensor(out=gout[:, i % 2, :], in0=ps[:, b:b + 2, :].rearrange("p b n -> p (b n)"),
                                             scalar=rs2[:, i:i + 1], in1=gg[:, min(i, 1), :],
                                             op0=ALU.mult, op1=ALU.mult).then_inc(s_og, 1)
                    dve.wait_ge(s_og, i + 1)
                    dve.wait_ge(s_xr[slot], 16 * (i // XO + 1))
                    dve.tensor_tensor(xr[:, slot, :], xr[:, slot, :], gout[:, i % 2, :], ALU.add).then_inc(s_or, 1)

                def rest(n):
                    a, cut = BLOCKS[n]
                    dve.wait_ge(f_yh, n + 1)
                    dve.tensor_tensor(y_lo[:, a, cut], y[:, a, cut], y_hi[:, a, cut].bitcast(F32), ALU.subtract).then_inc(f_yl, 1)

                for b in range(NB):
                    group = range(4 * b, 4 * b + 4)
                    if b == 2:
                        finish(1)
                    for n in group:
                        centre(n)
                    if b == 1:
                        dve.wait_ge(s_gg, 16)
                    if b:
                        finish(2 * b - 2)
                    invert(b)
                    for n in group:
                        normalise(n)
                        if n >= 4 * b + 2:
                            gate(n - 2)
                    gate(4 * b + 2)
                    gate(4 * b + 3)
                    for n in group:
                        rest(n)
                    if b == 0:
                        for c in range(1, WO_PARTS):
                            rest_of_w_out(dve, c)
                for i in range(NB, 9):
                    finish(i)


_INS = ["x_prompt", "x_sample", "c", "state_rwkv", "c_ctx", "ada_w", "ada_b", "g_pre", "g_post", "w_in",
        "conv_a", "conv_b", "conv_b_bias", "ln_b_g", "ln_b_b", "mu", "w0", "w2", "a0", "a2", "k_k", "k_a",
        "r_k", "gn_g", "gn_b", "w_out"]
_OUTS = [(1, SEQ, D_MODEL), (1, DEC_SEQ, D_MODEL), (1, 1, 2, 8, 64, 64)]


def kernel(**inputs):
    import numpy as _np
    import concourse.bacc as _bacc
    from concourse import mybir as _mybir
    from concourse.bass_utils import run_bass_kernel_spmd as _run

    nc = _bacc.Bacc("TRN2", target_bir_lowering=False, num_devices=1)
    arrays, args = {}, []
    for name in _INS:
        a = _np.ascontiguousarray(inputs[name])
        arrays[f"in_{name}"] = a
        args.append(nc.dram_tensor(f"in_{name}", a.shape, _mybir.dt.from_np(a.dtype), kind="ExternalInput").ap())
    for i, shape in enumerate(_OUTS):
        args.append(nc.dram_tensor(f"out_{i}", shape, _mybir.dt.float32, kind="ExternalOutput").ap())
    hybrid_step_kernel(nc, *args)
    r = _run(nc, [arrays], core_ids=[0])
    return tuple(r.results[0][f"out_{i}"] for i in range(len(_OUTS)))
```
